# Optimizing a Trainium2 kernel written in Bass

```python
import jax, jax.numpy as jnp
from jax import lax
import numpy as np

D_MODEL = 1024
BATCH = 1
SEQ = 512
DEPTH = 2
DEC_BATCH = 8
DEC_SEQ = 4
PAST_LEN = 2048
PAGE_SIZE = 128

N_META = 16
N_A = DEPTH // 2
N_B = DEPTH - N_A
POOL_WINDOWS = (2, 4, 8, 16)
N_POOL_GROUPS = 4
POOL_GROUP_DIM = D_MODEL // N_POOL_GROUPS
POOL_STATE = max(POOL_WINDOWS) - 1
N_HEADS = 16
HEAD_DIM = D_MODEL // N_HEADS
ATTN_SCALE = HEAD_DIM ** -0.5
Q_BLOCK = 128
N_GROUPS = 4
EXPERTS_PER_GROUP = 4
N_EXPERTS = N_GROUPS * EXPERTS_PER_GROUP
TOP_K = 2
D_EXPERT = D_MODEL // 2
FORGET_BIAS = 2.0
EPS = 1e-6
NEG_INF = -1e30

kernel_name = "yoco_pool_fox_hmoe_step"

def rms_norm(x, g):
    xf = x.astype(jnp.float32)
    y = xf * lax.rsqrt(jnp.mean(xf * xf, axis=-1, keepdims=True) + EPS)
    return (y * g.astype(jnp.float32)).astype(x.dtype)

def pool_mixer(u, prev, pos0, w_grp, scale):
    n, t, _ = u.shape
    ext = jnp.concatenate([prev.astype(u.dtype), u], axis=1)
    extf = ext.astype(jnp.float32)
    csum = jnp.concatenate([jnp.zeros_like(extf[:, :1]), jnp.cumsum(extf, axis=1)], axis=1)
    pos = pos0 + jnp.arange(t)
    end = csum[:, POOL_STATE + 1: POOL_STATE + 1 + t]
    groups = []
    for g, w in enumerate(POOL_WINDOWS):
        lo, hi = g * POOL_GROUP_DIM, (g + 1) * POOL_GROUP_DIM
        start = csum[:, POOL_STATE + 1 - w: POOL_STATE + 1 - w + t, lo:hi]
        cnt = jnp.minimum(pos + 1, w).astype(jnp.float32)[None, :, None]
        groups.append((end[..., lo:hi] - start) / cnt)
    pooled = jnp.stack(groups, axis=2)
    diff = (pooled - u.astype(jnp.float32).reshape(n, t, N_POOL_GROUPS, POOL_GROUP_DIM)).astype(u.dtype)
    out = jnp.einsum('ntgc,gcd->ntgd', diff, w_grp).reshape(n, t, D_MODEL)
    return out * scale, ext[:, -POOL_STATE:]

def hier_moe(x, norm_g, w_rg, w_re, w_gate, w_up, w_down):
    u = rms_norm(x, norm_g)
    lg = jnp.einsum('ntd,dg->ntg', u, w_rg).astype(jnp.float32)
    pg = jax.nn.softmax(lg, axis=-1)
    p_top, g_sel = lax.top_k(pg, 1)
    le_all = jnp.einsum('ntd,gde->ntge', u, w_re).astype(jnp.float32)
    le = jnp.take_along_axis(le_all, g_sel[..., None], axis=2)[:, :, 0, :]
    top_v, top_i = lax.top_k(le, TOP_K)
    gate = p_top * jax.nn.softmax(top_v, axis=-1)
    expert_id = g_sel * EXPERTS_PER_GROUP + top_i
    dense_w = jnp.sum(jax.nn.one_hot(expert_id, N_EXPERTS, dtype=jnp.float32) * gate[..., None], axis=-2)
    h = jax.nn.silu(jnp.einsum('ntd,edf->ntef', u, w_gate)) * jnp.einsum('ntd,edf->ntef', u, w_up)
    h = h * dense_w[..., None].astype(h.dtype)
    return jnp.einsum('ntef,efd->ntd', h, w_down)

def shared_kv(h, kv_norm_g, w_kvf, b_f, k_norm_g):
    n, t, _ = h.shape
    p = rms_norm(h, kv_norm_g) @ w_kvf
    k = rms_norm(p[..., :D_MODEL].reshape(n, t, N_HEADS, HEAD_DIM), k_norm_g)
    v = p[..., D_MODEL:2 * D_MODEL].reshape(n, t, N_HEADS, HEAD_DIM)
    logf = jax.nn.log_sigmoid((p[..., 2 * D_MODEL:] + b_f).astype(jnp.float32))
    return k, v, logf

def project_queries(h, norm_g, w_q, q_norm_g):
    n, t, _ = h.shape
    q = (rms_norm(h, norm_g) @ w_q).reshape(n, t, N_HEADS, HEAD_DIM)
    return rms_norm(q, q_norm_g)

def forget_attn_prompt(q, k, v, c):
    n, t, _, _ = q.shape
    tp = -(-t // Q_BLOCK) * Q_BLOCK
    pad = tp - t
    qp = jnp.pad(q, ((0, 0), (0, pad), (0, 0), (0, 0)))
    kp = jnp.pad(k, ((0, 0), (0, pad), (0, 0), (0, 0)))
    vp = jnp.pad(v, ((0, 0), (0, pad), (0, 0), (0, 0)))
    ct = jnp.pad(c, ((0, 0), (0, pad), (0, 0))).transpose(0, 2, 1)
    nb = tp // Q_BLOCK
    q_blocks = qp.reshape(n, nb, Q_BLOCK, N_HEADS, HEAD_DIM).transpose(1, 0, 2, 3, 4)
    c_blocks = ct.reshape(n, N_HEADS, nb, Q_BLOCK).transpose(2, 0, 1, 3)
    starts = jnp.arange(nb) * Q_BLOCK
    kpos = jnp.arange(tp)

    def one_block(args):
        qb, cb, s0 = args
        s = jnp.einsum('nqhd,nkhd->nhqk', qb, kp).astype(jnp.float32) * ATTN_SCALE
        s = s + cb[..., None] - ct[:, :, None, :]
        qpos = s0 + jnp.arange(Q_BLOCK)
        s = jnp.where(kpos[None, :] <= qpos[:, None], s, NEG_INF)
        p = jax.nn.softmax(s, axis=-1)
        return jnp.einsum('nhqk,nkhd->nqhd', p.astype(vp.dtype), vp)

    out = lax.map(one_block, (q_blocks, c_blocks, starts))
    return out.transpose(1, 0, 2, 3, 4).reshape(n, tp, N_HEADS, HEAD_DIM)[:, :t]

def forget_attn_sample(q, k_new, v_new, c_new, k_past, v_past, c_past):
    s_len = q.shape[1]
    past = k_past.shape[1]
    cq = c_new.transpose(0, 2, 1)[..., None]
    s_past = jnp.einsum('nqhd,nkhd->nhqk', q, k_past).astype(jnp.float32) * ATTN_SCALE
    s_past = s_past + cq - c_past.transpose(0, 2, 1)[:, :, None, :]
    s_new = jnp.einsum('nqhd,nkhd->nhqk', q, k_new).astype(jnp.float32) * ATTN_SCALE
    s_new = s_new + cq - c_new.transpose(0, 2, 1)[:, :, None, :]
    causal = jnp.arange(s_len)[None, :] <= jnp.arange(s_len)[:, None]
    s_new = jnp.where(causal, s_new, NEG_INF)
    p = jax.nn.softmax(jnp.concatenate([s_past, s_new], axis=-1), axis=-1)
    out = jnp.einsum('nhqk,nkhd->nqhd', p[..., :past].astype(v_past.dtype), v_past)
    return out + jnp.einsum('nhqk,nkhd->nqhd', p[..., past:].astype(v_new.dtype), v_new)

def setup_inputs(seed: int = 0) -> dict:
    key = jax.random.key(seed)
    ks = jax.random.split(key, 26)
    f32 = jnp.float32
    n_pages = PAST_LEN // PAGE_SIZE
    n_used = DEC_BATCH * n_pages
    n_phys = n_used + max(1, n_used // 4)

    def nrm(k, shape, scale=1.0):
        return jax.random.normal(k, shape, f32) * scale

    def gain(k, shape):
        return 1.0 + 0.1 * nrm(k, shape)

    return {
        'x_prompt': nrm(ks[0], (BATCH, SEQ, D_MODEL)),
        'x_sample': nrm(ks[1], (DEC_BATCH, DEC_SEQ, D_MODEL)),
        'state_pool': nrm(ks[2], (N_A, DEC_BATCH, POOL_STATE, D_MODEL)),
        'cache_k': nrm(ks[3], (n_phys, PAGE_SIZE, N_HEADS, HEAD_DIM)),
        'cache_v': nrm(ks[4], (n_phys, PAGE_SIZE, N_HEADS, HEAD_DIM)),
        'cache_logf': jax.nn.log_sigmoid(FORGET_BIAS + nrm(ks[5], (n_phys, PAGE_SIZE, N_HEADS))),
        'page_table': jax.random.permutation(ks[6], n_phys)[:n_used].reshape(DEC_BATCH, n_pages).astype(jnp.int32),
        'meta': nrm(ks[7], (N_META, D_MODEL)),
        'pool_norm_g': gain(ks[8], (N_A, D_MODEL)),
        'pool_w': nrm(ks[9], (N_A, N_POOL_GROUPS, POOL_GROUP_DIM, POOL_GROUP_DIM), POOL_GROUP_DIM ** -0.5),
        'pool_scale': gain(ks[10], (N_A, D_MODEL)),
        'kv_norm_g': gain(ks[11], (D_MODEL,)),
        'w_kvf': nrm(ks[12], (D_MODEL, 2 * D_MODEL + N_HEADS), D_MODEL ** -0.5),
        'b_f': FORGET_BIAS + 0.5 * nrm(ks[13], (N_HEADS,)),
        'k_norm_g': gain(ks[14], (HEAD_DIM,)),
        'attn_norm_g': gain(ks[15], (N_B, D_MODEL)),
        'w_q': nrm(ks[16], (N_B, D_MODEL, D_MODEL), D_MODEL ** -0.5),
        'q_norm_g': gain(ks[17], (N_B, HEAD_DIM)),
        'w_o': nrm(ks[18], (N_B, D_MODEL, D_MODEL), D_MODEL ** -0.5),
        'ffn_norm_g': gain(ks[19], (DEPTH, D_MODEL)),
        'w_router_group': nrm(ks[20], (DEPTH, D_MODEL, N_GROUPS), D_MODEL ** -0.5),
        'w_router_expert': nrm(ks[21], (DEPTH, N_GROUPS, D_MODEL, EXPERTS_PER_GROUP), D_MODEL ** -0.5),
        'w_gate': nrm(ks[22], (DEPTH, N_EXPERTS, D_MODEL, D_EXPERT), D_MODEL ** -0.5),
        'w_up': nrm(ks[23], (DEPTH, N_EXPERTS, D_MODEL, D_EXPERT), D_MODEL ** -0.5),
        'w_down': nrm(ks[24], (DEPTH, N_EXPERTS, D_EXPERT, D_MODEL), D_EXPERT ** -0.5),
    }

def reference(x_prompt, x_sample, state_pool, cache_k, cache_v, cache_logf, page_table, meta,
              pool_norm_g, pool_w, pool_scale, kv_norm_g, w_kvf, b_f, k_norm_g,
              attn_norm_g, w_q, q_norm_g, w_o, ffn_norm_g, w_router_group, w_router_expert,
              w_gate, w_up, w_down):
    n_p = x_prompt.shape[0]
    n_s = x_sample.shape[0]
    past_len = page_table.shape[1] * cache_k.shape[1]
    meta_rows = jnp.broadcast_to(meta.astype(x_prompt.dtype)[None], (n_p, N_META, D_MODEL))
    hp = jnp.concatenate([meta_rows, x_prompt], axis=1)
    hs = x_sample
    pool_new_p, pool_new_s = [], []
    for layer in range(DEPTH):
        if layer < N_A:
            up = rms_norm(hp, pool_norm_g[layer])
            us = rms_norm(hs, pool_norm_g[layer])
            zero_prev = jnp.zeros((n_p, POOL_STATE, D_MODEL), up.dtype)
            mp, tail_p = pool_mixer(up, zero_prev, 0, pool_w[layer], pool_scale[layer])
            ms, tail_s = pool_mixer(us, state_pool[layer], past_len, pool_w[layer], pool_scale[layer])
            hp = hp + mp
            hs = hs + ms
            pool_new_p.append(tail_p)
            pool_new_s.append(tail_s)
        else:
            if layer == N_A:
                k_p, v_p, logf_p = shared_kv(hp, kv_norm_g, w_kvf, b_f, k_norm_g)
                k_s, v_s, logf_s = shared_kv(hs, kv_norm_g, w_kvf, b_f, k_norm_g)
                c_p = jnp.cumsum(logf_p, axis=1)
                k_past = cache_k[page_table].reshape(n_s, past_len, N_HEADS, HEAD_DIM)
                v_past = cache_v[page_table].reshape(n_s, past_len, N_HEADS, HEAD_DIM)
                logf_past = cache_logf[page_table].reshape(n_s, past_len, N_HEADS).astype(jnp.float32)
                c_all = jnp.cumsum(jnp.concatenate([logf_past, logf_s], axis=1), axis=1)
                c_past, c_s = c_all[:, :past_len], c_all[:, past_len:]
            j = layer - N_A
            qp = project_queries(hp, attn_norm_g[j], w_q[j], q_norm_g[j])
            qs = project_queries(hs, attn_norm_g[j], w_q[j], q_norm_g[j])
            op = forget_attn_prompt(qp, k_p, v_p, c_p)
            os_ = forget_attn_sample(qs, k_s, v_s, c_s, k_past, v_past, c_past)
            hp = hp + op.reshape(hp.shape) @ w_o[j]
            hs = hs + os_.reshape(hs.shape) @ w_o[j]
        hp = hp + hier_moe(hp, ffn_norm_g[layer], w_router_group[layer], w_router_expert[layer],
                           w_gate[layer], w_up[layer], w_down[layer])
        hs = hs + hier_moe(hs, ffn_norm_g[layer], w_router_group[layer], w_router_expert[layer],
                           w_gate[layer], w_up[layer], w_down[layer])
    y_prompt = hp[:, N_META:]
    y_sample = hs
    pool_state_prompt = jnp.stack(pool_new_p, axis=0)
    pool_state_sample = jnp.stack(pool_new_s, axis=0)
    return (y_prompt, y_sample, pool_state_prompt, pool_state_sample, k_p, v_p, logf_p, k_s, v_s, logf_s)


_drawn_inputs = setup_inputs


def setup_inputs(seed=0):
    import zlib

    import numpy as np

    out = dict(_drawn_inputs(seed))
    spreads = {}
    factors = {}
    for name, (base, spread) in spreads.items():
        noise = np.random.default_rng([zlib.crc32(name.encode()), seed]).standard_normal(out[name].shape)
        drawn = base * np.exp(spread * noise) if base else spread * noise
        out[name] = __import__('jax').numpy.asarray(drawn.astype(out[name].dtype))
    for name, factor in factors.items():
        out[name] = (out[name] * factor).astype(out[name].dtype)
    return out
```

```python
from contextlib import ExitStack

import numpy as np

import concourse.bass as bass
from concourse import mybir
from concourse.alu_op_type import AluOpType as ALU

F32 = mybir.dt.float32
I32 = mybir.dt.int32
ACT = mybir.ActivationFunctionType
X = mybir.AxisListType.X

P = 128
D = 1024
KC = D // P
META, SEQ = 16, 512
TP = META + SEQ
NT = 5
ROWS = [P, P, P, P, 64]
LASTP = TP - 4 * P
S0 = 32
NB, NS = 8, 4
WINDOWS = (2, 4, 8, 16)
NG = 4
GD = D // NG
STATE = 15
NH, DH = 16, 64
HP = NH // 2
NE = 16
FF = D // 2
FC = FF // P
PAGES, PAGE = 16, 128
CH = 4
NCH = PAGES // CH
BIG = 1e30
EPS = 1e-6
RANKS = 5 * P
LISTN = RANKS * NE + P
LINKS = 5 + NT
SMALL = 20
NORMS = ("pool", "r0", "proj", "r1")
OUTS = 14
T0 = 4
TICKS = 46
PTICKS = (38, 40, 42)

CONST = {}
_at = 0
for _name, _n in (("ident", P), ("tails", P), ("before", P), ("upto", P), ("after", P), ("ones", P), ("causal", P),
                  ("negnew", 64), ("smask", NB * 64), ("w4", 4), ("w16", NE), ("eid", NE),
                  ("valid", NT), ("junk", 2 * NT)):
    CONST[_name] = (_at, _at + _n)
    _at += _n
NCONST = _at
BAND = {}
_at = 0
for _name, _n in (("cur0", P), ("cur", P), ("prev", P), ("cur4", 64), ("prev4", 64), ("state", 64)):
    BAND[_name] = (_at, _at + NG * _n, _n)
    _at += NG * _n
NBAND = _at


def shape_constants():
    c = np.zeros((P, NCONST), np.float32)

    def put(name, a):
        lo, hi = CONST[name]
        a = np.asarray(a, np.float32).reshape(np.shape(a)[0], -1)
        c[:a.shape[0], lo:hi] = a

    i = np.arange(P)
    put("ident", np.eye(P))
    b, g = i // PAGES, i % PAGES
    put("tails", (b[:, None] == b[None]) & (g[:, None] > g[None]))
    put("before", i[:, None] < i[None])
    put("upto", i[:, None] <= i[None])
    put("after", i[:, None] > i[None])
    put("ones", np.ones((P, P)))
    put("causal", np.where(i[None] <= i[:, None], 0.0, -BIG))
    r = np.arange(64)
    sb, ss = (r - S0) // NS, (r - S0) % NS
    new = r >= S0
    put("negnew", -1.0 * (new[:, None] & new[None] & (sb[:, None] == sb[None]) & (ss[:, None] <= ss[None])))
    q = r % NS
    see = new[None, None] & (sb[None, None] == np.arange(NB)[None, :, None]) & (ss[None, None] <= q[:, None, None])
    put("smask", np.where(see, 0.0, -BIG))
    put("w4", np.tile(4.0 - np.arange(4), (P, 1)))
    put("w16", np.tile(NE - np.arange(NE), (P, 1)))
    put("eid", np.tile(np.arange(NE), (P, 1)))
    valid = np.ones((P, NT))
    valid[LASTP:S0, 4] = 0
    valid[64:, 4] = 0
    put("valid", valid)
    junk = np.zeros((P, 2, NT))
    junk[:64, 0, 4] = np.where(valid[:64, 4] == 0, RANKS * NE + r, 0)
    junk[:64, 1, 4] = np.where(valid[:64, 4] == 0, RANKS * NE + 64 + r, 0)
    put("junk", junk)

    w = np.zeros((P, NBAND), np.float32)

    def band(name, rows, cols, f):
        lo, hi, n = BAND[name]
        a = np.zeros((P, NG, n), np.float32)
        for g, win in enumerate(WINDOWS):
            for s in range(rows):
                for t in range(cols):
                    a[s, g, t] = f(win, s, t)
        w[:, lo:hi] = a.reshape(P, -1)

    def own(win, s, t):
        return float(s == t)

    band("cur0", P, P, lambda n, s, t: (t - n < s <= t) / min(t + 1, n) - own(n, s, t))
    band("cur", P, P, lambda n, s, t: (t - n < s <= t) / n - own(n, s, t))
    band("prev", P, P, lambda n, s, t: (s - P > t - n) / n)

    def cur4(n, s, t):
        if s < LASTP and t < LASTP:
            return (t - n < s <= t) / n - own(n, s, t)
        if s >= S0 and t >= S0 and (s - S0) // NS == (t - S0) // NS:
            return (t - n < s <= t) / n - own(n, s, t)
        return 0.0

    band("cur4", 64, 64, cur4)
    band("prev4", P, LASTP, lambda n, s, t: (s - P > t - n) / n)

    def state(n, s, t):
        if t < S0 or s // STATE != (t - S0) // NS:
            return 0.0
        return (s % STATE - STATE > (t - S0) % NS - n) / n

    band("state", NB * STATE, 64, state)
    ids = (np.arange(NT)[None] * P + np.arange(P)[:, None]).astype(np.int32)
    return c, w, ids


def after(eng, sem, value):
    if isinstance(value, int) and value <= 0:
        return
    eng.wait_ge(sem, value)


def build(nc, A, O):
    ctx = ExitStack()
    with ctx:
        ctx.enter_context(nc.allow_non_contiguous_dma(reason="gains, router weights and row lists, small"))

        def sb(name, shape, dt=F32):
            return ctx.enter_context(nc.sbuf_tensor(name, shape, dt))

        sems = {}

        def sem(name):
            if name not in sems:
                sems[name] = ctx.enter_context(nc.semaphore(name))
            return sems[name]

        H = sb("H", [P, NT, D])
        W = sb("W", [P, 6, 4 * D])
        KB = sb("KB", [P, 2, 4 * D])
        VB = sb("VB", [P, 2, 4 * D])
        C = sb("C", [P, NCONST])
        ids = sb("ids", [P, NT], I32)
        gains = sb("gains", [P, 4, KC])
        qg = sb("qg", [P, 1])
        kgb = sb("kgb", [P, DH])
        bfb = sb("bfb", [P, NH])
        wr = sb("wr", [P, 2, KC, NG + NE])
        wf = sb("wf", [P, KC, NH])
        pt = sb("pt", [1, NB * PAGES], I32)
        ptc = sb("ptc", [P, 1], I32)
        zi = sb("zi", [P, LISTN // P], I32)
        ss = sb("ss", [P, NT])
        ms = sb("ms", [P, NT])
        sd = sb("sd", [P, NT])
        rs = sb("rs", [P, NT])
        KT4 = sb("KT4", [P, HP, 64])
        QT4 = sb("QT4", [P, HP, 64])
        V4 = sb("V4", [P, D])
        RP = sb("RP", [P, NH, P])
        LF = sb("LF", [P, NT, NH])
        SLi = sb("SLi", [P, 2, NT], I32)
        SSi = sb("SSi", [P, 2, NT], I32)
        gate = sb("gate", [P, 2, NT])
        gm = sb("gm", [P, 2, NT])
        gg = sb("gg", [P, 2, NT])
        SGi = sb("SGi", [P, 2, NT], I32)
        IDX = sb("IDX", [P, NE], I32)
        idc = sb("idc", [P, 2], I32)
        npi = sb("npi", [1, 1], I32)
        idg = sb("idg", [P, 1], I32)
        hss = sb("hss", [P, 2, NH])
        hms = sb("hms", [P, 2, NH])
        hsd = sb("hsd", [P, 2, NH])
        hrs = sb("hrs", [P, 2, NH])

        def c(name, rows=P):
            lo, hi = CONST[name]
            return C[0:rows, lo:hi]

        ident = c("ident")
        PS = ctx.enter_context(nc.psum_tensor("PS", [P, 8, 512], F32))

        K8 = KB[:, :, :].rearrange("p a (b n) -> p (a b) n", n=D)
        V8 = VB[:, :, :].rearrange("p a (b n) -> p (a b) n", n=D)
        Vf = VB[:, :, :].rearrange("p a n -> p (a n)")
        U = [K8[:, t, :] for t in range(NT)]
        ST = K8[:, 5, :]
        DT = [K8[:, 6 + j, :].rearrange("p (k n) -> p k n", k=8) for j in range(2)]
        bands = Vf[:, 0:NBAND]
        pw = Vf[:, NBAND:NBAND + 2 * D].rearrange("p (g c n) -> p g c n", g=NG, c=2)
        png = Vf[:, NBAND + 2 * D:NBAND + 3 * D]
        psc = Vf[:, NBAND + 3 * D:NBAND + 4 * D]
        LP = W[:, 5, 0:2 * D].rearrange("p (r h) -> p r h", h=NH)
        TT = W[:, 4, :].rearrange("p (h n) -> p h n", h=NH)
        XG = [V8[:, j, :] for j in range(2)]
        YS = [V8[:, 2 + j, :] for j in range(2)]
        XT = V8[:, 4, :].rearrange("p (k n) -> p k n", k=KC)
        SG = V8[:, 5, 0:FF]
        HH = V8[:, 5, FF:2 * FF]
        HT = V8[:, 6, 0:FF].rearrange("p (f n) -> p f n", f=FC)
        XU = [V8[:, j, :].rearrange("p (k n) -> p k n", k=KC) for j in range(2)]

        rt = {}
        at = 6 * D + FF
        for name, n in (("L", NT * 20), ("mx", NT), ("dl", NT * 4), ("eg", NT * 4), ("sum", NT), ("ptop", NT),
                        ("oh", NT * 4), ("v4", NT * 4), ("vm", NT), ("pen", NT * 4), ("LM", NT * NE), ("LM2", NT * NE),
                        ("m1", NT), ("m2", NT), ("e1", NT * NE), ("oh1", NT * NE), ("oh2", NT * NE), ("A", NT * NE),
                        ("ed", NT), ("den", NT), ("rden", NT), ("R", NT * NE), ("SL", 2 * NT), ("SS", 2 * NT), ("Sm", 2 * NT),
                        ("tot", NE), ("nm", 1), ("np", 4), ("nf", 1), ("d", NT)):
            rt[name] = Vf[:, at:at + n]
            at += n
        assert at <= 8 * D
        UN = V8[:, 0, :]
        UK = V8[:, 1, :].rearrange("p (k n) -> p k n", k=KC)
        UQ = V8[:, 2, :].rearrange("p (k n) -> p k n", k=KC)
        SQ = V8[:, 3, :]
        KN = V8[:, 4, :]
        QN = V8[:, 5, :]
        VN = V8[:, 6, :]
        TS = V8[:, 7, :].rearrange("p (k n) -> p k n", k=HP)
        Wf = W[:, :, :].rearrange("p a n -> p (a n)")
        aat = [0]

        def carve(n):
            aat[0] += n
            return Wf[:, aat[0] - n:aat[0]]

        KTR = carve(4 * 512).rearrange("p (s n) -> p s n", s=4)
        SROW = carve(PAGES * PAGE + 64)
        PTT = carve((PAGES + 1) * 80).rearrange("p (g n) -> p g n", n=80)
        QST = [carve(TP) for _ in range(2)]
        KST = [carve(TP) for _ in range(2)]
        VST = carve(NT * P).rearrange("p (t n) -> p t n", n=P)
        PR = carve(TP)
        PTS = carve(4 * P)
        RBB = carve(PAGES * 64).rearrange("p (g n) -> p g n", n=64)
        QBLK = carve(HP * 32).rearrange("p (k n) -> p k n", n=32)
        OB = carve(256)
        smx = carve(NCH + 1)
        sst = carve(4)
        pst = carve(12)
        CT = carve(TP)
        LR = carve(64)
        lfa = carve(NT * NH)
        lfe = carve(NT * NH)
        nots = HP * (4 * P + 64)
        OTS = Wf[:, 4 * 4 * D - nots:4 * 4 * D].rearrange("p (k n) -> p k n", k=HP)
        assert aat[0] + nots <= 4 * 4 * D, aat
        VSL = [VB[:, 0, :], VB[:, 1, :], W[:, 4, :], W[:, 5, :]]
        kst4 = lambda a: a.rearrange("p (g n) -> p g n", n=D)

        XS = nc.dram_tensor("xs", (4 * P + 64, D), F32).ap()
        LIST = [nc.dram_tensor(f"list{i}", (LISTN, 1), I32).ap() for i in range(2)]
        YD = [nc.dram_tensor(f"yd{i}", (P * NE, D), F32).ap() for i in range(2)]
        YG = [nc.dram_tensor(f"yg{i}", (P * NE, D), F32).ap() for i in range(2)]
        QTD = nc.dram_tensor("qtd", (NH, DH + 1, TP), F32).ap()
        KTD = nc.dram_tensor("ktd", (NH, DH + 1, TP), F32).ap()
        k_rows = A["cache_k"].rearrange("n r h d -> (n r) (h d)")
        v_rows = A["cache_v"].rearrange("n r h d -> (n r) (h d)")
        kp_out = O["k_prompt"].rearrange("a t h d -> (a t) (h d)")
        vp_out = O["v_prompt"].rearrange("a t h d -> (a t) (h d)")
        fp_out = O["logf_prompt"].rearrange("a t h -> (a t) h")
        ks_out = O["k_sample"].rearrange("b s h d -> (b s) (h d)")
        vs_out = O["v_sample"].rearrange("b s h d -> (b s) (h d)")
        fs_out = O["logf_sample"].rearrange("b s h -> (b s) h")
        xs_rows = A["x_sample"].rearrange("b s d -> (b s) d")
        wkvf = A["w_kvf"].rearrange("(p k) n -> p k n", k=KC)
        wq = A["w_q"].rearrange("l (p k) n -> (l p) k n", k=KC)
        wo = A["w_o"].rearrange("l (k p) n -> p (l k) n", p=P)

        n_out = [0]

        def put_out(eng, dst, src):
            n_out[0] += 1
            eng.dma_start(dst, src).then_inc(sem("out_done"), 16)

        def w_src(l, e, which):
            if which < 2:
                return A["w_gate" if which == 0 else "w_up"][l, e].rearrange("(p k) f -> p (k f)", k=KC)
            return A["w_down"][l, e].rearrange("(p f) n -> p (f n)", f=FC)

        def w_src_dyn(l, e, which):
            name = ("w_gate", "w_up", "w_down")[which]
            t = A[name][l]
            if which < 2:
                return t[bass.ds(e, 1)].rearrange("e (p k) f -> p (e k f)", k=KC)
            return t[bass.ds(e, 1)].rearrange("e (p f) n -> p (e f n)", f=FC)

        def settled(eng):
            eng.nop(nofuse=True)

        block = ctx.enter_context(nc.Block())

        @block.sync
        def _(sp):
            sp.dma_start(C[:, :], A["consts"]).then_inc(sem("consts_in"), 16)
            sp.wait_ge(sem("h4_zero"), 1)
            sp.dma_start(H[0:META, 0, :], A["meta"]).then_inc(sem("rows_in"), 16)
            sp.dma_start(H[META:P, 0, :], A["x_prompt"][0, 0:P - META, :]).then_inc(sem("rows_in"), 16)
            for t in range(1, 4):
                sp.dma_start(H[:, t, :], A["x_prompt"][0, t * P - META:(t + 1) * P - META, :]).then_inc(sem("rows_in"), 16)
            sp.dma_start(H[0:LASTP, 4, :], A["x_prompt"][0, 4 * P - META:SEQ, :]).then_inc(sem("rows_in"), 16)
            sp.dma_start(H[S0:64, 4, :], xs_rows).then_inc(sem("rows_in"), 16)
            sp.dma_start(png, A["pool_norm_g"][0:1, :].to_broadcast([P, D])).then_inc(sem("pool_in"), 16)
            sp.dma_start(psc, A["pool_scale"][0:1, :].to_broadcast([P, D])).then_inc(sem("pool_in"), 16)
            sp.dma_start(bands, A["bands"]).then_inc(sem("pool_in"), 16)
            sp.dma_start(ST[0:NB * STATE, :], A["state_pool"].rearrange("a b s d -> (a b s) d")).then_inc(sem("pool_in"), 16)
            sp.dma_start(pw, A["pool_w"].rearrange("a g (c p) n -> p (a g) c n", p=P)).then_inc(sem("pool_in"), 16)
            for n, (name, l) in enumerate((("ffn_norm_g", 0), ("ffn_norm_g", 1), ("kv_norm_g", None), ("attn_norm_g", 0))):
                g = A[name] if l is None else A[name][l]
                sp.dma_start(gains[:, n, :], g.rearrange("(p k) -> p k", k=KC)).then_inc(sem("small_in"), 16)
            for l in range(2):
                sp.dma_start(wr[:, l, :, 0:NG], A["w_router_group"][l].rearrange("(p k) n -> p k n", k=KC))\
                    .then_inc(sem("small_in"), 16)
                for g in range(NG):
                    sp.dma_start(wr[:, l, :, NG + 4 * g:NG + 4 * g + 4],
                                 A["w_router_expert"][l, g].rearrange("(p k) n -> p k n", k=KC)).then_inc(sem("small_in"), 16)
            sp.dma_start(wf[:, :, :], wkvf[:, :, 2 * D:2 * D + NH]).then_inc(sem("small_in"), 16)
            for half in range(2):
                sp.dma_start(qg[half * DH:(half + 1) * DH, :], A["q_norm_g"].rearrange("a d -> d a")).then_inc(sem("small_in"), 16)
            sp.dma_start(kgb[:, :], A["k_norm_g"].rearrange("(a d) -> a d", a=1).to_broadcast([P, DH])).then_inc(sem("small_in"), 16)
            sp.dma_start(bfb[:, :], A["b_f"].rearrange("(a d) -> a d", a=1).to_broadcast([P, NH])).then_inc(sem("small_in"), 16)
            sp.dma_start(pt[:, :], A["page_table"].rearrange("(a b) g -> a (b g)", a=1)).then_inc(sem("small_in"), 16)
            n_out[0] += 1
            sp.dma_start(O["pool_state_sample"][0, :, 0:STATE - NS, :], A["state_pool"][0, :, NS:STATE, :])\
                .then_inc(sem("out_done"), 16)

            def moe_weights(l):
                def load(e, which, j):
                    done = sem(f"{('gate', 'up', 'down')[which]}_done")
                    if isinstance(e, int):
                        after(sp, done, e - 1 + l * NE)
                        sp.dma_start(W[:, 3 * j + which, :], w_src(l, e, which)).then_inc(sem(f"w_in_{3 * j + which}"), 16)
                    else:
                        sp.wait_ge(done, e - 1 + l * NE)
                        settled(sp)
                        sp.dma_start(W[:, 3 * j + which, :], w_src_dyn(l, e, which)).then_inc(sem(f"w_in_{3 * j + which}"), 16)

                def first(part):
                    if part == 0:
                        load(0, 0, 0)
                        load(0, 1, 0)
                    else:
                        load(0, 2, 0)
                        load(1, 0, 1)

                def second():
                    load(1, 1, 1)
                    load(1, 2, 1)

                def rest():
                    with sp.Fori(2, NE - 1, 2) as e:
                        for j in range(2):
                            for which in range(3):
                                load(e + j, which, j)
                return first, second, rest

            def moe_rest(l):
                sp.wait_ge(sem("scattered"), 16 * 2 * NT + l * (32 * NT))
                sp.dma_start(IDX[:, :], LIST[l][0:P * NE, :].rearrange("(r e) o -> r (e o)", e=NE)).then_inc(sem("idx_in"), 16)

            def moe_general(l):
                sp.wait_ge(sem("np_ready"), 1 + l * 1)
                npass = sp.value_load(npi[0:1, 0:1], min_val=1, max_val=RANKS // P)
                with sp.If(npass > 1):
                    sp.wait_ge(sem("down_done"), NE + l * NE)
                    with sp.Fori(1, npass) as p:
                        with sp.Fori(0, NE) as e:
                            n = p * NE + e - NE
                            sp.dma_start(idg[:, :], LIST[l][0:RANKS * NE, :].rearrange("(r e) o -> r (e o)", e=NE)
                                         [bass.ds(p * P, P), bass.ds(e, 1)]).then_inc(sem(f"g_in{l}"), 16)
                            for which in range(3):
                                sp.dma_start(W[:, which, :], w_src_dyn(l, e, which)).then_inc(sem(f"g_in{l}"), 16)
                            sp.wait_ge(sem(f"g_y_out{l}"), 16 * (n + 1))
                            settled(sp)
                        sp.wait_ge(sem(f"g_sum{l}"), 6 * p)
                        settled(sp)
                sp.nop()

            first, second, rest = moe_weights(0)
            first(0)
            first(1)
            sp.wait_ge(sem("r_done"), 4)
            second()
            sp.wait_ge(sem("u_ready"), NT)
            sp.dma_start(O["pool_state_prompt"][0, 0], U[4][LASTP - STATE:LASTP, :]).then_inc(sem("state_out"), 16)
            for b in range(NB):
                sp.dma_start(O["pool_state_sample"][0, b, STATE - NS:STATE, :], U[4][S0 + NS * b:S0 + NS * b + NS, :])\
                    .then_inc(sem("state_out"), 16)
            moe_rest(0)
            rest()
            moe_general(0)
            for which, done in ((0, "gate"), (1, "up"), (2, "down"), (3, "gate"), (4, "up"), (5, "down")):
                sp.wait_ge(sem(f"{done}_done"), NE)
                src = wkvf[:, :, 512 * which:512 * which + 512] if which < 4 else wq[:, :, 512 * (which - 4):512 * (which - 3)]
                sp.dma_start(W[:, which, :].rearrange("p (k n) -> p k n", k=KC), src).then_inc(sem("proj_in"), 16)

            def load_chunk(dst, rows, i, ch, s):
                for g in range(CH):
                    page = sp.value_load(pt[0:1, bass.ds(i * PAGES + ch * CH + g, 1)], min_val=0,
                                         max_val=A["cache_k"].shape[0] - 1)
                    sp.dma_start(dst[:, g * D:(g + 1) * D], rows[bass.ds(page * PAGE, PAGE), :]).then_inc(s, 16)

            sp.wait_ge(sem("h_sum"), NT)
            sp.wait_ge(sem("small_in"), 16 * SMALL)
            for ch in range(2):
                load_chunk(KB[:, ch, :], k_rows, 0, ch, sem(f"k_in{ch}"))

            def attention_loads(i, last):
                for ch in range(NCH):
                    after(sp, sem("pv_done"), NCH * (i - 1) + ch + 1)
                    if isinstance(i, int) and i == 0:
                        sp.wait_ge(sem("proj_done"), 1)
                    settled(sp)
                    load_chunk(VSL[ch], v_rows, i, ch, sem(f"v_in{ch}"))
                    if ch < 2:
                        sp.wait_ge(sem("kt_tr"), 32 * i + 8 * (ch + 1))
                        settled(sp)
                        load_chunk(KB[:, ch, :], k_rows, i, ch + 2, sem(f"k_in{ch}"))
                    elif not last:
                        sp.wait_ge(sem("kt_tr"), 32 * i + 8 * (ch + 1))
                        settled(sp)
                        load_chunk(KB[:, ch - 2, :], k_rows, i + 1, ch - 2, sem(f"k_in{ch - 2}"))
                    else:
                        sp.wait_ge(sem("kt_tr"), 32 * i + 8 * (ch + 1))
                        h = ch - 2
                        sp.dma_start(KB[:, h, :].rearrange("p (k n) -> p k n", k=HP), wo[:, :, 512 * h:512 * h + 512])\
                            .then_inc(sem("wo_in"), 16)

            attention_loads(0, False)
            with sp.Fori(1, NB - 1) as i:
                attention_loads(i, False)
            attention_loads(NB - 1, True)
            first, second, rest = moe_weights(1)
            sp.wait_ge(sem("pv_done"), NCH * NB)
            second()
            sp.wait_ge(sem("ots_ready"), 2 * NB)
            sp.wait_ge(sem("pu_ot"), 10 * NB)
            first(0)
            sp.wait_ge(sem("wo_done"), NT)
            first(1)
            moe_rest(1)
            rest()
            moe_general(1)
            for t in range(NT):
                sp.wait_ge(sem("h_sum"), NT + t + 1)
                if t == 0:
                    put_out(sp, O["y_prompt"][0, 0:P - META, :], H[META:P, 0, :])
                elif t < 4:
                    put_out(sp, O["y_prompt"][0, t * P - META:(t + 1) * P - META, :], H[:, t, :])
                else:
                    put_out(sp, O["y_prompt"][0, 4 * P - META:SEQ, :], H[0:LASTP, 4, :])
                    put_out(sp, O["y_sample"].rearrange("b s d -> (b s) d"), H[S0:64, 4, :])

        @block.gpsimd
        def _(pool):
            pool.memset(H[0:64, 4, :], 0.0).then_inc(sem("h4_zero"), 1)
            pool.memset(zi[:, :], 0).then_inc(sem("zi_zero"), 1)
            pool.dma_start(ptc[:, :], A["page_table"].rearrange("b (g a) -> (b g) a", a=1)).then_inc(sem("ptc_in"), 16)
            pool.dma_start(ids[:, :], A["ids"]).then_inc(sem("ptc_in"), 16)
            pool.wait_ge(sem("ptc_in"), 32)
            pool.indirect_dma_start(out=W[:, 5, 0:2 * D], out_offset=None,
                                    in_=A["cache_logf"].rearrange("n r h -> n (r h)"),
                                    in_offset=bass.IndirectOffsetOnAxis(ap=ptc[:, 0:1], axis=0)).then_inc(sem("lp_in"), 16)
            pool.wait_ge(sem("zi_zero"), 1)
            for l in range(2):
                pool.dma_start(LIST[l].rearrange("(p n) o -> p (n o)", p=P), zi[:, :]).then_inc(sem("list_zero"), 16)

            def moe(l):
                pool.wait_ge(sem("list_zero"), 32)
                pool.wait_ge(sem("slots_ready"), 1 + l * 1)
                for ch in range(2):
                    for t in range(NT):
                        r = ROWS[t]
                        pool.indirect_dma_start(out=LIST[l], out_offset=bass.IndirectOffsetOnAxis(ap=SSi[0:r, ch, t:t + 1], axis=0),
                                                in_=ids[0:r, t:t + 1], in_offset=None).then_inc(sem("scattered"), 16)
                for j in range(2):
                    pool.wait_ge(sem(f"xs_out_{j}"), (48 - 16 * j) * (l + 1))
                pool.wait_ge(sem("idx_in"), 16 + l * 16)
                pool.wait_ge(sem("router_done"), NT + l * NT)

                def gather(e, j):
                    after(pool, sem("xt_tr"), e - 1 + l * NE)
                    settled(pool)
                    pool.tensor_copy(idc[:, j:j + 1], IDX[:, e:e + 1] if isinstance(e, int) else IDX[:, bass.ds(e, 1)])\
                        .then_inc(sem("idc_ready"), 1)
                    pool.wait_ge(sem("idc_ready"), e + 1 + l * NE)
                    settled(pool)
                    pool.indirect_dma_start(out=XG[j], out_offset=None, in_=XS,
                                            in_offset=bass.IndirectOffsetOnAxis(ap=idc[:, j:j + 1], axis=0))\
                        .then_inc(sem(f"xg_in_{j}"), 16)

                gather(0, 0)
                gather(1, 1)
                with pool.Fori(2, NE - 1, 2) as e:
                    for j in range(2):
                        gather(e + j, j)
                pool.wait_ge(sem("np_ready"), 1 + l * 1)
                npass = pool.value_load(npi[0:1, 0:1], min_val=1, max_val=RANKS // P)
                with pool.If(npass > 1):
                    with pool.Fori(1, npass) as p:
                        with pool.Fori(0, NE) as e:
                            pool.wait_ge(sem(f"g_in{l}"), 64 * (p * NE + e - NE + 1))
                            settled(pool)
                            pool.indirect_dma_start(out=XG[0], out_offset=None, in_=XS,
                                                    in_offset=bass.IndirectOffsetOnAxis(ap=idg[:, 0:1], axis=0))\
                                .then_inc(sem(f"g_xg{l}"), 16)
                            pool.wait_ge(sem(f"g_y_out{l}"), 16 * (p * NE + e - NE + 1))
                            settled(pool)
                        for t in range(NT):
                            r = ROWS[t]
                            pool.wait_ge(sem(f"g_sum{l}"), 6 * p + t - 5)
                            settled(pool)
                            for ch in range(2):
                                pool.indirect_dma_start(out=K8[0:r, ch, :], out_offset=None, in_=YG[l],
                                                        in_offset=bass.IndirectOffsetOnAxis(ap=SGi[0:r, ch, t:t + 1], axis=0))\
                                    .then_inc(sem(f"g_yg{l}"), 16)
                        pool.wait_ge(sem(f"g_sum{l}"), 6 * p)
                        settled(pool)
                    pool.nop()
                for j in range(2):
                    pool.wait_ge(sem(f"y_out_{j}"), 16 * NE // 2 + l * (8 * NE))
                if l == 0:
                    pool.wait_ge(sem("state_out"), 16 * (NB + 1))
                for t in range(NT):
                    r = ROWS[t]
                    for ch in range(2):
                        buf = (2 * t + ch) % 8
                        if t == 4:
                            pool.wait_ge(sem("h_sum"), 1 + l * NT)
                        pool.indirect_dma_start(out=K8[0:r, buf, :], out_offset=None, in_=YD[l],
                                                in_offset=bass.IndirectOffsetOnAxis(ap=SLi[0:r, ch, t:t + 1], axis=0))\
                            .then_inc(sem(f"yg_in_{t}"), 16)

            moe(0)

            def stage(i):
                if not (isinstance(i, int) and i == 0):
                    pool.wait_ge(sem("pu_s"), 10 * i)
                    settled(pool)
                for hh in range(2):
                    for dst, src in ((QST, QTD), (KST, KTD)):
                        s = src[2 * i + hh] if isinstance(i, int) else src[bass.ds(2 * i + hh, 1)].rearrange("a d t -> (a d) t")
                        pool.dma_start(dst[hh][0:DH + 1, :], s).then_inc(sem("st_in"), 16)
                if not (isinstance(i, int) and i == 0):
                    pool.wait_ge(sem("pu_v"), 10 * i)
                    settled(pool)
                cols = slice(P * i, P * i + P) if isinstance(i, int) else bass.ds(P * i, P)
                pool.dma_start(VST[:, 0:4, :], vp_out[0:4 * P, cols].rearrange("(t p) n -> p t n", p=P)).then_inc(sem("st_in"), 16)
                pool.dma_start(VST[0:LASTP, 4, :], vp_out[4 * P:TP, cols]).then_inc(sem("st_in"), 16)

            pool.wait_ge(sem("proj_stored"), 1)
            stage(0)
            with pool.Fori(1, NB) as i:
                stage(i)
            moe(1)
            pool.wait_ge(sem("kout"), 16 * (NT + 1))
            pool.wait_ge(sem("vout"), 16 * NT)
            pool.wait_ge(sem("state_out"), 16 * (NB + 1))
            pool.wait_ge(sem("out_done"), 16 * OUTS)
            pool.nop()

        @block.tensor
        def _(pe):
            pe.wait_ge(sem("consts_in"), 16)
            pe.wait_ge(sem("lp_in"), 16)
            lo = CONST["ident"][0]
            both = C[:, lo:lo + 2 * P]
            for h in range(NH):
                if h >= 4 and h % 2 == 0:
                    pe.wait_ge(sem("tt_ready"), h // 2 - 1)
                mm = pe.matmul(PS[:, 6 + h // 2 % 2, 256 * (h % 2):256 * (h % 2) + 256], LP[:, :, h], both, start=True, stop=True)
                if h % 2:
                    mm.then_inc(sem("tt_tr"), 1)
            for n in range(4):
                if n == 0:
                    pe.wait_ge(sem("tt_ready"), NH // 2)
                if n >= 2:
                    pe.wait_ge(sem("r_done"), n - 1)
                pe.matmul(PS[:, 4 + n % 2, :].rearrange("p (h m) -> p h m", h=4), c("after"), TT[:, 4 * n:4 * n + 4, 0:P],
                          start=True, stop=False)
                pe.matmul(PS[:, 4 + n % 2, :].rearrange("p (h m) -> p h m", h=4), c("ones"), TT[:, 4 * n:4 * n + 4, P:2 * P],
                          start=False, stop=True).then_inc(sem("r_mm"), 1)

            def bandv(name, g):
                lo, hi, n = BAND[name]
                return bands[:, lo + g * n:lo + (g + 1) * n]

            pe.wait_ge(sem("pool_in"), 16 * 5)
            pe.wait_ge(sem("ws_ready"), 1)
            for t in range(NT):
                r = ROWS[t]
                pe.wait_ge(sem("u_ready"), t + 1)
                if t >= 1:
                    pe.wait_ge(sem("dt_ready"), 2 * t)
                for k in range(8):
                    g = k // 2
                    cs = slice(k * P, k * P + P)
                    out = PS[:, k // 4, (k % 4) * P:(k % 4) * P + r]
                    if t == 4:
                        pe.matmul(out, U[3][:, cs], bandv("prev4", g), start=True, stop=False)
                        pe.matmul(out, ST[0:NB * STATE, cs], bandv("state", g)[0:NB * STATE], start=False, stop=False)
                        mm = pe.matmul(out, U[4][0:64, cs], bandv("cur4", g)[0:64], start=False, stop=True)
                    else:
                        if t:
                            pe.matmul(out, U[t - 1][:, cs], bandv("prev", g), start=True, stop=False)
                        mm = pe.matmul(out, U[t][:, cs], bandv("cur" if t else "cur0", g), start=(t == 0), stop=True)
                mm.then_inc(sem("dt_mm"), 1)
                pe.wait_ge(sem("dt_ready"), 2 * t + 2)
                if t >= 2:
                    pe.wait_ge(sem("h_pool"), t - 1)
                if t == 1:
                    pe.wait_ge(sem("r_done"), 4)
                for g in range(NG):
                    for cc in range(2):
                        mm = pe.matmul(PS[0:r, 2 + 2 * (t % 2) + g // 2, 256 * (g % 2):256 * (g % 2) + 256],
                                       DT[t % 2][:, 2 * g + cc, 0:r], pw[:, g, cc, :], start=(cc == 0), stop=(cc == 1))
                mm.then_inc(sem("pool_mm"), 1)

            def transposes(src, bank, r, step):
                for k in range(KC):
                    s = src[0:r, :].rearrange("p (n k) -> p k n", k=KC)[:, k, :] if step > 1 else src[0:r, k * P:(k + 1) * P]
                    mm = pe.transpose(PS[:, bank + k // 4, (k % 4) * P:(k % 4) * P + r], s, ident[0:r, 0:r])
                return mm

            def router(l):
                for t in range(NT):
                    r = ROWS[t]
                    pe.wait_ge(sem("un_ready"), t + 1 + l * NT)
                    if t >= 2:
                        pe.wait_ge(sem("xu_ready"), t - 1 + l * NT)
                    transposes(YS[t % 2], 2 * (t % 2), r, KC).then_inc(sem("un_tr"), 1)
                    pe.wait_ge(sem("xu_ready"), t + 1 + l * NT)
                    if t == 0 and l == 0:
                        pe.wait_ge(sem("small_in"), 16 * SMALL)
                    for k in range(KC):
                        mm = pe.matmul(PS[0:r, 6, 20 * t:20 * t + 20], XU[t % 2][:, k, 0:r], wr[:, l, k, :],
                                       start=(k == 0), stop=(k == KC - 1))
                    mm.then_inc(sem("router_done"), 1)
                pe.wait_ge(sem("picks_ready"), 1 + l * 1)
                Av = rt["A"].rearrange("p (t e) -> p t e", t=NT)
                for t in range(NT):
                    r = ROWS[t]
                    out = PS[0:r, 7, NE * t:NE * t + NE]
                    for t2 in range(t):
                        pe.matmul(out, c("ones")[:, 0:r], Av[:, t2, :], start=(t2 == 0), stop=False)
                    pe.matmul(out, c("before")[0:r, 0:r], Av[0:r, t, :], start=(t == 0), stop=True)
                for t in range(NT):
                    r = ROWS[t]
                    mm = pe.matmul(PS[:, 7, NE * NT:NE * NT + NE], c("ones")[0:r, :], Av[0:r, t, :], start=(t == 0), stop=(t == NT - 1))
                mm.then_inc(sem("ranks"), 1)

            def moe(l):
                def x_tr(e, j):
                    k = 8 * e + 16 - 8 * j
                    pe.wait_ge(sem(f"xg_in_{j}"), k + l * (8 * NE))
                    after(pe, sem("xt_ready"), e + l * NE)
                    transposes(XG[j], 0, P, KC).then_inc(sem("xt_tr"), 1)

                def product(bank, slot, count, name):
                    pe.wait_ge(sem(f"w_in_{slot}"), count + l * (8 * NE))
                    w = W[:, slot, :].rearrange("p (k n) -> p k n", k=KC)
                    for k in range(KC):
                        mm = pe.matmul(PS[:, bank, :], XT[:, k, :], w[:, k, :], start=(k == 0), stop=(k == KC - 1))
                    mm.then_inc(sem(f"{name}_done"), 1)

                def h_tr(e):
                    pe.wait_ge(sem("h_ready"), e + 1 + l * NE)
                    after(pe, sem("ht_ready"), e + l * NE)
                    for f in range(FC):
                        mm = pe.transpose(PS[:, 4, f * P:(f + 1) * P], HH.rearrange("p (n f) -> p f n", f=FC)[:, f, :], ident)
                    mm.then_inc(sem("ht_tr"), 1)

                def down(e, j):
                    pe.wait_ge(sem("ht_ready"), e + 1 + l * NE)
                    pe.wait_ge(sem(f"w_in_{3 * j + 2}"), 8 * e + 16 - 8 * j + l * (8 * NE))
                    after(pe, sem("y_ready"), e + l * NE)
                    w = W[:, 3 * j + 2, :].rearrange("p (f n) -> p f n", f=FC)
                    for n in range(2):
                        for f in range(FC):
                            mm = pe.matmul(PS[:, 5 + n, :], HT[:, f, :], w[:, f, n * 512:(n + 1) * 512],
                                           start=(f == 0), stop=(f == FC - 1))
                    mm.then_inc(sem("down_done"), 1)

                def expert(e, j, last=False):
                    count = 8 * e + 16 - 8 * j
                    first = isinstance(e, int) and e == 0
                    pe.wait_ge(sem("xt_ready"), e + 1 + l * NE)
                    after(pe, sem("silu_done"), e + l * NE)
                    product(2, 3 * j, count, "gate")
                    if not first:
                        h_tr(e - 1)
                    product(3, 3 * j + 1, count, "up")
                    if not last:
                        x_tr(e + 1, 1 - j)
                    if not first:
                        down(e - 1, 1 - j)

                x_tr(0, 0)
                expert(0, 0)
                expert(1, 1)
                with pe.Fori(2, NE - 3, 2) as e:
                    expert(e, 0)
                    expert(e + 1, 1)
                expert(NE - 2, 0)
                expert(NE - 1, 1, last=True)
                h_tr(NE - 1)
                down(NE - 1, 1)

                pe.wait_ge(sem("np_ready"), 1 + l * 1)
                npass = pe.value_load(npi[0:1, 0:1], min_val=1, max_val=RANKS // P)
                with pe.If(npass > 1):
                    with pe.Fori(1, npass) as p:
                        with pe.Fori(0, NE) as e:
                            n = p * NE + e - NE
                            pe.wait_ge(sem(f"g_in{l}"), 64 * (n + 1))
                            pe.wait_ge(sem(f"g_xg{l}"), 16 * (n + 1))
                            transposes(XG[0], 0, P, KC).then_inc(sem(f"g_step{l}"), 1)
                            pe.wait_ge(sem(f"g_step{l}"), 9 * n + 2)
                            for which in range(2):
                                w = W[:, which, :].rearrange("p (k n) -> p k n", k=KC)
                                for k in range(KC):
                                    mm = pe.matmul(PS[:, 2 + which, :], XT[:, k, :], w[:, k, :], start=(k == 0), stop=(k == KC - 1))
                            mm.then_inc(sem(f"g_step{l}"), 1)
                            pe.wait_ge(sem(f"g_step{l}"), 9 * n + 5)
                            for f in range(FC):
                                mm = pe.transpose(PS[:, 4, f * P:(f + 1) * P], HH.rearrange("p (n f) -> p f n", f=FC)[:, f, :], ident)
                            mm.then_inc(sem(f"g_step{l}"), 1)
                            pe.wait_ge(sem(f"g_step{l}"), 9 * n + 7)
                            w = W[:, 2, :].rearrange("p (f n) -> p f n", f=FC)
                            for nn in range(2):
                                for f in range(FC):
                                    mm = pe.matmul(PS[:, 5 + nn, :], HT[:, f, :], w[:, f, nn * 512:(nn + 1) * 512],
                                                   start=(f == 0), stop=(f == FC - 1))
                            mm.then_inc(sem(f"g_step{l}"), 1)
                pe.nop()

            router(0)
            moe(0)

            wv = [W[:, s, :].rearrange("p (k n) -> p k n", k=KC) for s in range(6)]
            pe.wait_ge(sem("proj_in"), 16 * 6)
            for t in range(NT):
                r = ROWS[t]
                pe.wait_ge(sem("pun_ready"), t + 1)
                if t:
                    pe.wait_ge(sem("qts_ready"), t)
                transposes(UN, 0, r, KC).then_inc(sem("proj_tr"), 1)
                pe.wait_ge(sem("ux_ready"), 2 * t + 1)

                def project(x, banks, slots, name):
                    for b, s in zip(banks, slots):
                        for k in range(KC):
                            mm = pe.matmul(PS[0:r, b, :], x[:, k, 0:r], wv[s][:, k, :], start=(k == 0), stop=(k == KC - 1))
                    mm.then_inc(sem(name), 1)

                if t:
                    pe.wait_ge(sem("kn_ready"), 2 * t)
                project(UK, (2, 3), (0, 1), "proj_mm")
                if t:
                    pe.wait_ge(sem("qn_ready"), t)
                for k in range(KC):
                    mm = pe.matmul(PS[0:r, 6, 0:NH], UK[:, k, 0:r], wf[:, k, :], start=(k == 0), stop=(k == KC - 1))
                mm.then_inc(sem("proj_mm"), 1)
                if t:
                    pe.wait_ge(sem("vn_ready"), t)
                project(UK, (4, 5), (2, 3), "proj_mm")
                pe.wait_ge(sem("kn_ready"), 2 * t + 2)
                transposes(KN, 0, r, 1).then_inc(sem("proj_tr"), 1)
                pe.wait_ge(sem("f_ready"), t + 1)
                pe.wait_ge(sem("ux_ready"), 2 * t + 2)
                project(UQ, (6, 7), (4, 5), "proj_mm")
                pe.wait_ge(sem("qn_ready"), t + 1)
                pe.wait_ge(sem("kts_ready"), t + 1)
                transposes(QN, 0, r, 1).then_inc(sem("proj_tr"), 1)
            pe.wait_ge(sem("lf_step"), 5)
            pe.wait_ge(sem("lr_ready"), 1)
            for t in range(NT):
                n = P if t < 4 else LASTP
                out = PS[0:NH, 2 + t // 4, (t % 4) * P:(t % 4) * P + n]
                for t2 in range(t):
                    pe.matmul(out, LF[:, t2, :], c("ones")[:, 0:n], start=(t2 == 0), stop=False)
                mm = pe.matmul(out, LF[0:n, t, :], c("upto")[0:n, 0:n], start=(t == 0), stop=True)
            mm.then_inc(sem("ct_mm"), 1)
            pe.matmul(PS[0:64, 4, 0:64], LR[0:64, :], c("negnew", 64), start=True, stop=True).then_inc(sem("nb_mm"), 1)
            pe.wait_ge(sem("proj_done"), 1)

            def attention(i):
                def unit(u):
                    return u // 5, u % 5

                def s_step(u):
                    hh, t = unit(u)
                    r = P if t < 4 else LASTP
                    nk = P * (t + 1) if t < 4 else 4 * P
                    if u == 0:
                        pe.wait_ge(sem("st_in"), 96 * (i + 1))
                    after(pe, sem("pu_exp"), 10 * i + u)
                    if t == 4:
                        after(pe, sem("ots_ready"), 2 * i)
                    pe.matmul(PS[0:r, 6, 0:nk], QST[hh][0:DH + 1, t * P:t * P + r], KST[hh][0:DH + 1, 0:nk],
                              start=True, stop=True)
                    if t < 4:
                        mm = pe.matmul(PS[:, 6, t * P:t * P + P], ident, c("causal"), start=False, stop=True, skip_group_check=True)
                    else:
                        pe.matmul(PS[0:r, 5, 0:r], QST[hh][0:DH + 1, t * P:t * P + r], KST[hh][0:DH + 1, nk:TP],
                                  start=True, stop=False)
                        mm = pe.matmul(PS[0:r, 5, 0:r], ident[0:r, 0:r], c("causal")[0:r, 0:r], start=False, stop=True)
                    mm.then_inc(sem("pu_s"), 1)

                def t_step(u):
                    hh, t = unit(u)
                    pe.wait_ge(sem("pu_norm"), 10 * i + u + 1)
                    after(pe, sem("pu_pts"), 10 * i + u)
                    if t == 4:
                        settled(pe)
                    if t < 4:
                        for j in range(t + 1):
                            mm = pe.transpose(PS[:, 7, j * P:(j + 1) * P], PR[:, j * P:(j + 1) * P], ident)
                    else:
                        r = LASTP
                        for j in range(4):
                            pe.transpose(PS[:, 7, j * r:(j + 1) * r], PR[0:r, j * P:(j + 1) * P], ident[0:r, 0:r])
                        mm = pe.transpose(PS[0:r, 7, 4 * r:5 * r], PR[0:r, 4 * P:TP], ident[0:r, 0:r])
                    mm.then_inc(sem("pu_t"), 1)

                def v_step(u):
                    hh, t = unit(u)
                    pe.wait_ge(sem("pu_pts"), 10 * i + u + 1)
                    after(pe, sem("pu_ot"), 10 * i + u)
                    r = P if t < 4 else LASTP
                    vc = slice(DH * hh, DH * hh + DH)
                    out = PS[DH * hh:DH * hh + DH, 3, 0:r]
                    for j in range(t + 1):
                        kr = P if j < 4 else LASTP
                        mm = pe.matmul(out, VST[0:kr, j, vc], PTS[0:kr, j * r:(j + 1) * r], start=(j == 0), stop=(j == t),
                                       tile_position=(0, DH * hh))
                    mm.then_inc(sem("pu_v"), 1)

                def k_tick(n):
                    ch, w = n // 8, n % 8
                    hp = w // 2 + 4 * (w % 2)
                    if w == 0:
                        pe.wait_ge(sem(f"k_in{ch % 2}"), 64 * (2 * i + ch // 2 + 1))
                    after(pe, sem("kt_even" if n % 2 == 0 else "kt_odd"), 16 * i + n // 2)
                    ks = kst4(KB[:, ch % 2, :])
                    for g in range(CH):
                        mm = pe.transpose(PS[:, n % 2, g * P:(g + 1) * P], ks[:, g, hp * P:(hp + 1) * P], ident)
                    mm.then_inc(sem("kt_tr"), 1)

                def qk(ch, p):
                    n = 8 * ch + 2 * p
                    pe.wait_ge(sem("kt_even"), 16 * i + n // 2 + 1)
                    pe.wait_ge(sem("kt_odd"), 16 * i + n // 2 + 1)
                    if p == 0:
                        if ch == 0:
                            pe.wait_ge(sem("sn_ready"), i + 1)
                        else:
                            pe.wait_ge(sem("s_ready"), 4 * i + ch)
                    for a in range(2):
                        mm = pe.matmul(PS[32 * a:32 * a + 32, 2, :], QBLK[:, 4 * a + p, :], KTR[:, (n + a) % 4, :],
                                       start=(p == 0), stop=(p == 3), tile_position=(0, 32 * a), skip_group_check=True)
                    mm.then_inc(sem("qk_done"), 1)
                    if p == 3:
                        for g in range(CH):
                            for a in range(2):
                                mm = pe.matmul(PS[32 * a:32 * a + 32, 2, g * P:(g + 1) * P],
                                               RBB[:, CH * ch + g, 32 * a:32 * a + 32], ident, start=False,
                                               stop=True, tile_position=(0, 32 * a), skip_group_check=True)
                        mm.then_inc(sem("s_mm"), 1)

                pe.wait_ge(sem("qb_ready"), i + 1)
                after(pe, sem("s_ready"), 4 * i)
                for p in range(4):
                    for a in range(2):
                        mm = pe.matmul(PS[32 * a:32 * a + 32, 2, 0:64], QBLK[:, 4 * a + p, :], KT4[:, 4 * a + p, :],
                                       start=(p == 0), stop=(p == 3), tile_position=(0, 32 * a), skip_group_check=True)
                mm.then_inc(sem("sn_mm"), 1)
                for n in range(TICKS):
                    if n < 32:
                        k_tick(n)
                    if n >= 3 and (n - 3) % 2 == 0 and (n - 3) // 2 < 16:
                        qk((n - 3) // 8, (n - 3) // 2 % 4)
                    u, w = (n - T0) // 4, (n - T0) % 4
                    if w == 0 and 0 <= u < 10:
                        s_step(u)
                    if w == 3 and 0 <= u < 10:
                        t_step(u)
                    if w == 1 and 1 <= u < 11:
                        v_step(u - 1)
                    if n in PTICKS:
                        part = PTICKS.index(n)
                        if part == 0:
                            pe.wait_ge(sem("sp_norm"), i + 1)
                        after(pe, sem("ptt_ready"), 3 * i + part)
                        if part == 0:
                            after(pe, sem("ob_ready"), i)
                        settled(pe)
                        pages = range(8 * part, 8 * part + 8) if part < 2 else [PAGES]
                        for g in pages:
                            nn = P if g < PAGES else 64
                            mm = pe.transpose(PS[0:nn, 4, (g % 8) * 64:(g % 8) * 64 + 64], SROW[0:64, g * P:g * P + nn],
                                              ident[0:64, 0:64])
                        mm.then_inc(sem("ptt_tr"), 1)
                after(pe, sem("ots_ready"), 2 * i)
                pe.wait_ge(sem("pu_exp"), 10 * i + 10)
                pe.wait_ge(sem("ptt_ready"), 3 * i + 3)
                for ch in range(NCH + 1):
                    if ch < NCH:
                        pe.wait_ge(sem(f"v_in{ch}"), 64 * (i + 1))
                    for g in (range(CH * ch, CH * ch + CH) if ch < NCH else [PAGES]):
                        nn = P if g < PAGES else 64
                        for q in range(4):
                            v = kst4(VSL[ch])[:, g % CH, 256 * q:256 * q + 256] if ch < NCH else V4[0:64, 256 * q:256 * q + 256]
                            mm = pe.matmul(PS[32 * q:32 * q + 32, 5, 0:256], PTT[0:nn, g, 16 * q:16 * q + 32], v,
                                           start=(g == 0), stop=(g == PAGES), tile_position=(0, 32 * q), skip_group_check=True)
                    mm.then_inc(sem("pv_done" if ch < NCH else "o_mm"), 1)
                pe.wait_ge(sem("ob_ready"), i + 1)
                for x in range(2):
                    mm = pe.transpose(PS[:, 5, 256 + x * P:256 + (x + 1) * P], OB[:, x * P:(x + 1) * P], ident)
                mm.then_inc(sem("ob_tr"), 1)

            attention(0)
            with pe.Fori(1, NB) as i:
                attention(i)

            pe.wait_ge(sem("wo_in"), 32)
            pe.wait_ge(sem("pu_ot"), 10 * NB)
            pe.wait_ge(sem("ots_ready"), 2 * NB)
            for t in range(NT):
                r = ROWS[t]
                if t >= 2:
                    pe.wait_ge(sem("h_attn"), t - 1)
                for n in range(2):
                    for k in range(HP):
                        mm = pe.matmul(PS[0:r, 2 * (t % 2) + n, :], OTS[:, k, t * P:t * P + r],
                                       KB[:, n, :].rearrange("p (k n) -> p k n", k=HP)[:, k, :], start=(k == 0), stop=(k == HP - 1))
                mm.then_inc(sem("wo_done"), 1)
            router(1)
            moe(1)

        @block.scalar
        def _(act):
            def roots(name):
                act.wait_ge(sem("ms"), NORMS.index(name) + 1)
                act.activation(sd[:, :], ms[:, :], ACT.Sqrt).then_inc(sem("sd"), 1)

            act.wait_ge(sem("ss_one"), 1)
            act.wait_ge(sem("rows_in"), 16 * 7)
            for t in range(NT):
                r = ROWS[t]
                act.activation(U[t][0:r, :], H[0:r, t, :], ACT.Square, accum_out=ss[0:r, t:t + 1]).then_inc(sem("sq"), 1)
            roots("pool")
            for n in range(4):
                act.wait_ge(sem("r_mm"), n + 1)
                act.activation(RP[:, 4 * n:4 * n + 4, :], PS[:, 4 + n % 2, :].rearrange("p (h m) -> p h m", h=4), ACT.Copy)\
                    .then_inc(sem("r_done"), 1)
            for t in range(NT):
                r = ROWS[t]
                act.wait_ge(sem("dt_mm"), t + 1)
                if t >= 2:
                    act.wait_ge(sem("pool_mm"), t - 1)
                act.activation(DT[t % 2][:, 4:8, 0:r], PS[:, 1, :].rearrange("p (k n) -> p k n", k=4)[:, :, 0:r], ACT.Copy)\
                    .then_inc(sem("dt_ready"), 1)

            def router(l, h_sem):
                act.wait_ge(sem("pool_mm" if l == 0 else "wo_done"), NT)
                if l == 1:
                    act.wait_ge(sem("pv_done"), NCH * NB)
                for t in range(NT):
                    r = ROWS[t]
                    act.wait_ge(sem(h_sem), t + 1)
                    if t >= 2:
                        act.wait_ge(sem("sq"), NT * (1 + 2 * l) + t - 1)
                    act.activation(XG[t % 2][0:r, :], H[0:r, t, :], ACT.Square, accum_out=ss[0:r, t:t + 1]).then_inc(sem("sq"), 1)
                roots(f"r{l}")
                for t in range(NT):
                    r = ROWS[t]
                    act.wait_ge(sem("un_ready"), t + 1 + l * NT)
                    act.dma_start(XS[t * P:t * P + r, :], YS[t % 2][0:r, :]).then_inc(sem(f"xs_out_{t % 2}"), 16)
                act.wait_ge(sem("rt_in"), 1 + l * 2)
                act.activation(rt["eg"], rt["dl"], ACT.Exp).then_inc(sem("rt_exp"), 1)
                act.wait_ge(sem("rt_in"), 2 + l * 2)
                act.activation(rt["ed"], rt["d"], ACT.Exp).then_inc(sem("rt_exp"), 1)

            def moe(l):
                def silu(e):
                    act.wait_ge(sem("gate_done"), e + 1 + l * NE)
                    after(act, sem("h_ready"), e + l * NE)
                    act.activation(SG, PS[:, 2, :], ACT.Silu).then_inc(sem("silu_done"), 1)

                def ht(e):
                    act.wait_ge(sem("ht_tr"), e + 1 + l * NE)
                    after(act, sem("down_done"), e + l * NE)
                    act.activation(HT.rearrange("p f n -> p (f n)"), PS[:, 4, :], ACT.Copy).then_inc(sem("ht_ready"), 1)

                def y(e, j):
                    act.wait_ge(sem("down_done"), e + 1 + l * NE)
                    after(act, sem(f"y_out_{j}"), 8 * e - 8 * j + l * (8 * NE))
                    act.activation(YS[j], PS[:, 5:7, :].rearrange("p a n -> p (a n)"), ACT.Copy).then_inc(sem("y_ready"), 1)
                    act.wait_ge(sem("y_ready"), e + 1 + l * NE)
                    settled(act)
                    rows = YD[l].rearrange("(r e) n -> e r n", e=NE)
                    dst = rows[e] if isinstance(e, int) else rows[bass.ds(e, 1)].rearrange("e r n -> (e r) n")
                    act.dma_start(dst, YS[j]).then_inc(sem(f"y_out_{j}"), 16)

                for j in range(2):
                    act.wait_ge(sem(f"xs_out_{j}"), (48 - 16 * j) * (l + 1))
                silu(0)
                silu(1)
                ht(0)
                y(0, 0)
                with act.Fori(2, NE - 1, 2) as e:
                    silu(e)
                    ht(e - 1)
                    y(e - 1, 1)
                    silu(e + 1)
                    ht(e)
                    y(e, 0)
                ht(NE - 1)
                y(NE - 1, 1)
                act.wait_ge(sem("np_ready"), 1 + l * 1)
                npass = act.value_load(npi[0:1, 0:1], min_val=1, max_val=RANKS // P)
                with act.If(npass > 1):
                    act.wait_ge(sem("y_out_0"), 16 * NE // 2 + l * (8 * NE))
                    with act.Fori(1, npass) as p:
                        with act.Fori(0, NE) as e:
                            n = p * NE + e - NE
                            act.wait_ge(sem(f"g_step{l}"), 9 * n + 3)
                            act.activation(SG, PS[:, 2, :], ACT.Silu).then_inc(sem(f"g_step{l}"), 1)
                            act.wait_ge(sem(f"g_step{l}"), 9 * n + 6)
                            act.activation(HT.rearrange("p f n -> p (f n)"), PS[:, 4, :], ACT.Copy).then_inc(sem(f"g_step{l}"), 1)
                            act.wait_ge(sem(f"g_step{l}"), 9 * n + 8)
                            act.activation(YS[0], PS[:, 5:7, :].rearrange("p a n -> p (a n)"), ACT.Copy).then_inc(sem(f"g_step{l}"), 1)
                            act.wait_ge(sem(f"g_step{l}"), 9 * n + 9)
                            settled(act)
                            rows = YG[l].rearrange("(r e) n -> e r n", e=NE)
                            act.dma_start(rows[bass.ds(e, 1)].rearrange("e r n -> (e r) n"), YS[0])\
                                .then_inc(sem(f"g_y_out{l}"), 16)
                act.nop()

            router(0, "h_pool")
            moe(0)

            act.wait_ge(sem("y_out_0"), 16 * NE // 2)
            act.wait_ge(sem("y_out_1"), 16 * NE // 2)
            for t in range(NT):
                r = ROWS[t]
                act.wait_ge(sem("h_sum"), t + 1)
                if t:
                    act.wait_ge(sem("sq"), 2 * NT + t)
                act.activation(SQ[0:r, :], H[0:r, t, :], ACT.Square, accum_out=ss[0:r, t:t + 1]).then_inc(sem("sq"), 1)
            roots("proj")
            for t in range(NT):
                r = ROWS[t]
                two = lambda b: PS[0:r, b:b + 2, :].rearrange("p a n -> p (a n)")
                act.wait_ge(sem("proj_mm"), 4 * t + 1)
                if t:
                    act.wait_ge(sem("ssq_ready"), t)
                act.activation(SQ[0:r, :], two(2), ACT.Square).then_inc(sem("head_sq"), 1)
                act.wait_ge(sem("head_ms"), 2 * t + 1)
                act.activation(hsd[:, 0, :], hms[:, 0, :], ACT.Sqrt).then_inc(sem("head_sd"), 1)
                act.wait_ge(sem("kn_ready"), 2 * t + 2)
                act.dma_start(kp_out[t * P:t * P + min(P, TP - t * P), :], KN[0:min(r, TP - t * P), :]).then_inc(sem("kout"), 16)
                if t == 4:
                    act.dma_start(ks_out, KN[S0:64, :]).then_inc(sem("kout"), 16)
                act.wait_ge(sem("proj_mm"), 4 * t + 3)
                dst = VN if t < 4 else V4
                if t:
                    act.wait_ge(sem("vout"), 16 * t)
                act.activation(dst[0:r, :], two(4), ACT.Copy).then_inc(sem("vn_ready"), 1)
                act.wait_ge(sem("vn_ready"), t + 1)
                act.dma_start(vp_out[t * P:t * P + min(P, TP - t * P), :], dst[0:min(r, TP - t * P), :]).then_inc(sem("vout"), 16)
                if t == 4:
                    put_out(act, vs_out, V4[S0:64, :])
                act.wait_ge(sem("proj_tr"), 3 * t + 2)
                dst = TS if t < 4 else KT4
                if t:
                    act.wait_ge(sem("qtd_out"), 32 * t)
                act.activation(dst[:, :, 0:r], PS[:, 0:2, :].rearrange("p a (k n) -> p (a k) n", n=P)[:, :, 0:r], ACT.Copy)\
                    .then_inc(sem("kts_ready"), 1)
                act.wait_ge(sem("kts_ready"), t + 1)
                n = r if t < 4 else LASTP
                for hh in range(2):
                    act.dma_start(KTD[hh:NH:2, 0:DH, t * P:t * P + n].rearrange("h d t -> d h t"), dst[DH * hh:DH * hh + DH, :, 0:n])\
                        .then_inc(sem("ktd_out"), 16)
                act.wait_ge(sem("proj_mm"), 4 * t + 4)
                act.activation(SQ[0:r, :], two(6), ACT.Square).then_inc(sem("head_sq"), 1)
                act.wait_ge(sem("head_ms"), 2 * t + 2)
                act.activation(hsd[:, 1, :], hms[:, 1, :], ACT.Sqrt).then_inc(sem("head_sd"), 1)
                act.wait_ge(sem("proj_tr"), 3 * t + 3)
                act.wait_ge(sem("ktd_out"), 32 * (t + 1))
                dst = TS if t < 4 else QT4
                act.activation(dst[:, :, 0:r], PS[:, 0:2, :].rearrange("p a (k n) -> p (a k) n", n=P)[:, :, 0:r], ACT.Copy,
                               scale=qg[:, 0:1]).then_inc(sem("qts_ready"), 1)
                act.wait_ge(sem("qts_ready"), t + 1)
                for hh in range(2):
                    act.dma_start(QTD[hh:NH:2, 0:DH, t * P:t * P + n].rearrange("h d t -> d h t"), dst[DH * hh:DH * hh + DH, :, 0:n])\
                        .then_inc(sem("qtd_out"), 16)
            act.wait_ge(sem("lf_step"), 1)
            act.activation(lfe, lfa, ACT.Exp, scale=-1.0).then_inc(sem("lf_step"), 1)
            act.wait_ge(sem("lf_step"), 3)
            act.activation(lfa, lfe, ACT.Ln).then_inc(sem("lf_step"), 1)
            act.wait_ge(sem("lf_step"), 5)
            for t in range(NT):
                n = P if t < 4 else LASTP
                put_out(act, fp_out[t * P:t * P + n, :], LF[0:n, t, :])
            put_out(act, fs_out, LF[S0:64, 4, :])
            act.wait_ge(sem("ct_mm"), 1)
            act.activation(CT[0:NH, 0:4 * P], PS[0:NH, 2, :], ACT.Copy, scale=-1.0).then_inc(sem("ct_ready"), 1)
            act.activation(CT[0:NH, 4 * P:TP], PS[0:NH, 3, 0:LASTP], ACT.Copy, scale=-1.0).then_inc(sem("ct_ready"), 1)
            act.wait_ge(sem("ct_ready"), 2)
            act.wait_ge(sem("one_ready"), 1)
            act.dma_start(KTD[:, DH, :], CT[0:NH, :]).then_inc(sem("ktd_out"), 16)
            act.dma_start(QTD[:, DH, :], PR[0:NH, :]).then_inc(sem("qtd_out"), 16)
            act.wait_ge(sem("ktd_out"), 32 * NT + 16)
            act.wait_ge(sem("qtd_out"), 32 * NT + 16)
            act.wait_ge(sem("vout"), 16 * NT)
            act.wait_ge(sem("proj_done"), 1)
            act.sem_inc(sem("proj_stored"), 1)

            def attention(i):
                def evac(n):
                    act.wait_ge(sem("kt_tr"), 32 * i + n + 1)
                    after(act, sem("qk_done"), 16 * i + n // 2 - 1)
                    act.activation(KTR[:, n % 4, :], PS[:, n % 2, :], ACT.Copy).then_inc(sem("kt_odd"), 1)

                def scores(ch):
                    act.wait_ge(sem("s_mm"), 4 * i + ch + 1)
                    if ch == 0:
                        after(act, sem("ptt_tr"), 3 * i)
                    act.activation(SROW[0:64, 512 * ch:512 * ch + 512], PS[0:64, 2, :], ACT.Copy).then_inc(sem("s_ready"), 1)

                def exp(u):
                    t = u % 5
                    r = P if t < 4 else LASTP
                    nk = P * (t + 1) if t < 4 else 4 * P
                    act.wait_ge(sem("pu_max"), 10 * i + u + 1)
                    after(act, sem("pu_t"), 10 * i + u)
                    if t < 4:
                        act.activation(PR[0:r, 0:nk], PS[0:r, 6, 0:nk], ACT.Exp, bias=pst[0:r, 0:1], accum_out=pst[0:r, 3:4])\
                            .then_inc(sem("pu_exp"), 1)
                    else:
                        act.activation(PR[0:r, 0:nk], PS[0:r, 6, 0:nk], ACT.Exp, bias=pst[0:r, 0:1], accum_out=pst[0:r, 4:5])
                        act.activation(PR[0:r, nk:TP], PS[0:r, 5, 0:r], ACT.Exp, bias=pst[0:r, 0:1], accum_out=pst[0:r, 5:6])\
                            .then_inc(sem("pu_exp"), 1)

                def ot(u):
                    hh, t = u // 5, u % 5
                    r = P if t < 4 else LASTP
                    act.wait_ge(sem("pu_v"), 10 * i + u + 1)
                    dst = OTS[DH * hh:DH * hh + DH, i, t * P:t * P + r] if isinstance(i, int) else \
                        OTS[DH * hh:DH * hh + DH, bass.ds(i, 1), t * P:t * P + r].rearrange("p a n -> p (a n)")
                    act.activation(dst, PS[DH * hh:DH * hh + DH, 3, 0:r], ACT.Copy).then_inc(sem("pu_ot"), 1)

                for n in range(TICKS):
                    if n < 32 and n % 2 == 1:
                        evac(n)
                    if n >= 3 and (n - 3) % 8 == 7 and (n - 3) // 8 < 4:
                        scores((n - 3) // 8)
                    u, w = (n - T0) // 4, (n - T0) % 4
                    if w == 0 and 0 <= u < 10:
                        exp(u)
                    if w == 1 and 1 <= u < 11:
                        ot(u - 1)
                    if n == PTICKS[0] - 2:
                        act.wait_ge(sem("sp_max"), i + 1)
                        act.activation(SROW[0:64, :], SROW[0:64, :], ACT.Exp, bias=sst[0:64, 0:1], accum_out=sst[0:64, 1:2])\
                            .then_inc(sem("sp_exp"), 1)
                act.wait_ge(sem("o_mm"), i + 1)
                after(act, sem("ob_tr"), i)
                act.activation(OB, PS[:, 5, 0:256], ACT.Copy).then_inc(sem("ob_ready"), 1)

            attention(0)
            with act.Fori(1, NB) as i:
                attention(i)
            router(1, "h_attn")
            moe(1)

        @block.vector
        def _(dve):
            steps = [0]

            def then(ins):
                steps[0] += 1
                ins.then_inc(sem("dve_step"), 1)
                dve.wait_ge(sem("dve_step"), steps[0])

            def root(name):
                n = NORMS.index(name) + 1
                dve.wait_ge(sem("sq"), NT * n)
                dve.tensor_scalar(ms[:, :], ss[:, :], 1.0 / D, EPS, ALU.mult, ALU.add).then_inc(sem("ms"), 1)
                dve.wait_ge(sem("sd"), n)
                then(dve.reciprocal(rs[:, :], sd[:, :]))

            dve.memset(ss[:, :], 1.0).then_inc(sem("ss_one"), 1)
            dve.wait_ge(sem("pool_in"), 16 * 5)
            for cc in range(2):
                ins = dve.tensor_tensor(pw[:, :, cc, :], pw[:, :, cc, :], psc.rearrange("p (g n) -> p g n", g=NG), ALU.mult)
            ins.then_inc(sem("ws_ready"), 1)
            root("pool")
            for t in range(NT):
                r = ROWS[t]
                dve.scalar_tensor_tensor(out=U[t][0:r, :], in0=H[0:r, t, :], scalar=rs[0:r, t:t + 1], in1=png[0:r, :],
                                         op0=ALU.mult, op1=ALU.mult).then_inc(sem("u_ready"), 1)
            for n in range(NH // 2):
                dve.wait_ge(sem("tt_tr"), n + 1)
                dve.tensor_copy(TT[:, 2 * n:2 * n + 2, :], PS[:, 6 + n % 2, :].rearrange("p (h m) -> p h m", h=2))\
                    .then_inc(sem("tt_ready"), 1)
            for t in range(NT):
                r = ROWS[t]
                dve.wait_ge(sem("dt_mm"), t + 1)
                if t >= 2:
                    dve.wait_ge(sem("pool_mm"), t - 1)
                dve.tensor_copy(DT[t % 2][:, 0:4, 0:r], PS[:, 0, :].rearrange("p (k n) -> p k n", k=4)[:, :, 0:r])\
                    .then_inc(sem("dt_ready"), 1)
                dve.wait_ge(sem("pool_mm"), t + 1)
                b = 2 + 2 * (t % 2)
                dve.tensor_tensor(H[0:r, t, :], H[0:r, t, :], PS[0:r, b:b + 2, :].rearrange("p a n -> p (a n)"), ALU.add)\
                    .then_inc(sem("h_pool"), 1)

            def gained(dst, bank, which, r):
                for half in range(2):
                    g = gains[:, which, 4 * half:4 * half + 4].rearrange("p (k a) -> p k a", a=1).to_broadcast([P, 4, r])
                    ins = dve.tensor_tensor(dst[:, 4 * half:4 * half + 4, 0:r],
                                            PS[:, bank + half, :].rearrange("p (k n) -> p k n", k=4)[:, :, 0:r], g, ALU.mult)
                return ins

            def router(l):
                root(f"r{l}")
                if l == 0:
                    dve.wait_ge(sem("small_in"), 16 * SMALL)
                for t in range(NT):
                    r = ROWS[t]
                    if t >= 2:
                        dve.wait_ge(sem("un_tr"), t - 1 + l * NT)
                        dve.wait_ge(sem(f"xs_out_{t % 2}"), 16 * (t // 2) + (48 - 16 * (t % 2)) * l)
                    dve.tensor_scalar(YS[t % 2][0:r, :], H[0:r, t, :], rs[0:r, t:t + 1], None, ALU.mult).then_inc(sem("un_ready"), 1)
                    dve.wait_ge(sem("un_tr"), t + 1 + l * NT)
                    if t >= 2:
                        dve.wait_ge(sem("router_done"), t - 1 + l * NT)
                    gained(XU[t % 2], 2 * (t % 2), l, r).then_inc(sem("xu_ready"), 1)
                dve.wait_ge(sem("router_done"), NT + l * NT)

                def v(name, n=None):
                    return rt[name] if n is None else rt[name].rearrange("p (t e) -> p t e", e=n)

                def bc(name, n):
                    return rt[name].rearrange("p (t a) -> p t a", a=1).to_broadcast([P, NT, n])

                def cb(name, n):
                    return c(name).rearrange("p (a n) -> p a n", a=1).to_broadcast([P, NT, n])

                then(dve.memset(v("L"), 0.0))
                dve.tensor_copy(v("L")[:, 0:80], PS[:, 6, 0:80])
                then(dve.tensor_copy(v("L")[0:64, 80:100], PS[0:64, 6, 80:100]))
                lg = v("L", 20)[:, :, 0:4]
                le = v("L", 20)[:, :, 4:20].rearrange("p t (g e) -> p t g e", g=NG)
                then(dve.tensor_reduce(v("mx"), lg, X, ALU.max))
                dve.tensor_tensor(v("dl", 4), lg, bc("mx", 4), ALU.subtract).then_inc(sem("rt_in"), 1)
                then(dve.tensor_tensor(v("v4", 4), lg, bc("mx", 4), ALU.is_equal))
                then(dve.tensor_tensor(v("v4", 4), v("v4", 4), cb("w4", 4), ALU.mult))
                then(dve.tensor_reduce(v("vm"), v("v4", 4), X, ALU.max))
                then(dve.tensor_tensor(v("oh", 4), v("v4", 4), bc("vm", 4), ALU.is_equal))
                dve.tensor_scalar(v("pen"), v("oh"), 1.0, BIG, ALU.subtract, ALU.mult)
                ohb = v("oh").rearrange("p (n a) -> p n a", a=1).to_broadcast([P, NT * 4, 4])
                penb = v("pen").rearrange("p (n a) -> p n a", a=1).to_broadcast([P, NT * 4, 4])
                LMg = v("LM").rearrange("p (n e) -> p n e", e=4)
                for t in range(NT):
                    ins = dve.tensor_tensor(LMg[:, 4 * t:4 * t + 4, :], le[:, t], ohb[:, 4 * t:4 * t + 4, :], ALU.mult)
                then(ins)
                then(dve.tensor_tensor(LMg, LMg, penb, ALU.add))
                then(dve.tensor_reduce(v("m1"), v("LM", NE), X, ALU.max))
                then(dve.tensor_tensor(v("e1", NE), v("LM", NE), bc("m1", NE), ALU.is_equal))
                then(dve.tensor_tensor(v("e1", NE), v("e1", NE), cb("w16", NE), ALU.mult))
                then(dve.tensor_reduce(v("vm"), v("e1", NE), X, ALU.max))
                then(dve.tensor_tensor(v("oh1", NE), v("e1", NE), bc("vm", NE), ALU.is_equal))
                then(dve.scalar_tensor_tensor(out=v("LM2"), in0=v("oh1"), scalar=-2 * BIG, in1=v("LM"), op0=ALU.mult, op1=ALU.add))
                then(dve.tensor_reduce(v("m2"), v("LM2", NE), X, ALU.max))
                dve.tensor_tensor(v("d"), v("m2"), v("m1"), ALU.subtract).then_inc(sem("rt_in"), 1)
                then(dve.tensor_tensor(v("e1", NE), v("LM2", NE), bc("m2", NE), ALU.is_equal))
                then(dve.tensor_tensor(v("e1", NE), v("e1", NE), cb("w16", NE), ALU.mult))
                then(dve.tensor_reduce(v("vm"), v("e1", NE), X, ALU.max))
                then(dve.tensor_tensor(v("oh2", NE), v("e1", NE), bc("vm", NE), ALU.is_equal))
                val = c("valid").rearrange("p (t a) -> p t a", a=1).to_broadcast([P, NT, NE])
                dve.tensor_tensor(v("oh1", NE), v("oh1", NE), val, ALU.mult)
                then(dve.tensor_tensor(v("oh2", NE), v("oh2", NE), val, ALU.mult))
                dve.tensor_tensor(v("A"), v("oh1"), v("oh2"), ALU.add).then_inc(sem("picks_ready"), 1)
                dve.wait_ge(sem("rt_exp"), 1 + l * 2)
                then(dve.tensor_reduce(v("sum"), v("eg", 4), X, ALU.add))
                dve.reciprocal(v("ptop"), v("sum"))
                dve.wait_ge(sem("rt_exp"), 2 + l * 2)
                then(dve.tensor_scalar(v("den"), v("ed"), 1.0, None, ALU.add))
                then(dve.reciprocal(v("rden"), v("den")))
                then(dve.tensor_tensor(gate[:, 0, :], v("ptop"), v("rden"), ALU.mult))
                then(dve.tensor_tensor(gate[:, 1, :], gate[:, 0, :], v("ed"), ALU.mult))
                then(dve.memset(v("R"), 0.0))
                dve.wait_ge(sem("ranks"), 1 + l * 1)
                dve.tensor_copy(v("R")[:, 0:4 * NE], PS[:, 7, 0:4 * NE])
                dve.tensor_copy(v("tot")[:, :], PS[:, 7, NT * NE:NT * NE + NE])
                then(dve.tensor_copy(v("R")[0:64, 4 * NE:], PS[0:64, 7, 4 * NE:NT * NE]))
                then(dve.scalar_tensor_tensor(out=v("R", NE), in0=v("R", NE), scalar=float(NE), in1=cb("eid", NE),
                                              op0=ALU.mult, op1=ALU.add))
                dve.tensor_tensor(v("oh1"), v("oh1"), v("R"), ALU.mult)
                then(dve.tensor_tensor(v("oh2"), v("oh2"), v("R"), ALU.mult))
                dve.tensor_reduce(v("SL")[:, 0:NT], v("oh1", NE), X, ALU.add)
                then(dve.tensor_reduce(v("SL")[:, NT:], v("oh2", NE), X, ALU.add))
                then(dve.tensor_tensor(v("SS"), v("SL"), c("junk"), ALU.add))
                then(dve.tensor_scalar(v("Sm"), v("SL"), float(P * NE), None, ALU.is_lt))
                dve.tensor_tensor(gm[:, :, :].rearrange("p c t -> p (c t)"), gate[:, :, :].rearrange("p c t -> p (c t)"), v("Sm"), ALU.mult)
                then(dve.tensor_tensor(v("Sm"), v("Sm"), v("SL"), ALU.mult))
                dve.tensor_copy(SLi[:, :, :].rearrange("p c t -> p (c t)"), v("Sm"))
                then(dve.tensor_copy(SSi[:, :, :].rearrange("p c t -> p (c t)"), v("SS")))
                dve.sem_inc(sem("slots_ready"), 1)
                then(dve.tensor_reduce(v("nm"), v("tot"), X, ALU.max))
                for k in range(1, 5):
                    ins = dve.tensor_scalar(v("np")[:, k - 1:k], v("nm"), P * k + 0.5, None, ALU.is_ge)
                then(ins)
                then(dve.tensor_reduce(v("nf"), v("np"), X, ALU.add))
                then(dve.tensor_scalar(v("nf"), v("nf"), 1.0, None, ALU.add))
                dve.tensor_copy(npi[0:1, 0:1], v("nf")[0:1, :]).then_inc(sem("np_ready"), 1)

            def moe(l):
                def xt(e):
                    dve.wait_ge(sem("xt_tr"), e + 1 + l * NE)
                    gained(XT, 0, l, P).then_inc(sem("xt_ready"), 1)

                def hidden(e):
                    dve.wait_ge(sem("silu_done"), e + 1 + l * NE)
                    dve.wait_ge(sem("up_done"), e + 1 + l * NE)
                    after(dve, sem("ht_tr"), e + l * NE)
                    dve.tensor_tensor(HH, SG, PS[:, 3, :], ALU.mult).then_inc(sem("h_ready"), 1)

                xt(0)
                hidden(0)
                xt(1)
                with dve.Fori(1, NE - 1) as e:
                    hidden(e)
                    xt(e + 1)
                hidden(NE - 1)
                dve.wait_ge(sem("np_ready"), 1 + l * 1)
                npass = dve.value_load(npi[0:1, 0:1], min_val=1, max_val=RANKS // P)
                with dve.If(npass > 1):
                    with dve.Fori(1, npass) as p:
                        with dve.Fori(0, NE) as e:
                            n = p * NE + e - NE
                            dve.wait_ge(sem(f"g_step{l}"), 9 * n + 1)
                            gained(XT, 0, l, P).then_inc(sem(f"g_step{l}"), 1)
                            dve.wait_ge(sem(f"g_step{l}"), 9 * n + 4)
                            dve.tensor_tensor(HH, SG, PS[:, 3, :], ALU.mult).then_inc(sem(f"g_step{l}"), 1)
                        chain = [0]

                        def link(ins):
                            chain[0] += 1
                            ins.then_inc(sem(f"g_dve{l}"), 1)
                            dve.wait_ge(sem(f"g_dve{l}"), LINKS * p - LINKS + chain[0])

                        SL, Sm = rt["SL"], rt["Sm"]
                        link(dve.tensor_scalar(SL, SL, float(P * NE), None, ALU.subtract))
                        link(dve.tensor_scalar(Sm, SL, 0.0, None, ALU.is_ge))
                        link(dve.scalar_tensor_tensor(out=Sm, in0=SL, scalar=float(P * NE), in1=Sm, op0=ALU.is_lt, op1=ALU.mult))
                        link(dve.tensor_tensor(gg[:, :, :].rearrange("p c t -> p (c t)"), gate[:, :, :].rearrange("p c t -> p (c t)"),
                                               Sm, ALU.mult))
                        link(dve.tensor_tensor(Sm, SL, Sm, ALU.mult))
                        dve.tensor_copy(SGi[:, :, :].rearrange("p c t -> p (c t)"), Sm).then_inc(sem(f"g_sum{l}"), 1)
                        for t in range(NT):
                            r = ROWS[t]
                            dve.wait_ge(sem(f"g_yg{l}"), 32 * NT * p + 32 * (t + 1 - NT))
                            link(dve.scalar_tensor_tensor(out=H[0:r, t, :], in0=K8[0:r, 0, :], scalar=gg[0:r, 0, t:t + 1],
                                                          in1=H[0:r, t, :], op0=ALU.mult, op1=ALU.add))
                            dve.scalar_tensor_tensor(out=H[0:r, t, :], in0=K8[0:r, 1, :], scalar=gg[0:r, 1, t:t + 1],
                                                     in1=H[0:r, t, :], op0=ALU.mult, op1=ALU.add).then_inc(sem(f"g_sum{l}"), 1)
                        assert chain[0] == LINKS
                for t in range(NT):
                    r = ROWS[t]
                    dve.wait_ge(sem(f"yg_in_{t}"), 32 + l * 32)
                    for ch in range(2):
                        ins = dve.scalar_tensor_tensor(out=H[0:r, t, :], in0=K8[0:r, (2 * t + ch) % 8, :], scalar=gm[0:r, ch, t:t + 1],
                                                       in1=H[0:r, t, :], op0=ALU.mult, op1=ALU.add)
                        if ch == 0:
                            then(ins)
                    ins.then_inc(sem("h_sum"), 1)

            router(0)
            moe(0)

            root("proj")
            then(dve.memset(LF[:, :, :], 0.0))
            dve.memset(hms[:, :, :], 1.0)
            dve.memset(hss[:, :, :], 1.0)
            ins = dve.tensor_scalar(qg[:, :], qg[:, :], float(DH) ** -0.5, None, ALU.mult)
            then(ins)

            def head_norm(which, r, t):
                dve.wait_ge(sem("head_sq"), 2 * t + which + 1)
                then(dve.tensor_reduce(hss[0:r, which, :], SQ[0:r, :].rearrange("p (h d) -> p h d", d=DH), X, ALU.add))
                dve.tensor_scalar(hms[0:r, which, :], hss[0:r, which, :], 1.0 / DH, EPS, ALU.mult, ALU.add).then_inc(sem("head_ms"), 1)
                dve.wait_ge(sem("head_sd"), 2 * t + which + 1)
                then(dve.reciprocal(hrs[:, which, :], hsd[:, which, :]))
                return hrs[0:r, which, :].rearrange("p (h a) -> p h a", a=1).to_broadcast([r, NH, DH])

            for t in range(NT):
                r = ROWS[t]
                heads = lambda a: a.rearrange("p (h d) -> p h d", d=DH)
                two = lambda b: PS[0:r, b:b + 2, :].rearrange("p a (h d) -> p (a h) d", d=DH)
                if t:
                    dve.wait_ge(sem("proj_tr"), 3 * t - 2)
                dve.tensor_scalar(UN[0:r, :], H[0:r, t, :], rs[0:r, t:t + 1], None, ALU.mult).then_inc(sem("pun_ready"), 1)
                dve.wait_ge(sem("proj_tr"), 3 * t + 1)
                if t:
                    dve.wait_ge(sem("proj_mm"), 4 * t)
                gained(UK, 0, 2, r).then_inc(sem("ux_ready"), 1)
                gained(UQ, 0, 3, r).then_inc(sem("ux_ready"), 1)
                rk = head_norm(0, r, t)
                if t:
                    dve.wait_ge(sem("proj_tr"), 3 * t - 1)
                    dve.wait_ge(sem("kout"), 16 * t)
                dve.tensor_tensor(heads(KN[0:r, :]), two(2), rk, ALU.mult).then_inc(sem("kn_ready"), 1)
                dve.wait_ge(sem("kn_ready"), 2 * t + 1)
                kg = kgb[0:r, :].rearrange("p (a d) -> p a d", a=1).to_broadcast([r, NH, DH])
                dve.tensor_tensor(heads(KN[0:r, :]), heads(KN[0:r, :]), kg, ALU.mult).then_inc(sem("kn_ready"), 1)
                dve.wait_ge(sem("proj_mm"), 4 * t + 2)
                dve.tensor_tensor(LF[0:r, t, :], PS[0:r, 6, 0:NH], bfb[0:r, :], ALU.add).then_inc(sem("f_ready"), 1)
                rq = head_norm(1, r, t)
                dve.sem_inc(sem("ssq_ready"), 1)
                if t:
                    dve.wait_ge(sem("proj_tr"), 3 * t - 0)
                dve.tensor_tensor(heads(QN[0:r, :]), two(6), rq, ALU.mult).then_inc(sem("qn_ready"), 1)
            lf = LF[:, :, :].rearrange("p t h -> p (t h)")
            dve.wait_ge(sem("f_ready"), NT)
            then(dve.scalar_tensor_tensor(out=lfa, in0=lf, scalar=-1.0, in1=lf, op0=ALU.mult, op1=ALU.max))
            dve.sem_inc(sem("lf_step"), 1)
            dve.wait_ge(sem("lf_step"), 2)
            dve.tensor_scalar(lfe, lfe, 1.0, None, ALU.add).then_inc(sem("lf_step"), 1)
            dve.wait_ge(sem("lf_step"), 4)
            then(dve.scalar_tensor_tensor(out=lf, in0=lf, scalar=0.0, in1=lfa, op0=ALU.min, op1=ALU.subtract))
            dve.sem_inc(sem("lf_step"), 1)
            dve.wait_ge(sem("proj_mm"), 4 * NT)
            dve.tensor_copy(LR[0:64, :].rearrange("p (h q) -> p h q", q=NS),
                            LF[0:64, 4, :].rearrange("p (h a) -> p h a", a=1).to_broadcast([64, NH, NS])).then_inc(sem("lr_ready"), 1)
            dve.memset(PR[:, :], 1.0).then_inc(sem("one_ready"), 1)
            dve.memset(OTS[:, :, 4 * P:4 * P + 64], 0.0)
            dve.memset(PTT[:, :, 64:80], 0.0)
            then(dve.memset(QBLK[:, :, :], 0.0))
            dve.wait_ge(sem("nb_mm"), 1)
            sm = c("smask", 64).rearrange("p (b n) -> p b n", b=NB)
            for b in range(NB):
                ins = dve.tensor_tensor(sm[:, b, :], sm[:, b, :], PS[0:64, 4, 0:64], ALU.add)
            then(ins)
            dve.wait_ge(sem("qts_ready"), NT)
            dve.wait_ge(sem("ct_ready"), 2)
            dve.wait_ge(sem("ktd_out"), 32 * NT + 16)
            dve.wait_ge(sem("qtd_out"), 32 * NT + 16)
            dve.wait_ge(sem("kout"), 16 * (NT + 1))
            dve.wait_ge(sem("vout"), 16 * NT)
            dve.sem_inc(sem("proj_done"), 1)

            def attention(i):
                one = isinstance(i, int)

                def evac(n):
                    dve.wait_ge(sem("kt_tr"), 32 * i + n + 1)
                    after(dve, sem("qk_done"), 16 * i + n // 2 - 1)
                    dve.tensor_copy(KTR[:, n % 4, :], PS[:, n % 2, :]).then_inc(sem("kt_even"), 1)

                def pmax(u):
                    t = u % 5
                    r = P if t < 4 else LASTP
                    nk = P * (t + 1) if t < 4 else 4 * P
                    dve.wait_ge(sem("pu_s"), 10 * i + u + 1)
                    after(dve, sem("pu_exp"), 10 * i + u)
                    if t < 4:
                        dve.tensor_reduce(pst[0:r, 0:1], PS[0:r, 6, 0:nk], X, ALU.max, negate=True).then_inc(sem("pu_max"), 1)
                    else:
                        dve.tensor_reduce(pst[0:r, 1:2], PS[0:r, 6, 0:nk], X, ALU.max, negate=True)
                        dve.tensor_reduce(pst[0:r, 2:3], PS[0:r, 5, 0:r], X, ALU.max, negate=True).then_inc(sem("pu_mx2"), 1)
                        dve.wait_ge(sem("pu_mx2"), 2 * i + u // 5 + 1)
                        dve.tensor_tensor(pst[0:r, 0:1], pst[0:r, 1:2], pst[0:r, 2:3], ALU.min).then_inc(sem("pu_max"), 1)

                def pnorm(u):
                    t = u % 5
                    r = P if t < 4 else LASTP
                    nk = P * (t + 1) if t < 4 else TP
                    dve.wait_ge(sem("pu_exp"), 10 * i + u + 1)
                    if t == 4:
                        dve.tensor_tensor(pst[0:r, 3:4], pst[0:r, 4:5], pst[0:r, 5:6], ALU.add).then_inc(sem("pu_sum"), 1)
                        dve.wait_ge(sem("pu_sum"), 2 * i + u // 5 + 1)
                    dve.reciprocal(pst[0:r, 6:7], pst[0:r, 3:4]).then_inc(sem("pu_rec"), 1)
                    dve.wait_ge(sem("pu_rec"), 10 * i + u + 1)
                    dve.tensor_scalar(PR[0:r, 0:nk], PR[0:r, 0:nk], pst[0:r, 6:7], None, ALU.mult).then_inc(sem("pu_norm"), 1)

                def pts(u):
                    t = u % 5
                    dve.wait_ge(sem("pu_t"), 10 * i + u + 1)
                    after(dve, sem("pu_v"), 10 * i + u)
                    if t < 4:
                        dve.tensor_copy(PTS[:, 0:P * (t + 1)], PS[:, 7, 0:P * (t + 1)]).then_inc(sem("pu_pts"), 1)
                    else:
                        r = LASTP
                        dve.tensor_copy(PTS[:, 0:4 * r], PS[:, 7, 0:4 * r])
                        dve.tensor_copy(PTS[0:r, 4 * r:5 * r], PS[0:r, 7, 4 * r:5 * r]).then_inc(sem("pu_pts"), 1)

                after(dve, sem("s_mm"), 4 * i)
                for half in range(2):
                    for a in range(2):
                        src = QT4[DH * half:DH * half + DH, 4 * a:4 * a + 4, :]
                        src = src[:, :, S0 + NS * i:S0 + NS * i + NS] if one else src[:, :, bass.ds(NS * i + S0, NS)]
                        lo = QBLK[DH * half:DH * half + DH, 4 * a:4 * a + 4, :].rearrange("p k n -> p (k n)")
                        for p in range(4):
                            at = 40 * p + NS * half
                            ins = dve.tensor_copy(lo[:, at:at + NS], src[:, p, :])
                for g0 in range(0, PAGES, 4):
                    src = RP[:, :, PAGES * i + g0:PAGES * i + g0 + 4] if one else RP[:, :, bass.ds(PAGES * i + g0, 4)]
                    for g in range(4):
                        ins = dve.tensor_copy(RBB[:, g0 + g, :].rearrange("p (h q) -> p h q", q=NS),
                                              src[:, :, g:g + 1].to_broadcast([P, NH, NS]))
                ins.then_inc(sem("qb_ready"), 1)
                dve.wait_ge(sem("sn_mm"), i + 1)
                after(dve, sem("ptt_tr"), 3 * i)
                m = sm[:, i, :] if one else sm[:, bass.ds(i, 1), :].rearrange("p a n -> p (a n)")
                dve.tensor_tensor(SROW[0:64, PAGES * PAGE:], PS[0:64, 2, 0:64], m, ALU.add).then_inc(sem("sn_ready"), 1)
                dve.wait_ge(sem("sn_ready"), i + 1)
                dve.tensor_reduce(smx[0:64, NCH:NCH + 1], SROW[0:64, PAGES * PAGE:], X, ALU.max)
                for n in range(TICKS):
                    if n < 32 and n % 2 == 0:
                        evac(n)
                    if n >= 5 and (n - 5) % 8 == 7 and (n - 5) // 8 < 4:
                        ch = (n - 5) // 8
                        dve.wait_ge(sem("s_ready"), 4 * i + ch + 1)
                        ins = dve.tensor_reduce(smx[0:64, ch:ch + 1], SROW[0:64, 512 * ch:512 * ch + 512], X, ALU.max)
                        if ch == NCH - 1:
                            ins.then_inc(sem("smx_ready"), 1)
                            dve.wait_ge(sem("smx_ready"), i + 1)
                            dve.tensor_reduce(sst[0:64, 0:1], smx[0:64, :], X, ALU.max, negate=True).then_inc(sem("sp_max"), 1)
                    u, w = (n - T0) // 4, (n - T0) % 4
                    if w == 0 and 0 <= u < 10:
                        pmax(u)
                    if w == 2 and 0 <= u < 10:
                        pnorm(u)
                    if w == 0 and 1 <= u < 11:
                        pts(u - 1)
                    if n == PTICKS[0] - 1:
                        dve.wait_ge(sem("sp_exp"), i + 1)
                        dve.reciprocal(sst[0:64, 2:3], sst[0:64, 1:2]).then_inc(sem("sp_rec"), 1)
                        dve.wait_ge(sem("sp_rec"), i + 1)
                        dve.tensor_scalar(SROW[0:64, :], SROW[0:64, :], sst[0:64, 2:3], None, ALU.mult).then_inc(sem("sp_norm"), 1)
                    if n in PTICKS:
                        part = PTICKS.index(n)
                        dve.wait_ge(sem("ptt_tr"), 3 * i + part + 1)
                        after(dve, sem("o_mm"), i)
                        if part < 2:
                            dve.tensor_copy(PTT[:, 8 * part:8 * part + 8, 0:64], PS[:, 4, :].rearrange("p (g n) -> p g n", n=64))\
                                .then_inc(sem("ptt_ready"), 1)
                        else:
                            dve.tensor_copy(PTT[0:64, PAGES, 0:64], PS[0:64, 4, 0:64]).then_inc(sem("ptt_ready"), 1)
                dve.wait_ge(sem("ob_tr"), i + 1)
                for half in range(2):
                    for x in range(2):
                        rows = slice(DH * half, DH * half + DH)
                        src = PS[rows, 5, 256 + x * P:256 + (x + 1) * P].rearrange("p (q n) -> p q n", q=4)[:, :, 8 * x + 4 * half:8 * x + 4 * half + NS]
                        dst = OTS[rows, x:HP:2, :]
                        dst = dst[:, :, 4 * P + S0 + NS * i:4 * P + S0 + NS * i + NS] if one else dst[:, :, bass.ds(NS * i + 4 * P + S0, NS)]
                        ins = dve.tensor_copy(dst, src)
                    ins.then_inc(sem("ots_ready"), 1)

            attention(0)
            with dve.Fori(1, NB) as i:
                attention(i)

            for t in range(NT):
                r = ROWS[t]
                dve.wait_ge(sem("wo_done"), t + 1)
                b = 2 * (t % 2)
                dve.tensor_tensor(H[0:r, t, :], H[0:r, t, :], PS[0:r, b:b + 2, :].rearrange("p a n -> p (a n)"), ALU.add)\
                    .then_inc(sem("h_attn"), 1)
            router(1)
            moe(1)

        assert n_out[0] == OUTS, n_out


INPUTS = ["x_prompt", "x_sample", "state_pool", "cache_k", "cache_v", "cache_logf", "page_table", "meta", "pool_norm_g",
          "pool_w", "pool_scale", "kv_norm_g", "w_kvf", "b_f", "k_norm_g", "attn_norm_g", "w_q", "q_norm_g", "w_o",
          "ffn_norm_g", "w_router_group", "w_router_expert", "w_gate", "w_up", "w_down"]
OUTPUTS = [("y_prompt", (1, SEQ, D)), ("y_sample", (NB, NS, D)), ("pool_state_prompt", (1, 1, STATE, D)),
           ("pool_state_sample", (1, NB, STATE, D)), ("k_prompt", (1, TP, NH, DH)), ("v_prompt", (1, TP, NH, DH)),
           ("logf_prompt", (1, TP, NH)), ("k_sample", (NB, NS, NH, DH)), ("v_sample", (NB, NS, NH, DH)),
           ("logf_sample", (NB, NS, NH))]


def kernel(**inputs):
    import concourse.bacc as bacc
    from concourse.bass_utils import run_bass_kernel_spmd

    nc = bacc.Bacc("TRN2", target_bir_lowering=False, num_devices=1)
    consts, bands, ids = shape_constants()
    arrays = {name: np.ascontiguousarray(inputs[name]) for name in INPUTS}
    arrays.update(consts=consts, bands=bands, ids=ids)
    A = {name: nc.dram_tensor(f"in_{name}", a.shape, mybir.dt.from_np(a.dtype), kind="ExternalInput").ap()
         for name, a in arrays.items()}
    O = {name: nc.dram_tensor(f"out_{name}", shape, F32, kind="ExternalOutput").ap() for name, shape in OUTPUTS}
    build(nc, A, O)
    r = run_bass_kernel_spmd(nc, [{f"in_{name}": a for name, a in arrays.items()}], core_ids=[0])
    return tuple(r.results[0][f"out_{name}"] for name, _ in OUTPUTS)
```

```python
from contextlib import ExitStack

import numpy as np

import concourse.bass as bass
from concourse import mybir
from concourse.alu_op_type import AluOpType as ALU

F32 = mybir.dt.float32
I32 = mybir.dt.int32
ACT = mybir.ActivationFunctionType
X = mybir.AxisListType.X

P = 128
D = 1024
KC = D // P
META, SEQ = 16, 512
TP = META + SEQ
NT = 5
ROWS = [P, P, P, P, 64]
LASTP = TP - 4 * P
S0 = 32
NB, NS = 8, 4
WINDOWS = (2, 4, 8, 16)
NG = 4
GD = D // NG
STATE = 15
NH, DH = 16, 64
HP = NH // 2
NE = 16
FF = D // 2
FC = FF // P
PAGES, PAGE = 16, 128
CH = 4
NCH = PAGES // CH
BIG = 1e30
EPS = 1e-6
RANKS = 5 * P
LISTN = RANKS * NE + P
LINKS = 5 + NT
SMALL = 20
NORMS = ("pool", "r0", "r1")
OUTS = 14

KTICKS = 32
TICKS = KTICKS + 2
UNITS = 10
S_TICK = [3 * u + 1 for u in range(UNITS)]
T_TICK = [3 * u + 4 for u in range(UNITS)]
V_TICK = [3 * u + 5 for u in range(UNITS)]
QK_TICK = [2 * x + 3 for x in range(KTICKS // 2)]
NEW_TICK = 18
P_TICK = (5, 7, 9, 11, 16)
O_TICK = [g + 8 for g in range(PAGES + 1)]
OT_TICK = 27

CONST = {}
_at = 0
for _name, _n in (("ident", P), ("tails", P), ("before", P), ("upto", P), ("after", P), ("ones", P), ("causal", P),
                  ("negnew", 64), ("smask", NB * 64), ("w4", 4), ("w16", NE), ("eid", NE),
                  ("valid", NT), ("junk", 2 * NT)):
    CONST[_name] = (_at, _at + _n)
    _at += _n
NCONST = _at
BAND = {}
_at = 0
for _name, _n in (("cur0", P), ("cur", P), ("prev", P), ("cur4", 64), ("prev4", 64), ("state", 64)):
    BAND[_name] = (_at, _at + NG * _n, _n)
    _at += NG * _n
NBAND = _at


def shape_constants():
    c = np.zeros((P, NCONST), np.float32)

    def put(name, a):
        lo, hi = CONST[name]
        a = np.asarray(a, np.float32).reshape(np.shape(a)[0], -1)
        c[:a.shape[0], lo:hi] = a

    i = np.arange(P)
    put("ident", np.eye(P))
    b, g = i // PAGES, i % PAGES
    put("tails", (b[:, None] == b[None]) & (g[:, None] > g[None]))
    put("before", i[:, None] < i[None])
    put("upto", i[:, None] <= i[None])
    put("after", i[:, None] > i[None])
    put("ones", np.ones((P, P)))
    put("causal", np.where(i[None] <= i[:, None], 0.0, -BIG))
    r = np.arange(64)
    sb, ss = (r - S0) // NS, (r - S0) % NS
    new = r >= S0
    put("negnew", -1.0 * (new[:, None] & new[None] & (sb[:, None] == sb[None]) & (ss[:, None] <= ss[None])))
    q = i % NS
    see = new[None, None] & (sb[None, None] == np.arange(NB)[None, :, None]) & (ss[None, None] <= q[:, None, None])
    put("smask", np.where(see, 0.0, -BIG))
    put("w4", np.tile(4.0 - np.arange(4), (P, 1)))
    put("w16", np.tile(NE - np.arange(NE), (P, 1)))
    put("eid", np.tile(np.arange(NE), (P, 1)))
    valid = np.ones((P, NT))
    valid[LASTP:S0, 4] = 0
    valid[64:, 4] = 0
    put("valid", valid)
    junk = np.zeros((P, 2, NT))
    junk[:64, 0, 4] = np.where(valid[:64, 4] == 0, RANKS * NE + r, 0)
    junk[:64, 1, 4] = np.where(valid[:64, 4] == 0, RANKS * NE + 64 + r, 0)
    put("junk", junk)

    w = np.zeros((P, NBAND), np.float32)

    def band(name, rows, cols, f):
        lo, hi, n = BAND[name]
        a = np.zeros((P, NG, n), np.float32)
        for g, win in enumerate(WINDOWS):
            for s in range(rows):
                for t in range(cols):
                    a[s, g, t] = f(win, s, t)
        w[:, lo:hi] = a.reshape(P, -1)

    def own(win, s, t):
        return float(s == t)

    band("cur0", P, P, lambda n, s, t: (t - n < s <= t) / min(t + 1, n) - own(n, s, t))
    band("cur", P, P, lambda n, s, t: (t - n < s <= t) / n - own(n, s, t))
    band("prev", P, P, lambda n, s, t: (s - P > t - n) / n)

    def cur4(n, s, t):
        if s < LASTP and t < LASTP:
            return (t - n < s <= t) / n - own(n, s, t)
        if s >= S0 and t >= S0 and (s - S0) // NS == (t - S0) // NS:
            return (t - n < s <= t) / n - own(n, s, t)
        return 0.0

    band("cur4", 64, 64, cur4)
    band("prev4", P, LASTP, lambda n, s, t: (s - P > t - n) / n)

    def state(n, s, t):
        if t < S0 or s // STATE != (t - S0) // NS:
            return 0.0
        return (s % STATE - STATE > (t - S0) % NS - n) / n

    band("state", NB * STATE, 64, state)
    ids = (np.arange(NT)[None] * P + np.arange(P)[:, None]).astype(np.int32)
    return c, w, ids


def after(eng, sem, value):
    if isinstance(value, int) and value <= 0:
        return
    eng.wait_ge(sem, value)


def build(nc, A, O):
    ctx = ExitStack()
    with ctx:
        ctx.enter_context(nc.allow_non_contiguous_dma(reason="gains, router weights and row lists, small"))

        def sb(name, shape, dt=F32):
            return ctx.enter_context(nc.sbuf_tensor(name, shape, dt))

        sems = {}

        def sem(name):
            if name not in sems:
                sems[name] = ctx.enter_context(nc.semaphore(name))
            return sems[name]

        H = sb("H", [P, NT, D])
        W = sb("W", [P, 6, 4 * D])
        KB = sb("KB", [P, 2, 4 * D])
        VB = sb("VB", [P, 2, 4 * D])
        C = sb("C", [P, NCONST])
        ids = sb("ids", [P, NT], I32)
        gains = sb("gains", [P, 4, KC])
        qg = sb("qg", [P, 1])
        kgb = sb("kgb", [P, DH])
        bfb = sb("bfb", [P, NH])
        wr = sb("wr", [P, 2, KC, NG + NE])
        wf = sb("wf", [P, KC, NH])
        pt = sb("pt", [1, NB * PAGES], I32)
        ptc = sb("ptc", [P, 1], I32)
        zi = sb("zi", [P, LISTN // P], I32)
        ss = sb("ss", [P, NT])
        ms = sb("ms", [P, NT])
        sd = sb("sd", [P, NT])
        rs = sb("rs", [P, NT])
        KT4 = sb("KT4", [P, HP, 64])
        QT4 = sb("QT4", [P, HP, 64])
        V4 = sb("V4", [P, D])
        BIAS = sb("BIAS", [P, PAGES * PAGE])
        LF = sb("LF", [P, NT, NH])
        SLi = sb("SLi", [P, 2, NT], I32)
        SSi = sb("SSi", [P, 2, NT], I32)
        gate = sb("gate", [P, 2, NT])
        gm = sb("gm", [P, 2, NT])
        gg = sb("gg", [P, 2, NT])
        SGi = sb("SGi", [P, 2, NT], I32)
        IDX = sb("IDX", [P, NE], I32)
        idc = sb("idc", [P, 2], I32)
        npi = sb("npi", [1, 1], I32)
        idg = sb("idg", [P, 1], I32)
        hss = sb("hss", [P, 2, NH])
        hms = sb("hms", [P, 2, NH])
        hsd = sb("hsd", [P, 2, NH])
        hrs = sb("hrs", [P, 2, NH])

        def c(name, rows=P):
            lo, hi = CONST[name]
            return C[0:rows, lo:hi]

        ident = c("ident")
        PS = ctx.enter_context(nc.psum_tensor("PS", [P, 8, 512], F32))

        K8 = KB[:, :, :].rearrange("p a (b n) -> p (a b) n", n=D)
        V8 = VB[:, :, :].rearrange("p a (b n) -> p (a b) n", n=D)
        Vf = VB[:, :, :].rearrange("p a n -> p (a n)")
        U = [K8[:, t, :] for t in range(NT)]
        ST = K8[:, 5, :]
        DT = [K8[:, 6 + j, :].rearrange("p (k n) -> p k n", k=8) for j in range(2)]
        bands = Vf[:, 0:NBAND]
        pw = Vf[:, NBAND:NBAND + 2 * D].rearrange("p (g c n) -> p g c n", g=NG, c=2)
        png = Vf[:, NBAND + 2 * D:NBAND + 3 * D]
        psc = Vf[:, NBAND + 3 * D:NBAND + 4 * D]
        LP = W[:, 5, 0:2 * D].rearrange("p (r h) -> p r h", h=NH)
        TT = W[:, 4, :].rearrange("p (h n) -> p h n", h=NH)
        RQ = BIAS[:, :].rearrange("p (h n) -> p h n", h=NH)
        XG = [V8[:, j, :] for j in range(2)]
        YS = [V8[:, 2 + j, :] for j in range(2)]
        XT = V8[:, 4, :].rearrange("p (k n) -> p k n", k=KC)
        SG = V8[:, 5, 0:FF]
        HH = V8[:, 5, FF:2 * FF]
        HT = V8[:, 6, 0:FF].rearrange("p (f n) -> p f n", f=FC)
        XU = [V8[:, j, :].rearrange("p (k n) -> p k n", k=KC) for j in range(2)]

        rt = {}
        at = 6 * D + FF
        for name, n in (("L", NT * 20), ("mx", NT), ("dl", NT * 4), ("eg", NT * 4), ("sum", NT), ("ptop", NT),
                        ("oh", NT * 4), ("v4", NT * 4), ("vm", NT), ("pen", NT * 4), ("LM", NT * NE), ("LM2", NT * NE),
                        ("m1", NT), ("m2", NT), ("e1", NT * NE), ("oh1", NT * NE), ("oh2", NT * NE), ("A", NT * NE),
                        ("ed", NT), ("den", NT), ("rden", NT), ("R", NT * NE), ("SL", 2 * NT), ("SS", 2 * NT), ("Sm", 2 * NT),
                        ("tot", NE), ("nm", 1), ("np", 4), ("nf", 1), ("d", NT)):
            rt[name] = Vf[:, at:at + n]
            at += n
        assert at <= 8 * D
        UN = V8[:, 0, :]
        UK = [a.rearrange("p (k n) -> p k n", k=KC) for a in (V8[:, 1, :], K8[:, 4, :])]
        UQ = [a.rearrange("p (k n) -> p k n", k=KC) for a in (V8[:, 2, :], K8[:, 5, :])]
        UPPER = K8[:, 6, :]
        SQ = V8[:, 3, :]
        KN = V8[:, 4, :]
        QN = V8[:, 5, :]
        VN = V8[:, 6, :]
        TS = V8[:, 7, :].rearrange("p (k n) -> p k n", k=HP)
        Wf = W[:, :, :].rearrange("p a n -> p (a n)")
        aat = [0]

        def carve(n):
            aat[0] += n
            return Wf[:, aat[0] - n:aat[0]]

        KTR = carve(4 * 512).rearrange("p (s n) -> p s n", s=4)
        SROW = carve(PAGES * PAGE + 64)
        PTT = carve((PAGES + 1) * P).rearrange("p (g n) -> p g n", n=P)
        QST = [carve(TP) for _ in range(2)]
        KST = [carve(TP) for _ in range(2)]
        VST = carve(NT * P).rearrange("p (t n) -> p t n", n=P)
        PR = carve(TP)
        PTS = carve(4 * P)
        QBLK = carve(HP * 32).rearrange("p (k n) -> p k n", n=32)
        OB = carve(256)
        smx = carve(NCH + 1)
        sst = carve(4)
        pst = carve(12)
        CT = carve(TP)
        LR = carve(P)
        lfa = carve(NT * NH)
        lfe = carve(NT * NH)
        nots = HP * (4 * P + 64)
        OTS = Wf[:, 4 * 4 * D - nots:4 * 4 * D].rearrange("p (k n) -> p k n", k=HP)
        assert aat[0] + nots <= 4 * 4 * D, aat
        VSL = [VB[:, 0, :], VB[:, 1, :], W[:, 4, :], W[:, 5, :]]

        def paged(a):
            return a.rearrange("p (g n) -> p g n", n=D)

        XS = nc.dram_tensor("xs", (4 * P + 64, D), F32).ap()
        LIST = [nc.dram_tensor(f"list{i}", (LISTN, 1), I32).ap() for i in range(2)]
        YD = [nc.dram_tensor(f"yd{i}", (P * NE, D), F32).ap() for i in range(2)]
        YG = [nc.dram_tensor(f"yg{i}", (P * NE, D), F32).ap() for i in range(2)]
        QTD = nc.dram_tensor("qtd", (NH, DH + 1, TP), F32).ap()
        KTD = nc.dram_tensor("ktd", (NH, DH + 1, TP), F32).ap()
        RPD = nc.dram_tensor("rpd", (NH, NS, NB * PAGES, PAGE), F32).ap()
        k_rows = A["cache_k"].rearrange("n r h d -> (n r) (h d)")
        v_rows = A["cache_v"].rearrange("n r h d -> (n r) (h d)")
        kp_out = O["k_prompt"].rearrange("a t h d -> (a t) (h d)")
        vp_out = O["v_prompt"].rearrange("a t h d -> (a t) (h d)")
        fp_out = O["logf_prompt"].rearrange("a t h -> (a t) h")
        ks_out = O["k_sample"].rearrange("b s h d -> (b s) (h d)")
        vs_out = O["v_sample"].rearrange("b s h d -> (b s) (h d)")
        fs_out = O["logf_sample"].rearrange("b s h -> (b s) h")
        xs_rows = A["x_sample"].rearrange("b s d -> (b s) d")
        wkvf = A["w_kvf"].rearrange("(p k) n -> p k n", k=KC)
        wq = A["w_q"].rearrange("l (p k) n -> (l p) k n", k=KC)
        wo = A["w_o"].rearrange("l (k p) n -> p (l k) n", p=P)

        n_out = [0]

        def put_out(eng, dst, src):
            n_out[0] += 1
            eng.dma_start(dst, src).then_inc(sem("out_done"), 16)

        def w_src(l, e, which):
            if which < 2:
                return A["w_gate" if which == 0 else "w_up"][l, e].rearrange("(p k) f -> p (k f)", k=KC)
            return A["w_down"][l, e].rearrange("(p f) n -> p (f n)", f=FC)

        def w_src_dyn(l, e, which):
            name = ("w_gate", "w_up", "w_down")[which]
            t = A[name][l]
            if which < 2:
                return t[bass.ds(e, 1)].rearrange("e (p k) f -> p (e k f)", k=KC)
            return t[bass.ds(e, 1)].rearrange("e (p f) n -> p (e f n)", f=FC)

        def settled(eng):
            eng.nop(nofuse=True)

        block = ctx.enter_context(nc.Block())

        @block.sync
        def _(sp):
            sp.dma_start(C[:, :], A["consts"]).then_inc(sem("consts_in"), 16)
            sp.wait_ge(sem("zeros"), 1)
            sp.dma_start(H[0:META, 0, :], A["meta"]).then_inc(sem("rows_in"), 16)
            sp.dma_start(H[META:P, 0, :], A["x_prompt"][0, 0:P - META, :]).then_inc(sem("rows_in"), 16)
            for t in range(1, 4):
                sp.dma_start(H[:, t, :], A["x_prompt"][0, t * P - META:(t + 1) * P - META, :]).then_inc(sem("rows_in"), 16)
            sp.dma_start(H[0:LASTP, 4, :], A["x_prompt"][0, 4 * P - META:SEQ, :]).then_inc(sem("rows_in"), 16)
            sp.dma_start(H[S0:64, 4, :], xs_rows).then_inc(sem("rows_in"), 16)
            sp.dma_start(png, A["pool_norm_g"][0:1, :].to_broadcast([P, D])).then_inc(sem("pool_in"), 16)
            sp.dma_start(psc, A["pool_scale"][0:1, :].to_broadcast([P, D])).then_inc(sem("pool_in"), 16)
            sp.dma_start(bands, A["bands"]).then_inc(sem("pool_in"), 16)
            sp.dma_start(ST[0:NB * STATE, :], A["state_pool"].rearrange("a b s d -> (a b s) d")).then_inc(sem("pool_in"), 16)
            sp.dma_start(pw, A["pool_w"].rearrange("a g (c p) n -> p (a g) c n", p=P)).then_inc(sem("pool_in"), 16)
            for n, (name, l) in enumerate((("ffn_norm_g", 0), ("ffn_norm_g", 1), ("kv_norm_g", None), ("attn_norm_g", 0))):
                g = A[name] if l is None else A[name][l]
                sp.dma_start(gains[:, n, :], g.rearrange("(p k) -> p k", k=KC)).then_inc(sem("small_in"), 16)
            for l in range(2):
                sp.dma_start(wr[:, l, :, 0:NG], A["w_router_group"][l].rearrange("(p k) n -> p k n", k=KC))\
                    .then_inc(sem("small_in"), 16)
                for g in range(NG):
                    sp.dma_start(wr[:, l, :, NG + 4 * g:NG + 4 * g + 4],
                                 A["w_router_expert"][l, g].rearrange("(p k) n -> p k n", k=KC)).then_inc(sem("small_in"), 16)
            sp.dma_start(wf[:, :, :], wkvf[:, :, 2 * D:2 * D + NH]).then_inc(sem("small_in"), 16)
            for half in range(2):
                sp.dma_start(qg[half * DH:(half + 1) * DH, :], A["q_norm_g"].rearrange("a d -> d a")).then_inc(sem("small_in"), 16)
            sp.dma_start(kgb[:, :], A["k_norm_g"].rearrange("(a d) -> a d", a=1).to_broadcast([P, DH])).then_inc(sem("small_in"), 16)
            sp.dma_start(bfb[:, :], A["b_f"].rearrange("(a d) -> a d", a=1).to_broadcast([P, NH])).then_inc(sem("small_in"), 16)
            sp.dma_start(pt[:, :], A["page_table"].rearrange("(a b) g -> a (b g)", a=1)).then_inc(sem("small_in"), 16)
            n_out[0] += 1
            sp.dma_start(O["pool_state_sample"][0, :, 0:STATE - NS, :], A["state_pool"][0, :, NS:STATE, :])\
                .then_inc(sem("out_done"), 16)

            def moe_weights(l):
                def load(e, which, j):
                    done = sem(f"{('gate', 'up', 'down')[which]}_done")
                    if isinstance(e, int):
                        after(sp, done, e - 1 + l * NE)
                        sp.dma_start(W[:, 3 * j + which, :], w_src(l, e, which)).then_inc(sem(f"w_in_{3 * j + which}"), 16)
                    else:
                        sp.wait_ge(done, e - 1 + l * NE)
                        settled(sp)
                        sp.dma_start(W[:, 3 * j + which, :], w_src_dyn(l, e, which)).then_inc(sem(f"w_in_{3 * j + which}"), 16)

                def first(part):
                    if part == 0:
                        load(0, 0, 0)
                        load(0, 1, 0)
                    else:
                        load(0, 2, 0)
                        load(1, 0, 1)

                def second():
                    load(1, 1, 1)
                    load(1, 2, 1)

                def rest():
                    with sp.Fori(2, NE - 1, 2) as e:
                        for j in range(2):
                            for which in range(3):
                                load(e + j, which, j)
                return first, second, rest

            def moe_rest(l):
                sp.wait_ge(sem("scattered"), 16 * 2 * NT + l * (32 * NT))
                sp.dma_start(IDX[:, :], LIST[l][0:P * NE, :].rearrange("(r e) o -> r (e o)", e=NE)).then_inc(sem("idx_in"), 16)

            def moe_general(l):
                sp.wait_ge(sem("np_ready"), 1 + l * 1)
                npass = sp.value_load(npi[0:1, 0:1], min_val=1, max_val=RANKS // P)
                with sp.If(npass > 1):
                    sp.wait_ge(sem("down_done"), NE + l * NE)
                    with sp.Fori(1, npass) as p:
                        with sp.Fori(0, NE) as e:
                            n = p * NE + e - NE
                            sp.dma_start(idg[:, :], LIST[l][0:RANKS * NE, :].rearrange("(r e) o -> r (e o)", e=NE)
                                         [bass.ds(p * P, P), bass.ds(e, 1)]).then_inc(sem(f"g_in{l}"), 16)
                            for which in range(3):
                                sp.dma_start(W[:, which, :], w_src_dyn(l, e, which)).then_inc(sem(f"g_in{l}"), 16)
                            sp.wait_ge(sem(f"g_y_out{l}"), 16 * (n + 1))
                            settled(sp)
                        sp.wait_ge(sem(f"g_sum{l}"), 6 * p)
                        settled(sp)
                sp.nop()

            first, second, rest = moe_weights(0)
            first(0)
            first(1)
            sp.wait_ge(sem("r_done"), 4)
            second()
            sp.wait_ge(sem("u_ready"), NT)
            sp.dma_start(O["pool_state_prompt"][0, 0], U[4][LASTP - STATE:LASTP, :]).then_inc(sem("state_out"), 16)
            for b in range(NB):
                sp.dma_start(O["pool_state_sample"][0, b, STATE - NS:STATE, :], U[4][S0 + NS * b:S0 + NS * b + NS, :])\
                    .then_inc(sem("state_out"), 16)
            moe_rest(0)
            rest()
            moe_general(0)
            for which, done in ((0, "gate"), (1, "up"), (2, "down"), (3, "gate"), (4, "up"), (5, "down")):
                sp.wait_ge(sem(f"{done}_done"), NE - 1 if which < 3 else NE)
                src = wkvf[:, :, 512 * which:512 * which + 512] if which < 4 else wq[:, :, 512 * (which - 4):512 * (which - 3)]
                sp.dma_start(W[:, which, :].rearrange("p (k n) -> p k n", k=KC), src)\
                    .then_inc(sem(f"proj_in_{'kvq'[which // 2]}"), 16)

            def load_chunk(dst, rows, i, ch, s):
                for g in range(CH):
                    page = sp.value_load(pt[0:1, bass.ds(i * PAGES + ch * CH + g, 1)], min_val=0,
                                         max_val=A["cache_k"].shape[0] - 1)
                    sp.dma_start(dst[:, g * D:(g + 1) * D], rows[bass.ds(page * PAGE, PAGE), :]).then_inc(s, 16)

            def load_bias(i, half):
                for a in range(4):
                    src = RPD[4 * a:4 * a + 4, :, 8 * half + PAGES * i:8 * half + PAGES * i + 8, :] if isinstance(i, int) else \
                        RPD[4 * a:4 * a + 4, :, bass.ds(PAGES * i + 8 * half, 8), :]
                    sp.dma_start(BIAS[32 * a:32 * a + 16, D * half:D * half + D], src.rearrange("h q g r -> (h q) (g r)"))\
                        .then_inc(sem(f"bias_in{half}"), 16)

            sp.wait_ge(sem("zeros"), 3)
            for half in range(2):
                load_bias(0, half)
            sp.wait_ge(sem("h_sum"), NT)
            sp.wait_ge(sem("small_in"), 16 * SMALL)
            load_chunk(KB[:, 0, :], k_rows, 0, 0, sem("k_in0"))
            sp.wait_ge(sem("q_mm"), NT - 1)
            sp.wait_ge(sem("merged"), 3)
            load_chunk(KB[:, 1, :], k_rows, 0, 1, sem("k_in1"))

            def attention_loads(i, last):
                if not (isinstance(i, int) and i == 0):
                    sp.wait_ge(sem("s_ready"), 4 * i)
                    settled(sp)
                    load_bias(i, 1)
                for ch in range(NCH):
                    sp.wait_ge(sem("kt_tr"), 32 * i + 8 * (ch + 1))
                    settled(sp)
                    if ch < 2:
                        load_chunk(KB[:, ch, :], k_rows, i, ch + 2, sem(f"k_in{ch}"))
                    elif not last:
                        load_chunk(KB[:, ch - 2, :], k_rows, i + 1, ch - 2, sem(f"k_in{ch - 2}"))
                    else:
                        h = ch - 2
                        sp.dma_start(KB[:, h, :].rearrange("p (k n) -> p k n", k=HP), wo[:, :, 512 * h:512 * h + 512])\
                            .then_inc(sem("wo_in"), 16)
                    after(sp, sem("pv_done"), NCH * (i - 1) + ch + 1)
                    settled(sp)
                    load_chunk(VSL[ch], v_rows, i, ch, sem(f"v_in{ch}"))
                    if ch == 1 and not last:
                        sp.wait_ge(sem("s_ready"), 4 * i + 2)
                        settled(sp)
                        load_bias(i + 1, 0)

            sp.wait_ge(sem("proj_done"), 1)
            attention_loads(0, False)
            with sp.Fori(1, NB - 1) as i:
                attention_loads(i, False)
            attention_loads(NB - 1, True)
            first, second, rest = moe_weights(1)
            sp.wait_ge(sem("pv_done"), NCH * NB)
            second()
            sp.wait_ge(sem("ots_ready"), 2 * NB)
            sp.wait_ge(sem("pu_ot"), 10 * NB)
            first(0)
            sp.wait_ge(sem("wo_done"), NT)
            first(1)
            moe_rest(1)
            rest()
            moe_general(1)
            for t in range(NT):
                sp.wait_ge(sem("h_sum"), NT + t + 1)
                if t == 0:
                    put_out(sp, O["y_prompt"][0, 0:P - META, :], H[META:P, 0, :])
                elif t < 4:
                    put_out(sp, O["y_prompt"][0, t * P - META:(t + 1) * P - META, :], H[:, t, :])
                else:
                    put_out(sp, O["y_prompt"][0, 4 * P - META:SEQ, :], H[0:LASTP, 4, :])
                    put_out(sp, O["y_sample"].rearrange("b s d -> (b s) d"), H[S0:64, 4, :])

        @block.gpsimd
        def _(pool):
            pool.memset(H[0:64, 4, :], 0.0).then_inc(sem("zeros"), 1)
            pool.memset(zi[:, :], 0).then_inc(sem("zeros"), 1)
            pool.dma_start(ptc[:, :], A["page_table"].rearrange("b (g a) -> (b g) a", a=1)).then_inc(sem("ptc_in"), 16)
            pool.dma_start(ids[:, :], A["ids"]).then_inc(sem("ptc_in"), 16)
            pool.wait_ge(sem("ptc_in"), 32)
            pool.indirect_dma_start(out=W[:, 5, 0:2 * D], out_offset=None,
                                    in_=A["cache_logf"].rearrange("n r h -> n (r h)"),
                                    in_offset=bass.IndirectOffsetOnAxis(ap=ptc[:, 0:1], axis=0)).then_inc(sem("ptc_in"), 16)
            pool.wait_ge(sem("zeros"), 2)
            for l in range(2):
                pool.dma_start(LIST[l].rearrange("(p n) o -> p (n o)", p=P), zi[:, :]).then_inc(sem("list_zero"), 16)

            def moe(l):
                pool.wait_ge(sem("list_zero"), 32)
                pool.wait_ge(sem("slots_ready"), 1 + l * 1)
                for ch in range(2):
                    for t in range(NT):
                        r = ROWS[t]
                        pool.indirect_dma_start(out=LIST[l], out_offset=bass.IndirectOffsetOnAxis(ap=SSi[0:r, ch, t:t + 1], axis=0),
                                                in_=ids[0:r, t:t + 1], in_offset=None).then_inc(sem("scattered"), 16)
                for j in range(2):
                    pool.wait_ge(sem(f"xs_out_{j}"), (48 - 16 * j) * (l + 1))
                pool.wait_ge(sem("idx_in"), 16 + l * 16)
                pool.wait_ge(sem("router_done"), NT + l * NT)

                def gather(e, j):
                    after(pool, sem("xt_tr"), e - 1 + l * NE)
                    settled(pool)
                    pool.tensor_copy(idc[:, j:j + 1], IDX[:, e:e + 1] if isinstance(e, int) else IDX[:, bass.ds(e, 1)])\
                        .then_inc(sem("idc_ready"), 1)
                    pool.wait_ge(sem("idc_ready"), e + 1 + l * NE)
                    settled(pool)
                    pool.indirect_dma_start(out=XG[j], out_offset=None, in_=XS,
                                            in_offset=bass.IndirectOffsetOnAxis(ap=idc[:, j:j + 1], axis=0))\
                        .then_inc(sem(f"xg_in_{j}"), 16)

                gather(0, 0)
                gather(1, 1)
                with pool.Fori(2, NE - 1, 2) as e:
                    for j in range(2):
                        gather(e + j, j)
                pool.wait_ge(sem("np_ready"), 1 + l * 1)
                npass = pool.value_load(npi[0:1, 0:1], min_val=1, max_val=RANKS // P)
                with pool.If(npass > 1):
                    with pool.Fori(1, npass) as p:
                        with pool.Fori(0, NE) as e:
                            pool.wait_ge(sem(f"g_in{l}"), 64 * (p * NE + e - NE + 1))
                            settled(pool)
                            pool.indirect_dma_start(out=XG[0], out_offset=None, in_=XS,
                                                    in_offset=bass.IndirectOffsetOnAxis(ap=idg[:, 0:1], axis=0))\
                                .then_inc(sem(f"g_xg{l}"), 16)
                            pool.wait_ge(sem(f"g_y_out{l}"), 16 * (p * NE + e - NE + 1))
                            settled(pool)
                        for t in range(NT):
                            r = ROWS[t]
                            pool.wait_ge(sem(f"g_sum{l}"), 6 * p + t - 5)
                            settled(pool)
                            for ch in range(2):
                                pool.indirect_dma_start(out=K8[0:r, ch, :], out_offset=None, in_=YG[l],
                                                        in_offset=bass.IndirectOffsetOnAxis(ap=SGi[0:r, ch, t:t + 1], axis=0))\
                                    .then_inc(sem(f"g_yg{l}"), 16)
                        pool.wait_ge(sem(f"g_sum{l}"), 6 * p)
                        settled(pool)
                    pool.nop()
                for j in range(2):
                    pool.wait_ge(sem(f"y_out_{j}"), 16 * NE // 2 + l * (8 * NE))
                if l == 0:
                    pool.wait_ge(sem("state_out"), 16 * (NB + 1))
                for t in range(NT):
                    r = ROWS[t]
                    for ch in range(2):
                        buf = (2 * t + ch) % 8
                        if t == 4:
                            pool.wait_ge(sem("h_sum"), 1 + l * NT)
                        pool.indirect_dma_start(out=K8[0:r, buf, :], out_offset=None, in_=YD[l],
                                                in_offset=bass.IndirectOffsetOnAxis(ap=SLi[0:r, ch, t:t + 1], axis=0))\
                            .then_inc(sem(f"yg_in_{t}"), 16)

            pool.wait_ge(sem("rq_out"), 16 * NS)
            pool.memset(BIAS[:, :], 0.0).then_inc(sem("zeros"), 1)
            moe(0)

            def stage(i, hh):
                if not (isinstance(i, int) and i == 0):
                    pool.wait_ge(sem("pu_v"), 10 * i - 5 + 5 * hh)
                    settled(pool)
                for dst, src in ((QST, QTD), (KST, KTD)):
                    s = src[2 * i + hh] if isinstance(i, int) else src[bass.ds(2 * i + hh, 1)].rearrange("a d t -> (a d) t")
                    pool.dma_start(dst[hh][0:DH + 1, :], s).then_inc(sem(f"st_in{hh}"), 16)
                cols = slice(P * i + DH * hh, P * i + DH * hh + DH) if isinstance(i, int) else bass.ds(P * i + DH * hh, DH)
                own = slice(DH * hh, DH * hh + DH)
                pool.dma_start(VST[:, 0:4, own], vp_out[0:4 * P, cols].rearrange("(t p) n -> p t n", p=P)).then_inc(sem(f"st_in{hh}"), 16)
                pool.dma_start(VST[0:LASTP, 4, own], vp_out[4 * P:TP, cols]).then_inc(sem(f"st_in{hh}"), 16)

            pool.wait_ge(sem("proj_stored"), 1)
            for hh in range(2):
                stage(0, hh)
            with pool.Fori(1, HP) as i:
                for hh in range(2):
                    stage(i, hh)
            moe(1)
            pool.wait_ge(sem("kout"), 16 * (NT + 1))
            pool.wait_ge(sem("vout"), 16 * NT)
            pool.wait_ge(sem("state_out"), 16 * (NB + 1))
            pool.wait_ge(sem("out_done"), 16 * OUTS)
            pool.nop()

        @block.tensor
        def _(pe):
            pe.wait_ge(sem("consts_in"), 16)
            pe.wait_ge(sem("ptc_in"), 48)
            lo = CONST["ident"][0]
            both = C[:, lo:lo + 2 * P]
            for h in range(NH):
                if h >= 4 and h % 2 == 0:
                    pe.wait_ge(sem("tt_ready"), h // 2 - 1)
                mm = pe.matmul(PS[:, 6 + h // 2 % 2, 256 * (h % 2):256 * (h % 2) + 256], LP[:, :, h], both, start=True, stop=True)
                if h % 2:
                    mm.then_inc(sem("tt_tr"), 1)
            for n in range(4):
                if n == 0:
                    pe.wait_ge(sem("tt_ready"), NH // 2)
                if n >= 2:
                    pe.wait_ge(sem("r_done"), n - 1)
                for h in range(4 * n, 4 * n + 4):
                    out = PS[:, 4 + n % 2, (h % 4) * P:(h % 4) * P + P]
                    pe.matmul(out, TT[:, h, 0:P], c("after"), start=True, stop=False)
                    mm = pe.matmul(out, TT[:, h, P:2 * P], c("ones"), start=False, stop=True)
                mm.then_inc(sem("r_mm"), 1)

            def bandv(name, g):
                lo, hi, n = BAND[name]
                return bands[:, lo + g * n:lo + (g + 1) * n]

            pe.wait_ge(sem("pool_in"), 16 * 5)
            pe.wait_ge(sem("ws_ready"), 1)
            for t in range(NT):
                r = ROWS[t]
                pe.wait_ge(sem("u_ready"), t + 1)
                if t >= 1:
                    pe.wait_ge(sem("dt_ready"), 2 * t)
                for k in range(8):
                    g = k // 2
                    cs = slice(k * P, k * P + P)
                    out = PS[:, k // 4, (k % 4) * P:(k % 4) * P + r]
                    if t == 4:
                        pe.matmul(out, U[3][:, cs], bandv("prev4", g), start=True, stop=False)
                        pe.matmul(out, ST[0:NB * STATE, cs], bandv("state", g)[0:NB * STATE], start=False, stop=False)
                        mm = pe.matmul(out, U[4][0:64, cs], bandv("cur4", g)[0:64], start=False, stop=True)
                    else:
                        if t:
                            pe.matmul(out, U[t - 1][:, cs], bandv("prev", g), start=True, stop=False)
                        mm = pe.matmul(out, U[t][:, cs], bandv("cur" if t else "cur0", g), start=(t == 0), stop=True)
                mm.then_inc(sem("dt_mm"), 1)
                pe.wait_ge(sem("dt_ready"), 2 * t + 2)
                if t >= 2:
                    pe.wait_ge(sem("h_pool"), t - 1)
                if t == 1:
                    pe.wait_ge(sem("r_done"), 4)
                for g in range(NG):
                    for cc in range(2):
                        mm = pe.matmul(PS[0:r, 2 + 2 * (t % 2) + g // 2, 256 * (g % 2):256 * (g % 2) + 256],
                                       DT[t % 2][:, 2 * g + cc, 0:r], pw[:, g, cc, :], start=(cc == 0), stop=(cc == 1))
                mm.then_inc(sem("pool_mm"), 1)

            def transposes(src, bank, r, step):
                for k in range(KC):
                    s = src[0:r, :].rearrange("p (n k) -> p k n", k=KC)[:, k, :] if step > 1 else src[0:r, k * P:(k + 1) * P]
                    mm = pe.transpose(PS[:, bank + k // 4, (k % 4) * P:(k % 4) * P + r], s, ident[0:r, 0:r])
                return mm

            def router(l):
                for t in range(NT):
                    r = ROWS[t]
                    pe.wait_ge(sem("un_ready"), t + 1 + l * NT)
                    if t >= 2:
                        pe.wait_ge(sem("xu_ready"), t - 1 + l * NT)
                    transposes(YS[t % 2], 2 * (t % 2), r, KC).then_inc(sem("un_tr"), 1)
                    pe.wait_ge(sem("xu_ready"), t + 1 + l * NT)
                    if t == 0 and l == 0:
                        pe.wait_ge(sem("small_in"), 16 * SMALL)
                    for k in range(KC):
                        mm = pe.matmul(PS[0:r, 6, 20 * t:20 * t + 20], XU[t % 2][:, k, 0:r], wr[:, l, k, :],
                                       start=(k == 0), stop=(k == KC - 1))
                    mm.then_inc(sem("router_done"), 1)
                pe.wait_ge(sem("picks_ready"), 1 + l * 1)
                Av = rt["A"].rearrange("p (t e) -> p t e", t=NT)
                for t in range(NT):
                    r = ROWS[t]
                    out = PS[0:r, 7, NE * t:NE * t + NE]
                    for t2 in range(t):
                        pe.matmul(out, c("ones")[:, 0:r], Av[:, t2, :], start=(t2 == 0), stop=False)
                    pe.matmul(out, c("before")[0:r, 0:r], Av[0:r, t, :], start=(t == 0), stop=True)
                for t in range(NT):
                    r = ROWS[t]
                    mm = pe.matmul(PS[:, 7, NE * NT:NE * NT + NE], c("ones")[0:r, :], Av[0:r, t, :], start=(t == 0), stop=(t == NT - 1))
                mm.then_inc(sem("ranks"), 1)

            def moe(l):
                def x_tr(e, j):
                    k = 8 * e + 16 - 8 * j
                    pe.wait_ge(sem(f"xg_in_{j}"), k + l * (8 * NE))
                    after(pe, sem("xt_ready"), e + l * NE)
                    transposes(XG[j], 0, P, KC).then_inc(sem("xt_tr"), 1)

                def product(bank, slot, count, name):
                    pe.wait_ge(sem(f"w_in_{slot}"), count + l * (8 * NE))
                    w = W[:, slot, :].rearrange("p (k n) -> p k n", k=KC)
                    for k in range(KC):
                        mm = pe.matmul(PS[:, bank, :], XT[:, k, :], w[:, k, :], start=(k == 0), stop=(k == KC - 1))
                    mm.then_inc(sem(f"{name}_done"), 1)

                def h_tr(e):
                    pe.wait_ge(sem("h_ready"), e + 1 + l * NE)
                    after(pe, sem("ht_ready"), e + l * NE)
                    for f in range(FC):
                        mm = pe.transpose(PS[:, 4, f * P:(f + 1) * P], HH.rearrange("p (n f) -> p f n", f=FC)[:, f, :], ident)
                    mm.then_inc(sem("ht_tr"), 1)

                def down(e, j):
                    pe.wait_ge(sem("ht_ready"), e + 1 + l * NE)
                    pe.wait_ge(sem(f"w_in_{3 * j + 2}"), 8 * e + 16 - 8 * j + l * (8 * NE))
                    after(pe, sem("y_ready"), e + l * NE)
                    w = W[:, 3 * j + 2, :].rearrange("p (f n) -> p f n", f=FC)
                    for n in range(2):
                        for f in range(FC):
                            mm = pe.matmul(PS[:, 5 + n, :], HT[:, f, :], w[:, f, n * 512:(n + 1) * 512],
                                           start=(f == 0), stop=(f == FC - 1))
                    mm.then_inc(sem("down_done"), 1)

                def expert(e, j, last=False):
                    count = 8 * e + 16 - 8 * j
                    first = isinstance(e, int) and e == 0
                    pe.wait_ge(sem("xt_ready"), e + 1 + l * NE)
                    after(pe, sem("silu_done"), e + l * NE)
                    product(2, 3 * j, count, "gate")
                    if not first:
                        h_tr(e - 1)
                    product(3, 3 * j + 1, count, "up")
                    if not last:
                        x_tr(e + 1, 1 - j)
                    if not first:
                        down(e - 1, 1 - j)

                x_tr(0, 0)
                expert(0, 0)
                expert(1, 1)
                with pe.Fori(2, NE - 3, 2) as e:
                    expert(e, 0)
                    expert(e + 1, 1)
                expert(NE - 2, 0)
                expert(NE - 1, 1, last=True)
                h_tr(NE - 1)
                down(NE - 1, 1)

                pe.wait_ge(sem("np_ready"), 1 + l * 1)
                npass = pe.value_load(npi[0:1, 0:1], min_val=1, max_val=RANKS // P)
                with pe.If(npass > 1):
                    with pe.Fori(1, npass) as p:
                        with pe.Fori(0, NE) as e:
                            n = p * NE + e - NE
                            pe.wait_ge(sem(f"g_in{l}"), 64 * (n + 1))
                            pe.wait_ge(sem(f"g_xg{l}"), 16 * (n + 1))
                            transposes(XG[0], 0, P, KC).then_inc(sem(f"g_step{l}"), 1)
                            pe.wait_ge(sem(f"g_step{l}"), 9 * n + 2)
                            for which in range(2):
                                w = W[:, which, :].rearrange("p (k n) -> p k n", k=KC)
                                for k in range(KC):
                                    mm = pe.matmul(PS[:, 2 + which, :], XT[:, k, :], w[:, k, :], start=(k == 0), stop=(k == KC - 1))
                            mm.then_inc(sem(f"g_step{l}"), 1)
                            pe.wait_ge(sem(f"g_step{l}"), 9 * n + 5)
                            for f in range(FC):
                                mm = pe.transpose(PS[:, 4, f * P:(f + 1) * P], HH.rearrange("p (n f) -> p f n", f=FC)[:, f, :], ident)
                            mm.then_inc(sem(f"g_step{l}"), 1)
                            pe.wait_ge(sem(f"g_step{l}"), 9 * n + 7)
                            w = W[:, 2, :].rearrange("p (f n) -> p f n", f=FC)
                            for nn in range(2):
                                for f in range(FC):
                                    mm = pe.matmul(PS[:, 5 + nn, :], HT[:, f, :], w[:, f, nn * 512:(nn + 1) * 512],
                                                   start=(f == 0), stop=(f == FC - 1))
                            mm.then_inc(sem(f"g_step{l}"), 1)
                pe.nop()

            router(0)
            moe(0)

            wv = [W[:, s, :].rearrange("p (k n) -> p k n", k=KC) for s in range(6)]
            def project(t, x, banks, slots, done=None):
                r = ROWS[t]
                for b, s in zip(banks, slots):
                    for k in range(KC) if t < 4 else (0, 4, 1, 5, 2, 6, 3, 7):
                        if t < 4:
                            mm = pe.matmul(PS[0:r, b, :], x[:, k, 0:r], wv[s][:, k, :], start=(k == 0), stop=(k == KC - 1))
                        else:
                            up = 64 * (k // 4)
                            mm = pe.matmul(PS[up:up + 64, b, :], x[:, k, 0:r], wv[s][:, k, :], start=(k % 4 == 0),
                                           stop=(k % 4 == 3), tile_position=(0, up), skip_group_check=True)
                if done:
                    mm.then_inc(sem(done), 1)

            for t in range(NT):
                r = ROWS[t]
                x, y = UK[t % 2], UQ[t % 2]
                if t == 0:
                    pe.wait_ge(sem("pun_ready"), 1)
                    transposes(UN, 0, r, KC).then_inc(sem("pun_tr"), 1)
                    pe.wait_ge(sem("proj_in_k"), 32)
                pe.wait_ge(sem("ux_ready"), 2 * t + 1)
                after(pe, sem("kn_ready"), 2 * t)
                project(t, x, (2, 3), (0, 1), "k_mm")
                after(pe, sem("qn_ready"), t)
                for k in range(KC):
                    mm = pe.matmul(PS[0:r, 6, 0:NH], x[:, k, 0:r], wf[:, k, :], start=(k == 0), stop=(k == KC - 1))
                mm.then_inc(sem("f_mm"), 1)
                pe.wait_ge(sem("ux_ready"), 2 * t + 2)
                if t:
                    transposes(QN, 0, ROWS[t - 1], 1).then_inc(sem("qn_tr"), 1)
                if t == 0:
                    pe.wait_ge(sem("proj_in_v"), 32)
                after(pe, sem("vn_ready"), t)
                project(t, x, (4, 5), (2, 3), "v_mm")
                pe.wait_ge(sem("kn_ready"), 2 * t + 2)
                after(pe, sem("qts_ready"), t)
                transposes(KN, 0, r, 1).then_inc(sem("kn_tr"), 1)
                if t == 0:
                    pe.wait_ge(sem("proj_in_q"), 32)
                pe.wait_ge(sem("f_ready"), t + 1)
                project(t, y, (6,), (4,))
                if t + 1 < NT:
                    pe.wait_ge(sem("pun_ready"), t + 2)
                    pe.wait_ge(sem("kts_ready"), t + 1)
                    transposes(UN, 0, ROWS[t + 1], KC).then_inc(sem("pun_tr"), 1)
                project(t, y, (7,), (5,), "q_mm")
            pe.wait_ge(sem("qn_ready"), NT)
            pe.wait_ge(sem("kts_ready"), NT)
            transposes(QN, 0, ROWS[NT - 1], 1).then_inc(sem("qn_tr"), 1)
            pe.wait_ge(sem("lf_step"), 5)
            pe.wait_ge(sem("extra_ready"), 1)
            for t in range(NT):
                n = P if t < 4 else LASTP
                out = PS[0:NH, 2 + t // 4, (t % 4) * P:(t % 4) * P + n]
                for t2 in range(t):
                    pe.matmul(out, LF[:, t2, :], c("ones")[:, 0:n], start=(t2 == 0), stop=False)
                mm = pe.matmul(out, LF[0:n, t, :], c("upto")[0:n, 0:n], start=(t == 0), stop=True)
            mm.then_inc(sem("ct_mm"), 1)
            pe.matmul(PS[:, 4, 0:64], LR[0:64, :], c("negnew", 64), start=True, stop=True).then_inc(sem("ct_mm"), 1)
            pe.wait_ge(sem("proj_done"), 1)

            def attention(i, front=True, back=True):
                def s_step(u):
                    hh, t = u // 5, u % 5
                    r = P if t < 4 else LASTP
                    nk = P * (t + 1) if t < 4 else 4 * P
                    if t == 0:
                        pe.wait_ge(sem(f"st_in{hh}"), 64 * (i + 1))
                    after(pe, sem("pu_exp"), 10 * i + u)
                    pe.matmul(PS[0:r, 6, 0:nk], QST[hh][0:DH + 1, t * P:t * P + r], KST[hh][0:DH + 1, 0:nk],
                              start=True, stop=True)
                    if t < 4:
                        mm = pe.matmul(PS[:, 6, t * P:t * P + P], ident, c("causal"), start=False, stop=True, skip_group_check=True)
                    else:
                        if back:
                            pe.wait_ge(sem("ptt_ready"), 5 * i - 5 + (4 if u == 4 else 5))
                        pe.matmul(PS[0:r, 4, 0:r], QST[hh][0:DH + 1, t * P:t * P + r], KST[hh][0:DH + 1, nk:TP],
                                  start=True, stop=False)
                        mm = pe.matmul(PS[0:r, 4, 0:r], ident[0:r, 0:r], c("causal")[0:r, 0:r], start=False, stop=True)
                    mm.then_inc(sem("pu_s"), 1)

                def t_step(u):
                    t = u % 5
                    pe.wait_ge(sem("pu_norm"), 10 * i + u + 1)
                    after(pe, sem("pu_pts"), 10 * i + u)
                    if t < 4:
                        for j in range(t + 1):
                            mm = pe.transpose(PS[:, 7, j * P:(j + 1) * P], PR[:, j * P:(j + 1) * P], ident)
                    else:
                        settled(pe)
                        r = LASTP
                        for j in range(4):
                            pe.transpose(PS[:, 7, j * r:(j + 1) * r], PR[0:r, j * P:(j + 1) * P], ident[0:r, 0:r])
                        mm = pe.transpose(PS[0:r, 7, 4 * r:5 * r], PR[0:r, 4 * P:TP], ident[0:r, 0:r])
                    mm.then_inc(sem("pu_t"), 1)

                def v_step(u):
                    hh, t = u // 5, u % 5
                    pe.wait_ge(sem("pu_pts"), 10 * i + u + 1)
                    after(pe, sem("pu_ot"), 10 * i + u)
                    r = P if t < 4 else LASTP
                    vc = slice(DH * hh, DH * hh + DH)
                    out = PS[DH * hh:DH * hh + DH, 3, 0:r]
                    for j in range(t + 1):
                        kr = P if j < 4 else LASTP
                        mm = pe.matmul(out, VST[0:kr, j, vc], PTS[0:kr, j * r:(j + 1) * r], start=(j == 0), stop=(j == t),
                                       tile_position=(0, DH * hh))
                    mm.then_inc(sem("pu_v"), 1)

                def k_tick(n):
                    ch, half, j, m = n // 8, n // 4 % 2, n // 2 % 2, n % 2
                    if n % 8 == 0:
                        pe.wait_ge(sem(f"k_in{ch % 2}"), 64 * (2 * i + ch // 2 + 1))
                    after(pe, sem("kt_even" if n % 2 == 0 else "kt_odd"), 16 * i + n // 2)
                    ks = paged(KB[:, ch % 2, :])
                    for x in range(2):
                        hp = 4 * m + 2 * x + j
                        for g in range(2):
                            mm = pe.transpose(PS[:, n % 2, (2 * x + g) * P:(2 * x + g + 1) * P],
                                              ks[:, 2 * half + g, hp * P:(hp + 1) * P], ident)
                    mm.then_inc(sem("kt_tr"), 1)

                def qk(x):
                    ch, half, j = x // 4, x // 2 % 2, x % 2
                    pe.wait_ge(sem("kt_even"), 16 * i + x + 1)
                    pe.wait_ge(sem("kt_odd"), 16 * i + x + 1)
                    if x == 0:
                        pe.wait_ge(sem("qb_ready"), i + 1)
                    if x % 4 == 0:
                        if ch == 2:
                            pe.wait_ge(sem("sn_ready"), i + 1)
                        else:
                            after(pe, sem("s_ready"), 4 * i + ch)
                    for a in range(4):
                        mm = pe.matmul(PS[32 * a:32 * a + 32, 2, 256 * half:256 * half + 256], QBLK[:, 2 * a + j, :],
                                       KTR[:, (2 * x + a // 2) % 4, 256 * (a % 2):256 * (a % 2) + 256],
                                       start=(j == 0), stop=(j == 1), tile_position=(0, 32 * a), skip_group_check=True)
                    mm.then_inc(sem("qk_done"), 1)

                def new_keys():
                    pe.wait_ge(sem("s_ready"), 4 * i + 2)
                    for j in range(2):
                        for a in range(4):
                            mm = pe.matmul(PS[32 * a:32 * a + 32, 2, 0:64], QBLK[:, 2 * a + j, :], KT4[:, 2 * a + j, :],
                                           start=(j == 0), stop=(j == 1), tile_position=(0, 32 * a), skip_group_check=True)
                    mm.then_inc(sem("sn_mm"), 1)

                def p_transposes(part):
                    if part == 0:
                        pe.wait_ge(sem("sp_exp"), i)
                    after(pe, sem("ptt_ready"), 5 * i - 5 + part)
                    if front and part == NCH:
                        pe.wait_ge(sem("pu_exp"), 10 * i + 5)
                    elif front and part == 0:
                        pe.wait_ge(sem("pu_exp"), 10 * i)
                    if part == NCH:
                        settled(pe)
                        mm = pe.transpose(PS[0:64, 4, 0:P], SROW[:, PAGES * PAGE:PAGES * PAGE + 64], ident)
                    else:
                        for g in range(CH):
                            at = (CH * part + g) * PAGE
                            mm = pe.transpose(PS[:, 4, g * P:(g + 1) * P], SROW[:, at:at + PAGE], ident)
                    mm.then_inc(sem("ptt_tr"), 1)

                def values(g):
                    ch = g // CH
                    if g == 0:
                        after(pe, sem("ots_ready"), 2 * i - 2)
                    if g % CH == 0:
                        pe.wait_ge(sem("ptt_ready"), 5 * i - 5 + ch + 1)
                        if ch < NCH:
                            pe.wait_ge(sem(f"v_in{ch}"), 64 * i)
                        else:
                            settled(pe)
                    nn = P if g < PAGES else 64
                    for q in range(4):
                        v = paged(VSL[ch])[:, g % CH, 256 * q:256 * q + 256] if ch < NCH else V4[0:64, 256 * q:256 * q + 256]
                        mm = pe.matmul(PS[32 * q:32 * q + 32, 5, 0:256], PTT[0:nn, g, 32 * q:32 * q + 32], v,
                                       start=(g == 0), stop=(g == PAGES), tile_position=(0, 32 * q), skip_group_check=True)
                    if g == PAGES:
                        mm.then_inc(sem("o_mm"), 1)
                    elif g % CH == CH - 1:
                        mm.then_inc(sem("pv_done"), 1)

                for n in range(TICKS):
                    if front:
                        if n < KTICKS:
                            k_tick(n)
                        if n in QK_TICK:
                            qk(QK_TICK.index(n))
                        if n == NEW_TICK:
                            new_keys()
                        if n in V_TICK:
                            v_step(V_TICK.index(n))
                        if n in T_TICK:
                            t_step(T_TICK.index(n))
                        if n in S_TICK:
                            s_step(S_TICK.index(n))
                    if back:
                        if n in P_TICK:
                            p_transposes(P_TICK.index(n))
                        if n in O_TICK:
                            values(O_TICK.index(n))
                        if n == OT_TICK:
                            pe.wait_ge(sem("ob_ready"), i)
                            for x in range(2):
                                mm = pe.transpose(PS[:, 5, 256 + x * P:256 + (x + 1) * P], OB[:, x * P:(x + 1) * P], ident)
                            mm.then_inc(sem("ob_tr"), 1)

            attention(0, back=False)
            with pe.Fori(1, NB) as i:
                attention(i)
            attention(NB, front=False)

            pe.wait_ge(sem("wo_in"), 32)
            pe.wait_ge(sem("pu_ot"), 10 * NB)
            pe.wait_ge(sem("ots_ready"), 2 * NB)
            for t in range(NT):
                r = ROWS[t]
                if t >= 2:
                    pe.wait_ge(sem("h_attn"), t - 1)
                for n in range(2):
                    for k in range(HP):
                        mm = pe.matmul(PS[0:r, 2 * (t % 2) + n, :], OTS[:, k, t * P:t * P + r],
                                       KB[:, n, :].rearrange("p (k n) -> p k n", k=HP)[:, k, :], start=(k == 0), stop=(k == HP - 1))
                mm.then_inc(sem("wo_done"), 1)
            router(1)
            moe(1)

        @block.scalar
        def _(act):
            def roots(name):
                act.wait_ge(sem("ms"), NORMS.index(name) + 1)
                act.activation(sd[:, :], ms[:, :], ACT.Sqrt).then_inc(sem("sd"), 1)

            act.wait_ge(sem("ss_one"), 1)
            act.wait_ge(sem("rows_in"), 16 * 7)
            for t in range(NT):
                r = ROWS[t]
                act.activation(U[t][0:r, :], H[0:r, t, :], ACT.Square, accum_out=ss[0:r, t:t + 1]).then_inc(sem("sq"), 1)
            roots("pool")
            for n in range(4):
                act.wait_ge(sem("r_mm"), n + 1)
                act.activation(RQ[:, 4 * n:4 * n + 4, :], PS[:, 4 + n % 2, :].rearrange("p (h m) -> p h m", h=4), ACT.Copy)\
                    .then_inc(sem("r_done"), 1)
            act.wait_ge(sem("r_done"), 4)
            for q in range(NS):
                act.dma_start(RPD[:, q].rearrange("h g r -> g h r"), RQ).then_inc(sem("rq_out"), 16)
            for t in range(NT):
                r = ROWS[t]
                act.wait_ge(sem("dt_mm"), t + 1)
                if t >= 2:
                    act.wait_ge(sem("pool_mm"), t - 1)
                act.activation(DT[t % 2][:, 4:8, 0:r], PS[:, 1, :].rearrange("p (k n) -> p k n", k=4)[:, :, 0:r], ACT.Copy)\
                    .then_inc(sem("dt_ready"), 1)

            def router(l, h_sem):
                act.wait_ge(sem("pool_mm" if l == 0 else "wo_done"), NT)
                if l == 1:
                    act.wait_ge(sem("pv_done"), NCH * NB)
                for t in range(NT):
                    r = ROWS[t]
                    act.wait_ge(sem(h_sem), t + 1)
                    if t >= 2:
                        act.wait_ge(sem("sq"), NT * (1 + 2 * l) + t - 1)
                    act.activation(XG[t % 2][0:r, :], H[0:r, t, :], ACT.Square, accum_out=ss[0:r, t:t + 1]).then_inc(sem("sq"), 1)
                roots(f"r{l}")
                for t in range(NT):
                    r = ROWS[t]
                    act.wait_ge(sem("un_ready"), t + 1 + l * NT)
                    act.dma_start(XS[t * P:t * P + r, :], YS[t % 2][0:r, :]).then_inc(sem(f"xs_out_{t % 2}"), 16)
                act.wait_ge(sem("rt_in"), 1 + l * 2)
                act.activation(rt["eg"], rt["dl"], ACT.Exp).then_inc(sem("rt_exp"), 1)
                act.wait_ge(sem("rt_in"), 2 + l * 2)
                act.activation(rt["ed"], rt["d"], ACT.Exp).then_inc(sem("rt_exp"), 1)

            def moe(l):
                def silu(e):
                    act.wait_ge(sem("gate_done"), e + 1 + l * NE)
                    after(act, sem("h_ready"), e + l * NE)
                    act.activation(SG, PS[:, 2, :], ACT.Silu).then_inc(sem("silu_done"), 1)

                def ht(e):
                    act.wait_ge(sem("ht_tr"), e + 1 + l * NE)
                    after(act, sem("down_done"), e + l * NE)
                    act.activation(HT.rearrange("p f n -> p (f n)"), PS[:, 4, :], ACT.Copy).then_inc(sem("ht_ready"), 1)

                def y(e, j):
                    act.wait_ge(sem("down_done"), e + 1 + l * NE)
                    after(act, sem(f"y_out_{j}"), 8 * e - 8 * j + l * (8 * NE))
                    act.activation(YS[j], PS[:, 5:7, :].rearrange("p a n -> p (a n)"), ACT.Copy).then_inc(sem("y_ready"), 1)
                    act.wait_ge(sem("y_ready"), e + 1 + l * NE)
                    settled(act)
                    rows = YD[l].rearrange("(r e) n -> e r n", e=NE)
                    dst = rows[e] if isinstance(e, int) else rows[bass.ds(e, 1)].rearrange("e r n -> (e r) n")
                    act.dma_start(dst, YS[j]).then_inc(sem(f"y_out_{j}"), 16)

                for j in range(2):
                    act.wait_ge(sem(f"xs_out_{j}"), (48 - 16 * j) * (l + 1))
                silu(0)
                silu(1)
                ht(0)
                y(0, 0)
                with act.Fori(2, NE - 1, 2) as e:
                    silu(e)
                    ht(e - 1)
                    y(e - 1, 1)
                    silu(e + 1)
                    ht(e)
                    y(e, 0)
                ht(NE - 1)
                y(NE - 1, 1)
                act.wait_ge(sem("np_ready"), 1 + l * 1)
                npass = act.value_load(npi[0:1, 0:1], min_val=1, max_val=RANKS // P)
                with act.If(npass > 1):
                    act.wait_ge(sem("y_out_0"), 16 * NE // 2 + l * (8 * NE))
                    with act.Fori(1, npass) as p:
                        with act.Fori(0, NE) as e:
                            n = p * NE + e - NE
                            act.wait_ge(sem(f"g_step{l}"), 9 * n + 3)
                            act.activation(SG, PS[:, 2, :], ACT.Silu).then_inc(sem(f"g_step{l}"), 1)
                            act.wait_ge(sem(f"g_step{l}"), 9 * n + 6)
                            act.activation(HT.rearrange("p f n -> p (f n)"), PS[:, 4, :], ACT.Copy).then_inc(sem(f"g_step{l}"), 1)
                            act.wait_ge(sem(f"g_step{l}"), 9 * n + 8)
                            act.activation(YS[0], PS[:, 5:7, :].rearrange("p a n -> p (a n)"), ACT.Copy).then_inc(sem(f"g_step{l}"), 1)
                            act.wait_ge(sem(f"g_step{l}"), 9 * n + 9)
                            settled(act)
                            rows = YG[l].rearrange("(r e) n -> e r n", e=NE)
                            act.dma_start(rows[bass.ds(e, 1)].rearrange("e r n -> (e r) n"), YS[0])\
                                .then_inc(sem(f"g_y_out{l}"), 16)
                act.nop()

            router(0, "h_pool")
            moe(0)

            act.wait_ge(sem("y_out_0"), 16 * NE // 2)
            act.wait_ge(sem("y_out_1"), 16 * NE // 2)
            def row_root(t):
                r = ROWS[t]
                act.wait_ge(sem("h_sum"), t + 1)
                after(act, sem("sq"), 2 * NT + t)
                act.activation(SQ[0:r, :], H[0:r, t, :], ACT.Square, accum_out=ss[0:r, t:t + 1]).then_inc(sem("sq"), 1)
                act.wait_ge(sem("row_ms"), t + 1)
                act.activation(sd[:, t:t + 1], ms[:, t:t + 1], ACT.Sqrt).then_inc(sem("row_sd"), 1)

            def merge(b):
                act.activation(UPPER[0:64, :], PS[64:128, b:b + 2, :].rearrange("p a n -> p (a n)"), ACT.Copy)\
                    .then_inc(sem("upper_ready"), 1)
                act.wait_ge(sem("merged"), b // 2)

            def queries_out(t):
                r = ROWS[t]
                act.wait_ge(sem("qn_tr"), t + 1)
                act.wait_ge(sem("ktd_out"), 32 * (t + 1))
                dst = TS if t < 4 else QT4
                act.activation(dst[:, :, 0:r], PS[:, 0:2, :].rearrange("p a (k n) -> p (a k) n", n=P)[:, :, 0:r], ACT.Copy,
                               scale=qg[:, 0:1]).then_inc(sem("qts_ready"), 1)
                act.wait_ge(sem("qts_ready"), t + 1)
                n = r if t < 4 else LASTP
                for hh in range(2):
                    act.dma_start(QTD[hh:NH:2, 0:DH, t * P:t * P + n].rearrange("h d t -> d h t"), dst[DH * hh:DH * hh + DH, :, 0:n])\
                        .then_inc(sem("qtd_out"), 16)

            for j in range(2):
                act.wait_ge(sem(f"y_out_{j}"), 16 * NE // 2)
            row_root(0)
            row_root(1)
            for t in range(NT):
                r = ROWS[t]
                two = lambda b: PS[0:r, b:b + 2, :].rearrange("p a n -> p (a n)")
                act.wait_ge(sem("k_mm"), t + 1)
                if t:
                    act.wait_ge(sem("ssq_ready"), t)
                if t == 4:
                    merge(2)
                act.activation(SQ[0:r, :], two(2), ACT.Square).then_inc(sem("head_sq"), 1)
                act.wait_ge(sem("head_ms"), 2 * t + 1)
                act.activation(hsd[:, 0, :], hms[:, 0, :], ACT.Sqrt).then_inc(sem("head_sd"), 1)
                act.wait_ge(sem("kn_ready"), 2 * t + 2)
                act.dma_start(kp_out[t * P:t * P + min(P, TP - t * P), :], KN[0:min(r, TP - t * P), :]).then_inc(sem("kout"), 16)
                if t == 4:
                    act.dma_start(ks_out, KN[S0:64, :]).then_inc(sem("kout"), 16)
                if t:
                    queries_out(t - 1)
                act.wait_ge(sem("v_mm"), t + 1)
                dst = VN if t < 4 else V4
                if t:
                    act.wait_ge(sem("vout"), 16 * t)
                if t == 4:
                    merge(4)
                act.activation(dst[0:r, :], two(4), ACT.Copy).then_inc(sem("vn_ready"), 1)
                act.wait_ge(sem("vn_ready"), t + 1)
                act.dma_start(vp_out[t * P:t * P + min(P, TP - t * P), :], dst[0:min(r, TP - t * P), :]).then_inc(sem("vout"), 16)
                if t == 4:
                    put_out(act, vs_out, V4[S0:64, :])
                act.wait_ge(sem("kn_tr"), t + 1)
                dst = TS if t < 4 else KT4
                if t:
                    act.wait_ge(sem("qtd_out"), 32 * t)
                act.activation(dst[:, :, 0:r], PS[:, 0:2, :].rearrange("p a (k n) -> p (a k) n", n=P)[:, :, 0:r], ACT.Copy)\
                    .then_inc(sem("kts_ready"), 1)
                act.wait_ge(sem("kts_ready"), t + 1)
                n = r if t < 4 else LASTP
                for hh in range(2):
                    act.dma_start(KTD[hh:NH:2, 0:DH, t * P:t * P + n].rearrange("h d t -> d h t"), dst[DH * hh:DH * hh + DH, :, 0:n])\
                        .then_inc(sem("ktd_out"), 16)
                if t + 2 < NT:
                    row_root(t + 2)
                act.wait_ge(sem("q_mm"), t + 1)
                if t == 4:
                    merge(6)
                act.activation(SQ[0:r, :], two(6), ACT.Square).then_inc(sem("head_sq"), 1)
                act.wait_ge(sem("head_ms"), 2 * t + 2)
                act.activation(hsd[:, 1, :], hms[:, 1, :], ACT.Sqrt).then_inc(sem("head_sd"), 1)
            queries_out(NT - 1)
            act.wait_ge(sem("lf_step"), 1)
            act.activation(lfe, lfa, ACT.Exp, scale=-1.0).then_inc(sem("lf_step"), 1)
            act.wait_ge(sem("lf_step"), 3)
            act.activation(lfa, lfe, ACT.Ln).then_inc(sem("lf_step"), 1)
            act.wait_ge(sem("lf_step"), 5)
            for t in range(NT):
                n = P if t < 4 else LASTP
                put_out(act, fp_out[t * P:t * P + n, :], LF[0:n, t, :])
            put_out(act, fs_out, LF[S0:64, 4, :])
            act.wait_ge(sem("ct_mm"), 1)
            act.activation(CT[0:NH, 0:4 * P], PS[0:NH, 2, :], ACT.Copy, scale=-1.0).then_inc(sem("ct_ready"), 1)
            act.activation(CT[0:NH, 4 * P:TP], PS[0:NH, 3, 0:LASTP], ACT.Copy, scale=-1.0).then_inc(sem("ct_ready"), 1)
            act.wait_ge(sem("ct_ready"), 2)
            act.wait_ge(sem("extra_ready"), 2)
            act.dma_start(KTD[:, DH, :], CT[0:NH, :]).then_inc(sem("ktd_out"), 16)
            act.dma_start(QTD[:, DH, :], PR[0:NH, :]).then_inc(sem("qtd_out"), 16)
            act.wait_ge(sem("ktd_out"), 32 * NT + 16)
            act.wait_ge(sem("qtd_out"), 32 * NT + 16)
            act.wait_ge(sem("vout"), 16 * NT)
            act.wait_ge(sem("proj_done"), 1)
            act.sem_inc(sem("proj_stored"), 1)

            def attention(i, front=True, back=True):
                def evac(n):
                    act.wait_ge(sem("kt_tr"), 32 * i + n + 1)
                    after(act, sem("qk_done"), 16 * i + n // 2 - 1)
                    act.activation(KTR[:, n % 4, :], PS[:, n % 2, :], ACT.Copy).then_inc(sem("kt_odd"), 1)

                def exp(u):
                    t = u % 5
                    r = P if t < 4 else LASTP
                    nk = P * (t + 1) if t < 4 else 4 * P
                    act.wait_ge(sem("pu_max"), 10 * i + u + 1)
                    after(act, sem("pu_t"), 10 * i + u)
                    if t < 4:
                        act.activation(PR[0:r, 0:nk], PS[0:r, 6, 0:nk], ACT.Exp, bias=pst[0:r, 0:1], accum_out=pst[0:r, 3:4])\
                            .then_inc(sem("pu_exp"), 1)
                    else:
                        act.activation(PR[0:r, 0:nk], PS[0:r, 6, 0:nk], ACT.Exp, bias=pst[0:r, 0:1], accum_out=pst[0:r, 4:5])
                        act.activation(PR[0:r, nk:TP], PS[0:r, 4, 0:r], ACT.Exp, bias=pst[0:r, 0:1], accum_out=pst[0:r, 5:6])\
                            .then_inc(sem("pu_exp"), 1)

                def ot(u):
                    hh, t = u // 5, u % 5
                    r = P if t < 4 else LASTP
                    act.wait_ge(sem("pu_v"), 10 * i + u + 1)
                    dst = OTS[DH * hh:DH * hh + DH, i, t * P:t * P + r] if isinstance(i, int) else \
                        OTS[DH * hh:DH * hh + DH, bass.ds(i, 1), t * P:t * P + r].rearrange("p a n -> p (a n)")
                    act.activation(dst, PS[DH * hh:DH * hh + DH, 3, 0:r], ACT.Copy).then_inc(sem("pu_ot"), 1)

                def p_out(part):
                    act.wait_ge(sem("ptt_tr"), 5 * i - 5 + part + 1)
                    after(act, sem("o_mm"), i - 1)
                    if part < NCH:
                        act.activation(PTT[:, CH * part:CH * part + CH, :], PS[:, 4, :].rearrange("p (g n) -> p g n", n=P), ACT.Copy)\
                            .then_inc(sem("ptt_ready"), 1)
                    else:
                        act.activation(PTT[0:64, PAGES, :], PS[0:64, 4, 0:P], ACT.Copy).then_inc(sem("ptt_ready"), 1)

                for n in range(TICKS):
                    if front:
                        if n % 2 == 1 and n < KTICKS:
                            evac(n)
                        if n in V_TICK:
                            ot(V_TICK.index(n))
                        if n in S_TICK:
                            exp(S_TICK.index(n))
                    if back:
                        if n == 1:
                            act.wait_ge(sem("sp_max"), 2 * i)
                            act.activation(SROW[:, :], SROW[:, :], ACT.Exp, bias=sst[:, 0:1], accum_out=sst[:, 1:2])\
                                .then_inc(sem("sp_exp"), 1)
                        if n in P_TICK:
                            p_out(P_TICK.index(n))
                        if n == OT_TICK - 1:
                            act.wait_ge(sem("o_mm"), i)
                            act.wait_ge(sem("sp_rec"), i)
                            after(act, sem("ob_tr"), i - 1)
                            act.activation(OB, PS[:, 5, 0:256], ACT.Copy, scale=sst[:, 2:3]).then_inc(sem("ob_ready"), 1)

            attention(0, back=False)
            with act.Fori(1, NB) as i:
                attention(i)
            attention(NB, front=False)
            router(1, "h_attn")
            moe(1)

        @block.vector
        def _(dve):
            steps = [0]

            def then(ins):
                steps[0] += 1
                ins.then_inc(sem("dve_step"), 1)
                dve.wait_ge(sem("dve_step"), steps[0])

            def root(name):
                n = NORMS.index(name) + 1
                dve.wait_ge(sem("sq"), NT * (n + (name == "r1")))
                dve.tensor_scalar(ms[:, :], ss[:, :], 1.0 / D, EPS, ALU.mult, ALU.add).then_inc(sem("ms"), 1)
                dve.wait_ge(sem("sd"), n)
                then(dve.reciprocal(rs[:, :], sd[:, :]))

            dve.memset(ss[:, :], 1.0).then_inc(sem("ss_one"), 1)
            dve.wait_ge(sem("pool_in"), 16 * 5)
            for cc in range(2):
                ins = dve.tensor_tensor(pw[:, :, cc, :], pw[:, :, cc, :], psc.rearrange("p (g n) -> p g n", g=NG), ALU.mult)
            ins.then_inc(sem("ws_ready"), 1)
            root("pool")
            for t in range(NT):
                r = ROWS[t]
                dve.scalar_tensor_tensor(out=U[t][0:r, :], in0=H[0:r, t, :], scalar=rs[0:r, t:t + 1], in1=png[0:r, :],
                                         op0=ALU.mult, op1=ALU.mult).then_inc(sem("u_ready"), 1)
            for n in range(NH // 2):
                dve.wait_ge(sem("tt_tr"), n + 1)
                dve.tensor_copy(TT[:, 2 * n:2 * n + 2, :], PS[:, 6 + n % 2, :].rearrange("p (h m) -> p h m", h=2))\
                    .then_inc(sem("tt_ready"), 1)
            for t in range(NT):
                r = ROWS[t]
                dve.wait_ge(sem("dt_mm"), t + 1)
                if t >= 2:
                    dve.wait_ge(sem("pool_mm"), t - 1)
                dve.tensor_copy(DT[t % 2][:, 0:4, 0:r], PS[:, 0, :].rearrange("p (k n) -> p k n", k=4)[:, :, 0:r])\
                    .then_inc(sem("dt_ready"), 1)
                dve.wait_ge(sem("pool_mm"), t + 1)
                b = 2 + 2 * (t % 2)
                dve.tensor_tensor(H[0:r, t, :], H[0:r, t, :], PS[0:r, b:b + 2, :].rearrange("p a n -> p (a n)"), ALU.add)\
                    .then_inc(sem("h_pool"), 1)

            def gained(dst, bank, which, r):
                for half in range(2):
                    g = gains[:, which, 4 * half:4 * half + 4].rearrange("p (k a) -> p k a", a=1).to_broadcast([P, 4, r])
                    ins = dve.tensor_tensor(dst[:, 4 * half:4 * half + 4, 0:r],
                                            PS[:, bank + half, :].rearrange("p (k n) -> p k n", k=4)[:, :, 0:r], g, ALU.mult)
                return ins

            def router(l):
                root(f"r{l}")
                if l == 0:
                    dve.wait_ge(sem("small_in"), 16 * SMALL)
                for t in range(NT):
                    r = ROWS[t]
                    if t >= 2:
                        dve.wait_ge(sem("un_tr"), t - 1 + l * NT)
                        dve.wait_ge(sem(f"xs_out_{t % 2}"), 16 * (t // 2) + (48 - 16 * (t % 2)) * l)
                    dve.tensor_scalar(YS[t % 2][0:r, :], H[0:r, t, :], rs[0:r, t:t + 1], None, ALU.mult).then_inc(sem("un_ready"), 1)
                    dve.wait_ge(sem("un_tr"), t + 1 + l * NT)
                    if t >= 2:
                        dve.wait_ge(sem("router_done"), t - 1 + l * NT)
                    gained(XU[t % 2], 2 * (t % 2), l, r).then_inc(sem("xu_ready"), 1)
                dve.wait_ge(sem("router_done"), NT + l * NT)

                def v(name, n=None):
                    return rt[name] if n is None else rt[name].rearrange("p (t e) -> p t e", e=n)

                def bc(name, n):
                    return rt[name].rearrange("p (t a) -> p t a", a=1).to_broadcast([P, NT, n])

                def cb(name, n):
                    return c(name).rearrange("p (a n) -> p a n", a=1).to_broadcast([P, NT, n])

                then(dve.memset(v("L"), 0.0))
                dve.tensor_copy(v("L")[:, 0:80], PS[:, 6, 0:80])
                then(dve.tensor_copy(v("L")[0:64, 80:100], PS[0:64, 6, 80:100]))
                lg = v("L", 20)[:, :, 0:4]
                le = v("L", 20)[:, :, 4:20].rearrange("p t (g e) -> p t g e", g=NG)
                then(dve.tensor_reduce(v("mx"), lg, X, ALU.max))
                dve.tensor_tensor(v("dl", 4), lg, bc("mx", 4), ALU.subtract).then_inc(sem("rt_in"), 1)
                then(dve.tensor_tensor(v("v4", 4), lg, bc("mx", 4), ALU.is_equal))
                then(dve.tensor_tensor(v("v4", 4), v("v4", 4), cb("w4", 4), ALU.mult))
                then(dve.tensor_reduce(v("vm"), v("v4", 4), X, ALU.max))
                then(dve.tensor_tensor(v("oh", 4), v("v4", 4), bc("vm", 4), ALU.is_equal))
                dve.tensor_scalar(v("pen"), v("oh"), 1.0, BIG, ALU.subtract, ALU.mult)
                ohb = v("oh").rearrange("p (n a) -> p n a", a=1).to_broadcast([P, NT * 4, 4])
                penb = v("pen").rearrange("p (n a) -> p n a", a=1).to_broadcast([P, NT * 4, 4])
                LMg = v("LM").rearrange("p (n e) -> p n e", e=4)
                for t in range(NT):
                    ins = dve.tensor_tensor(LMg[:, 4 * t:4 * t + 4, :], le[:, t], ohb[:, 4 * t:4 * t + 4, :], ALU.mult)
                then(ins)
                then(dve.tensor_tensor(LMg, LMg, penb, ALU.add))
                then(dve.tensor_reduce(v("m1"), v("LM", NE), X, ALU.max))
                then(dve.tensor_tensor(v("e1", NE), v("LM", NE), bc("m1", NE), ALU.is_equal))
                then(dve.tensor_tensor(v("e1", NE), v("e1", NE), cb("w16", NE), ALU.mult))
                then(dve.tensor_reduce(v("vm"), v("e1", NE), X, ALU.max))
                then(dve.tensor_tensor(v("oh1", NE), v("e1", NE), bc("vm", NE), ALU.is_equal))
                then(dve.scalar_tensor_tensor(out=v("LM2"), in0=v("oh1"), scalar=-2 * BIG, in1=v("LM"), op0=ALU.mult, op1=ALU.add))
                then(dve.tensor_reduce(v("m2"), v("LM2", NE), X, ALU.max))
                dve.tensor_tensor(v("d"), v("m2"), v("m1"), ALU.subtract).then_inc(sem("rt_in"), 1)
                then(dve.tensor_tensor(v("e1", NE), v("LM2", NE), bc("m2", NE), ALU.is_equal))
                then(dve.tensor_tensor(v("e1", NE), v("e1", NE), cb("w16", NE), ALU.mult))
                then(dve.tensor_reduce(v("vm"), v("e1", NE), X, ALU.max))
                then(dve.tensor_tensor(v("oh2", NE), v("e1", NE), bc("vm", NE), ALU.is_equal))
                val = c("valid").rearrange("p (t a) -> p t a", a=1).to_broadcast([P, NT, NE])
                dve.tensor_tensor(v("oh1", NE), v("oh1", NE), val, ALU.mult)
                then(dve.tensor_tensor(v("oh2", NE), v("oh2", NE), val, ALU.mult))
                dve.tensor_tensor(v("A"), v("oh1"), v("oh2"), ALU.add).then_inc(sem("picks_ready"), 1)
                dve.wait_ge(sem("rt_exp"), 1 + l * 2)
                then(dve.tensor_reduce(v("sum"), v("eg", 4), X, ALU.add))
                dve.reciprocal(v("ptop"), v("sum"))
                dve.wait_ge(sem("rt_exp"), 2 + l * 2)
                then(dve.tensor_scalar(v("den"), v("ed"), 1.0, None, ALU.add))
                then(dve.reciprocal(v("rden"), v("den")))
                then(dve.tensor_tensor(gate[:, 0, :], v("ptop"), v("rden"), ALU.mult))
                then(dve.tensor_tensor(gate[:, 1, :], gate[:, 0, :], v("ed"), ALU.mult))
                then(dve.memset(v("R"), 0.0))
                dve.wait_ge(sem("ranks"), 1 + l * 1)
                dve.tensor_copy(v("R")[:, 0:4 * NE], PS[:, 7, 0:4 * NE])
                dve.tensor_copy(v("tot")[:, :], PS[:, 7, NT * NE:NT * NE + NE])
                then(dve.tensor_copy(v("R")[0:64, 4 * NE:], PS[0:64, 7, 4 * NE:NT * NE]))
                then(dve.scalar_tensor_tensor(out=v("R", NE), in0=v("R", NE), scalar=float(NE), in1=cb("eid", NE),
                                              op0=ALU.mult, op1=ALU.add))
                dve.tensor_tensor(v("oh1"), v("oh1"), v("R"), ALU.mult)
                then(dve.tensor_tensor(v("oh2"), v("oh2"), v("R"), ALU.mult))
                dve.tensor_reduce(v("SL")[:, 0:NT], v("oh1", NE), X, ALU.add)
                then(dve.tensor_reduce(v("SL")[:, NT:], v("oh2", NE), X, ALU.add))
                then(dve.tensor_tensor(v("SS"), v("SL"), c("junk"), ALU.add))
                then(dve.tensor_scalar(v("Sm"), v("SL"), float(P * NE), None, ALU.is_lt))
                dve.tensor_tensor(gm[:, :, :].rearrange("p c t -> p (c t)"), gate[:, :, :].rearrange("p c t -> p (c t)"), v("Sm"), ALU.mult)
                then(dve.tensor_tensor(v("Sm"), v("Sm"), v("SL"), ALU.mult))
                dve.tensor_copy(SLi[:, :, :].rearrange("p c t -> p (c t)"), v("Sm"))
                then(dve.tensor_copy(SSi[:, :, :].rearrange("p c t -> p (c t)"), v("SS")))
                dve.sem_inc(sem("slots_ready"), 1)
                then(dve.tensor_reduce(v("nm"), v("tot"), X, ALU.max))
                for k in range(1, 5):
                    ins = dve.tensor_scalar(v("np")[:, k - 1:k], v("nm"), P * k + 0.5, None, ALU.is_ge)
                then(ins)
                then(dve.tensor_reduce(v("nf"), v("np"), X, ALU.add))
                then(dve.tensor_scalar(v("nf"), v("nf"), 1.0, None, ALU.add))
                dve.tensor_copy(npi[0:1, 0:1], v("nf")[0:1, :]).then_inc(sem("np_ready"), 1)

            def moe(l):
                def xt(e):
                    dve.wait_ge(sem("xt_tr"), e + 1 + l * NE)
                    gained(XT, 0, l, P).then_inc(sem("xt_ready"), 1)

                def hidden(e):
                    dve.wait_ge(sem("silu_done"), e + 1 + l * NE)
                    dve.wait_ge(sem("up_done"), e + 1 + l * NE)
                    after(dve, sem("ht_tr"), e + l * NE)
                    dve.tensor_tensor(HH, SG, PS[:, 3, :], ALU.mult).then_inc(sem("h_ready"), 1)

                xt(0)
                hidden(0)
                xt(1)
                with dve.Fori(1, NE - 1) as e:
                    hidden(e)
                    xt(e + 1)
                hidden(NE - 1)
                dve.wait_ge(sem("np_ready"), 1 + l * 1)
                npass = dve.value_load(npi[0:1, 0:1], min_val=1, max_val=RANKS // P)
                with dve.If(npass > 1):
                    with dve.Fori(1, npass) as p:
                        with dve.Fori(0, NE) as e:
                            n = p * NE + e - NE
                            dve.wait_ge(sem(f"g_step{l}"), 9 * n + 1)
                            gained(XT, 0, l, P).then_inc(sem(f"g_step{l}"), 1)
                            dve.wait_ge(sem(f"g_step{l}"), 9 * n + 4)
                            dve.tensor_tensor(HH, SG, PS[:, 3, :], ALU.mult).then_inc(sem(f"g_step{l}"), 1)
                        chain = [0]

                        def link(ins):
                            chain[0] += 1
                            ins.then_inc(sem(f"g_dve{l}"), 1)
                            dve.wait_ge(sem(f"g_dve{l}"), LINKS * p - LINKS + chain[0])

                        SL, Sm = rt["SL"], rt["Sm"]
                        link(dve.tensor_scalar(SL, SL, float(P * NE), None, ALU.subtract))
                        link(dve.tensor_scalar(Sm, SL, 0.0, None, ALU.is_ge))
                        link(dve.scalar_tensor_tensor(out=Sm, in0=SL, scalar=float(P * NE), in1=Sm, op0=ALU.is_lt, op1=ALU.mult))
                        link(dve.tensor_tensor(gg[:, :, :].rearrange("p c t -> p (c t)"), gate[:, :, :].rearrange("p c t -> p (c t)"),
                                               Sm, ALU.mult))
                        link(dve.tensor_tensor(Sm, SL, Sm, ALU.mult))
                        dve.tensor_copy(SGi[:, :, :].rearrange("p c t -> p (c t)"), Sm).then_inc(sem(f"g_sum{l}"), 1)
                        for t in range(NT):
                            r = ROWS[t]
                            dve.wait_ge(sem(f"g_yg{l}"), 32 * NT * p + 32 * (t + 1 - NT))
                            link(dve.scalar_tensor_tensor(out=H[0:r, t, :], in0=K8[0:r, 0, :], scalar=gg[0:r, 0, t:t + 1],
                                                          in1=H[0:r, t, :], op0=ALU.mult, op1=ALU.add))
                            dve.scalar_tensor_tensor(out=H[0:r, t, :], in0=K8[0:r, 1, :], scalar=gg[0:r, 1, t:t + 1],
                                                     in1=H[0:r, t, :], op0=ALU.mult, op1=ALU.add).then_inc(sem(f"g_sum{l}"), 1)
                        assert chain[0] == LINKS
                for t in range(NT):
                    r = ROWS[t]
                    dve.wait_ge(sem(f"yg_in_{t}"), 32 + l * 32)
                    for ch in range(2):
                        ins = dve.scalar_tensor_tensor(out=H[0:r, t, :], in0=K8[0:r, (2 * t + ch) % 8, :], scalar=gm[0:r, ch, t:t + 1],
                                                       in1=H[0:r, t, :], op0=ALU.mult, op1=ALU.add)
                        if ch == 0:
                            then(ins)
                    ins.then_inc(sem("h_sum"), 1)

            router(0)
            moe(0)

            then(dve.memset(LF[:, :, :], 0.0))
            dve.memset(hms[:, :, :], 1.0)
            dve.memset(hss[:, :, :], 1.0)
            ins = dve.tensor_scalar(qg[:, :], qg[:, :], float(DH) ** -0.5, None, ALU.mult)
            then(ins)

            def head_norm(which, r, t):
                dve.wait_ge(sem("head_sq"), 2 * t + which + 1)
                then(dve.tensor_reduce(hss[0:r, which, :], SQ[0:r, :].rearrange("p (h d) -> p h d", d=DH), X, ALU.add))
                dve.tensor_scalar(hms[0:r, which, :], hss[0:r, which, :], 1.0 / DH, EPS, ALU.mult, ALU.add).then_inc(sem("head_ms"), 1)
                dve.wait_ge(sem("head_sd"), 2 * t + which + 1)
                then(dve.reciprocal(hrs[:, which, :], hsd[:, which, :]))
                return hrs[0:r, which, :].rearrange("p (h a) -> p h a", a=1).to_broadcast([r, NH, DH])

            def rows(t):
                r = ROWS[t]
                dve.wait_ge(sem("sq"), 2 * NT + t + 1)
                dve.tensor_scalar(ms[:, t:t + 1], ss[:, t:t + 1], 1.0 / D, EPS, ALU.mult, ALU.add).then_inc(sem("row_ms"), 1)
                dve.wait_ge(sem("row_sd"), t + 1)
                then(dve.reciprocal(rs[:, t:t + 1], sd[:, t:t + 1]))
                after(dve, sem("pun_tr"), t)
                dve.tensor_scalar(UN[0:r, :], H[0:r, t, :], rs[0:r, t:t + 1], None, ALU.mult).then_inc(sem("pun_ready"), 1)

            def gains_in(t):
                r = ROWS[t]
                dve.wait_ge(sem("pun_tr"), t + 1)
                after(dve, sem("v_mm"), t - 1)
                if t == 1:
                    dve.wait_ge(sem("h_sum"), NT)
                gained(UK[t % 2], 0, 2, r).then_inc(sem("ux_ready"), 1)
                after(dve, sem("q_mm"), t - 1)
                gained(UQ[t % 2], 0, 3, r).then_inc(sem("ux_ready"), 1)

            def merge(b, done):
                dve.wait_ge(sem(done), NT)
                dve.wait_ge(sem("upper_ready"), b // 2)
                both = PS[0:64, b:b + 2, :].rearrange("p a n -> p (a n)")
                dve.tensor_tensor(both, both, UPPER[0:64, :], ALU.add).then_inc(sem("merged"), 1)

            rows(0)
            gains_in(0)
            for t in range(NT):
                r = ROWS[t]
                heads = lambda a: a.rearrange("p (h d) -> p h d", d=DH)
                two = lambda b: PS[0:r, b:b + 2, :].rearrange("p a (h d) -> p (a h) d", d=DH)
                if t == 0:
                    rows(1)
                if t == 4:
                    merge(2, "k_mm")
                rk = head_norm(0, r, t)
                if t:
                    dve.wait_ge(sem("kn_tr"), t)
                    dve.wait_ge(sem("kout"), 16 * t)
                dve.tensor_tensor(heads(KN[0:r, :]), two(2), rk, ALU.mult).then_inc(sem("kn_ready"), 1)
                dve.wait_ge(sem("kn_ready"), 2 * t + 1)
                kg = kgb[0:r, :].rearrange("p (a d) -> p a d", a=1).to_broadcast([r, NH, DH])
                dve.tensor_tensor(heads(KN[0:r, :]), heads(KN[0:r, :]), kg, ALU.mult).then_inc(sem("kn_ready"), 1)
                dve.wait_ge(sem("f_mm"), t + 1)
                dve.tensor_tensor(LF[0:r, t, :], PS[0:r, 6, 0:NH], bfb[0:r, :], ALU.add).then_inc(sem("f_ready"), 1)
                if t == 4:
                    merge(4, "v_mm")
                if t + 1 < NT:
                    gains_in(t + 1)
                if t + 2 < NT:
                    rows(t + 2)
                if t == 4:
                    merge(6, "q_mm")
                rq = head_norm(1, r, t)
                dve.sem_inc(sem("ssq_ready"), 1)
                if t:
                    dve.wait_ge(sem("qn_tr"), t)
                dve.tensor_tensor(heads(QN[0:r, :]), two(6), rq, ALU.mult).then_inc(sem("qn_ready"), 1)
            lf = LF[:, :, :].rearrange("p t h -> p (t h)")
            dve.wait_ge(sem("f_ready"), NT)
            then(dve.scalar_tensor_tensor(out=lfa, in0=lf, scalar=-1.0, in1=lf, op0=ALU.mult, op1=ALU.max))
            dve.sem_inc(sem("lf_step"), 1)
            dve.wait_ge(sem("lf_step"), 2)
            dve.tensor_scalar(lfe, lfe, 1.0, None, ALU.add).then_inc(sem("lf_step"), 1)
            dve.wait_ge(sem("lf_step"), 4)
            then(dve.scalar_tensor_tensor(out=lf, in0=lf, scalar=0.0, in1=lfa, op0=ALU.min, op1=ALU.subtract))
            dve.sem_inc(sem("lf_step"), 1)
            dve.wait_ge(sem("q_mm"), NT)
            then(dve.memset(LR[0:64, :], 0.0))
            dve.tensor_copy(LR[0:64, :].rearrange("p (a h q) -> p a h q", a=4, q=NS)[:, :, 0:4, :],
                            LF[0:64, 4, :].rearrange("p (a h o) -> p a h o", a=4, o=1).to_broadcast([64, 4, 4, NS]))\
                .then_inc(sem("extra_ready"), 1)
            dve.memset(PR[:, :], 1.0).then_inc(sem("extra_ready"), 1)
            dve.memset(OTS[:, :, 4 * P:4 * P + 64], 0.0)
            then(dve.memset(QBLK[:, :, :], 0.0))
            dve.wait_ge(sem("ct_mm"), 2)
            sm = c("smask").rearrange("p (b n) -> p b n", b=NB)
            for b in range(NB):
                ins = dve.tensor_tensor(sm[:, b, :], sm[:, b, :], PS[:, 4, 0:64], ALU.add)
            then(ins)
            dve.wait_ge(sem("qts_ready"), NT)
            dve.wait_ge(sem("ct_ready"), 2)
            dve.wait_ge(sem("ktd_out"), 32 * NT + 16)
            dve.wait_ge(sem("qtd_out"), 32 * NT + 16)
            dve.wait_ge(sem("kout"), 16 * (NT + 1))
            dve.wait_ge(sem("vout"), 16 * NT)
            dve.sem_inc(sem("proj_done"), 1)

            def attention(i, front=True, back=True):
                one = isinstance(i, int)

                def evac(n):
                    dve.wait_ge(sem("kt_tr"), 32 * i + n + 1)
                    after(dve, sem("qk_done"), 16 * i + n // 2 - 1)
                    dve.tensor_copy(KTR[:, n % 4, :], PS[:, n % 2, :]).then_inc(sem("kt_even"), 1)

                def pmax(u):
                    t = u % 5
                    r = P if t < 4 else LASTP
                    nk = P * (t + 1) if t < 4 else 4 * P
                    dve.wait_ge(sem("pu_s"), 10 * i + u + 1)
                    after(dve, sem("pu_exp"), 10 * i + u)
                    if t < 4:
                        dve.tensor_reduce(pst[0:r, 0:1], PS[0:r, 6, 0:nk], X, ALU.max, negate=True).then_inc(sem("pu_max"), 1)
                    else:
                        dve.tensor_reduce(pst[0:r, 1:2], PS[0:r, 6, 0:nk], X, ALU.max, negate=True)
                        dve.tensor_reduce(pst[0:r, 2:3], PS[0:r, 4, 0:r], X, ALU.max, negate=True).then_inc(sem("pu_last"), 1)
                        dve.wait_ge(sem("pu_last"), 4 * i + 2 * (u // 5) + 1)
                        dve.tensor_tensor(pst[0:r, 0:1], pst[0:r, 1:2], pst[0:r, 2:3], ALU.min).then_inc(sem("pu_max"), 1)

                def pnorm(u):
                    t = u % 5
                    r = P if t < 4 else LASTP
                    nk = P * (t + 1) if t < 4 else TP
                    dve.wait_ge(sem("pu_exp"), 10 * i + u + 1)
                    if t == 4:
                        dve.tensor_tensor(pst[0:r, 3:4], pst[0:r, 4:5], pst[0:r, 5:6], ALU.add).then_inc(sem("pu_last"), 1)
                        dve.wait_ge(sem("pu_last"), 4 * i + 2 * (u // 5) + 2)
                    dve.reciprocal(pst[0:r, 6:7], pst[0:r, 3:4]).then_inc(sem("pu_rec"), 1)
                    dve.wait_ge(sem("pu_rec"), 10 * i + u + 1)
                    dve.tensor_scalar(PR[0:r, 0:nk], PR[0:r, 0:nk], pst[0:r, 6:7], None, ALU.mult).then_inc(sem("pu_norm"), 1)

                def pts(u):
                    t = u % 5
                    dve.wait_ge(sem("pu_t"), 10 * i + u + 1)
                    after(dve, sem("pu_v"), 10 * i + u)
                    if t < 4:
                        dve.tensor_copy(PTS[:, 0:P * (t + 1)], PS[:, 7, 0:P * (t + 1)]).then_inc(sem("pu_pts"), 1)
                    else:
                        r = LASTP
                        dve.tensor_copy(PTS[:, 0:4 * r], PS[:, 7, 0:4 * r])
                        dve.tensor_copy(PTS[0:r, 4 * r:5 * r], PS[0:r, 7, 4 * r:5 * r]).then_inc(sem("pu_pts"), 1)

                def scores(b, ch):
                    dve.wait_ge(sem("qk_done"), 16 * b + 4 * ch + 4)
                    dve.wait_ge(sem(f"bias_in{ch // 2}"), 64 * (b + 1))
                    if ch < NCH - 1 and not (isinstance(b, int) and b == 0):
                        dve.wait_ge(sem("ptt_tr"), 5 * b - 5 + ch + 1)
                    row = SROW[:, 512 * ch:512 * ch + 512]
                    dve.tensor_tensor(row, PS[:, 2, :], BIAS[:, 512 * ch:512 * ch + 512], ALU.add).then_inc(sem("s_ready"), 1)

                def largest(b, ch):
                    dve.wait_ge(sem("s_ready"), 4 * b + ch + 1)
                    return dve.tensor_reduce(smx[:, ch:ch + 1], SROW[:, 512 * ch:512 * ch + 512], X, ALU.max)

                if back:
                    scores(i - 1, NCH - 1)
                for n in range(TICKS):
                    if front and n % 2 == 0 and n < KTICKS:
                        evac(n)
                    if n == 0:
                        if back:
                            largest(i - 1, NCH - 1).then_inc(sem("sp_max"), 1)
                            dve.wait_ge(sem("sp_max"), 2 * i - 1)
                            dve.tensor_reduce(sst[:, 0:1], smx[:, :], X, ALU.max, negate=True).then_inc(sem("sp_max"), 1)
                        if front:
                            after(dve, sem("qk_done"), 16 * i)
                            for half in range(2):
                                for j in range(2):
                                    src = QT4[DH * half:DH * half + DH, j:HP:2, :]
                                    src = src[:, :, S0 + NS * i:S0 + NS * i + NS] if one else src[:, :, bass.ds(NS * i + S0, NS)]
                                    at = 8 * j + NS * half
                                    ins = dve.tensor_copy(QBLK[DH * half:DH * half + DH, j:HP:2, at:at + NS], src)
                            ins.then_inc(sem("qb_ready"), 1)
                    if back and n == P_TICK[0]:
                        dve.wait_ge(sem("sp_exp"), i)
                        after(dve, sem("ob_ready"), i - 1)
                        dve.reciprocal(sst[:, 2:3], sst[:, 1:2]).then_inc(sem("sp_rec"), 1)
                    if front:
                        if n in QK_TICK[3:-1:4]:
                            ch = QK_TICK.index(n) // 4
                            scores(i, ch)
                            largest(i, ch)
                        if n == NEW_TICK:
                            dve.wait_ge(sem("sn_mm"), i + 1)
                            after(dve, sem("ptt_tr"), 5 * i)
                            m = sm[:, i, :] if one else sm[:, bass.ds(i, 1), :].rearrange("p a n -> p (a n)")
                            dve.tensor_tensor(SROW[:, PAGES * PAGE:], PS[:, 2, 0:64], m, ALU.add).then_inc(sem("sn_ready"), 1)
                            dve.wait_ge(sem("sn_ready"), i + 1)
                            dve.tensor_reduce(smx[:, NCH:NCH + 1], SROW[:, PAGES * PAGE:], X, ALU.max)
                        if n in T_TICK:
                            pts(T_TICK.index(n))
                        if n in S_TICK:
                            pmax(S_TICK.index(n))
                        if n - 1 in S_TICK:
                            pnorm(S_TICK.index(n - 1))
                    if back and n == OT_TICK:
                        dve.wait_ge(sem("ob_tr"), i)
                        for half in range(2):
                            for x in range(2):
                                rows = slice(DH * half, DH * half + DH)
                                src = PS[rows, 5, 256 + x * P:256 + (x + 1) * P].rearrange("p (q n) -> p q n", q=4)
                                src = src[:, :, 8 * x + 4 * half:8 * x + 4 * half + NS]
                                at = 4 * P + S0 - NS
                                dst = OTS[rows, x:HP:2, :]
                                dst = dst[:, :, at + NS * i:at + NS * i + NS] if one else dst[:, :, bass.ds(NS * i + at, NS)]
                                ins = dve.tensor_copy(dst, src)
                            ins.then_inc(sem("ots_ready"), 1)

            attention(0, back=False)
            with dve.Fori(1, NB) as i:
                attention(i)
            attention(NB, front=False)

            for t in range(NT):
                r = ROWS[t]
                dve.wait_ge(sem("wo_done"), t + 1)
                b = 2 * (t % 2)
                dve.tensor_tensor(H[0:r, t, :], H[0:r, t, :], PS[0:r, b:b + 2, :].rearrange("p a n -> p (a n)"), ALU.add)\
                    .then_inc(sem("h_attn"), 1)
            router(1)
            moe(1)

        assert n_out[0] == OUTS, n_out


INPUTS = ["x_prompt", "x_sample", "state_pool", "cache_k", "cache_v", "cache_logf", "page_table", "meta", "pool_norm_g",
          "pool_w", "pool_scale", "kv_norm_g", "w_kvf", "b_f", "k_norm_g", "attn_norm_g", "w_q", "q_norm_g", "w_o",
          "ffn_norm_g", "w_router_group", "w_router_expert", "w_gate", "w_up", "w_down"]
OUTPUTS = [("y_prompt", (1, SEQ, D)), ("y_sample", (NB, NS, D)), ("pool_state_prompt", (1, 1, STATE, D)),
           ("pool_state_sample", (1, NB, STATE, D)), ("k_prompt", (1, TP, NH, DH)), ("v_prompt", (1, TP, NH, DH)),
           ("logf_prompt", (1, TP, NH)), ("k_sample", (NB, NS, NH, DH)), ("v_sample", (NB, NS, NH, DH)),
           ("logf_sample", (NB, NS, NH))]


def kernel(**inputs):
    import concourse.bacc as bacc
    from concourse.bass_utils import run_bass_kernel_spmd

    nc = bacc.Bacc("TRN2", target_bir_lowering=False, num_devices=1)
    consts, bands, ids = shape_constants()
    arrays = {name: np.ascontiguousarray(inputs[name]) for name in INPUTS}
    arrays.update(consts=consts, bands=bands, ids=ids)
    A = {name: nc.dram_tensor(f"in_{name}", a.shape, mybir.dt.from_np(a.dtype), kind="ExternalInput").ap()
         for name, a in arrays.items()}
    O = {name: nc.dram_tensor(f"out_{name}", shape, F32, kind="ExternalOutput").ap() for name, shape in OUTPUTS}
    build(nc, A, O)
    r = run_bass_kernel_spmd(nc, [{f"in_{name}": a for name, a in arrays.items()}], core_ids=[0])
    return tuple(r.results[0][f"out_{name}"] for name, _ in OUTPUTS)
```

```python
from contextlib import ExitStack

import numpy as np

import concourse.bass as bass
from concourse import mybir
from concourse.alu_op_type import AluOpType as ALU

F32 = mybir.dt.float32
I32 = mybir.dt.int32
ACT = mybir.ActivationFunctionType
X = mybir.AxisListType.X

P = 128
D = 1024
KC = D // P
META, SEQ = 16, 512
TP = META + SEQ
NT = 5
ROWS = [P, P, P, P, 64]
LASTP = TP - 4 * P
S0 = 32
NB, NS = 8, 4
WINDOWS = (2, 4, 8, 16)
NG = 4
STATE = 15
NH, DH = 16, 64
HP = NH // 2
NE = 16
FF = D // 2
FC = FF // P
PAGES, PAGE = 16, 128
CH = 4
NCH = PAGES // CH
BIG = 1e30
EPS = 1e-6
RANKS = 5 * P
LISTN = RANKS * NE + P
LINKS = 5 + NT
SMALL = 20
NORMS = [("pool", 0)]
for _t in range(NT + 1):
    NORMS += [("pool", _t + 1)] * (_t + 1 < NT) + [("r0", _t - 1)] * (_t > 0)
NORMS += [("proj", _t) for _t in range(NT)] + [("r1", _t) for _t in range(NT)]
OUTS = 14

KTICKS = 32
SHIFT = 3
TICKS = KTICKS + 2
UNITS = 10
S_TICK = [3 * u + 1 for u in range(UNITS)]
T_TICK = [3 * u + 4 for u in range(UNITS)]
V_TICK = [3 * u + 5 for u in range(UNITS)]
QK_TICK = [2 * x + 3 for x in range(KTICKS // 2)]
NEW_TICK = 18
P_TICK = (5, 7, 9, 11, 16)
O_TICK = [g + 8 for g in range(PAGES + 1)]
OT_TICK = 27

CONST = {}
_at = 0
for _name, _n in (("ident", P), ("tails", P), ("before", P), ("upto", P), ("after", P), ("ones", P), ("causal", P),
                  ("negnew", 64), ("smask", NB * 64), ("w4", 4), ("w16", NE), ("eid", NE), ("place", P),
                  ("rid", NT), ("valid", NT), ("junk", 2 * NT)):
    CONST[_name] = (_at, _at + _n)
    _at += _n
NCONST = _at
BAND = {}
_at = 0
for _name, _n in (("cur0", P), ("cur", P), ("prev", P), ("cur4", 64), ("prev4", 64), ("state", 64)):
    BAND[_name] = (_at, _at + NG * _n, _n)
    _at += NG * _n
NBAND = _at


def shape_constants():
    c = np.zeros((P, NCONST), np.float32)

    def put(name, a):
        lo, hi = CONST[name]
        a = np.asarray(a, np.float32).reshape(np.shape(a)[0], -1)
        c[:a.shape[0], lo:hi] = a

    i = np.arange(P)
    put("ident", np.eye(P))
    b, g = i // PAGES, i % PAGES
    put("tails", (b[:, None] == b[None]) & (g[:, None] > g[None]))
    put("before", i[:, None] < i[None])
    put("upto", i[:, None] <= i[None])
    put("after", i[:, None] > i[None])
    put("ones", np.ones((P, P)))
    put("causal", np.where(i[None] <= i[:, None], 0.0, -BIG))
    r = np.arange(64)
    sb, ss = (r - S0) // NS, (r - S0) % NS
    new = r >= S0
    put("negnew", -1.0 * (new[:, None] & new[None] & (sb[:, None] == sb[None]) & (ss[:, None] <= ss[None])))
    q = i % NS
    see = new[None, None] & (sb[None, None] == np.arange(NB)[None, :, None]) & (ss[None, None] <= q[:, None, None])
    put("smask", np.where(see, 0.0, -BIG))
    put("w4", np.tile(4.0 - np.arange(4), (P, 1)))
    put("w16", np.tile(NE - np.arange(NE), (P, 1)))
    put("eid", np.tile(np.arange(NE), (P, 1)))
    put("place", np.tile(i, (P, 1)))
    put("rid", i[:, None] + P * np.arange(NT)[None])
    valid = np.ones((P, NT))
    valid[LASTP:S0, 4] = 0
    valid[64:, 4] = 0
    put("valid", valid)
    junk = np.zeros((P, 2, NT))
    junk[:64, 0, 4] = np.where(valid[:64, 4] == 0, RANKS * NE + r, 0)
    junk[:64, 1, 4] = np.where(valid[:64, 4] == 0, RANKS * NE + 64 + r, 0)
    put("junk", junk)

    w = np.zeros((P, NBAND), np.float32)

    def band(name, rows, cols, f):
        lo, hi, n = BAND[name]
        a = np.zeros((P, NG, n), np.float32)
        for g, win in enumerate(WINDOWS):
            for s in range(rows):
                for t in range(cols):
                    a[s, g, t] = f(win, s, t)
        w[:, lo:hi] = a.reshape(P, -1)

    def own(win, s, t):
        return float(s == t)

    band("cur0", P, P, lambda n, s, t: (t - n < s <= t) / min(t + 1, n) - own(n, s, t))
    band("cur", P, P, lambda n, s, t: (t - n < s <= t) / n - own(n, s, t))
    band("prev", P, P, lambda n, s, t: (s - P > t - n) / n)

    def cur4(n, s, t):
        if s < LASTP and t < LASTP:
            return (t - n < s <= t) / n - own(n, s, t)
        if s >= S0 and t >= S0 and (s - S0) // NS == (t - S0) // NS:
            return (t - n < s <= t) / n - own(n, s, t)
        return 0.0

    band("cur4", 64, 64, cur4)
    band("prev4", P, LASTP, lambda n, s, t: (s - P > t - n) / n)

    def state(n, s, t):
        if t < S0 or s // STATE != (t - S0) // NS:
            return 0.0
        return (s % STATE - STATE > (t - S0) % NS - n) / n

    band("state", NB * STATE, 64, state)
    ids = (np.arange(NT)[None] * P + np.arange(P)[:, None]).astype(np.int32)
    return c, w, ids


def after(eng, sem, value):
    if isinstance(value, int) and value <= 0:
        return
    eng.wait_ge(sem, value)


def build(nc, A, O):
    ctx = ExitStack()
    with ctx:
        ctx.enter_context(nc.allow_non_contiguous_dma(reason="gains, router weights and row lists, small"))

        def sb(name, shape, dt=F32):
            return ctx.enter_context(nc.sbuf_tensor(name, shape, dt))

        sems = {}

        def sem(name):
            if name not in sems:
                sems[name] = ctx.enter_context(nc.semaphore(name))
            return sems[name]

        H = sb("H", [P, NT, D])
        W = sb("W", [P, 6, 4 * D])
        KB = sb("KB", [P, 2, 4 * D])
        VB = sb("VB", [P, 2, 4 * D])
        C = sb("C", [P, NCONST])
        ids = sb("ids", [P, NT], I32)
        gains = sb("gains", [P, 4, KC])
        qg = sb("qg", [P, 1])
        kgb = sb("kgb", [P, DH])
        bfb = sb("bfb", [P, NH])
        wr = sb("wr", [P, 2, KC, NG + NE])
        wf = sb("wf", [P, KC, NH])
        pt = sb("pt", [1, NB * PAGES], I32)
        ptc = sb("ptc", [P, 1], I32)
        ss = sb("ss", [P, NT])
        ms = sb("ms", [P, NT])
        sd = sb("sd", [P, NT])
        rs = sb("rs", [P, NT])
        KQ4 = sb("KQ4", [P, D])
        KT4, QT4 = [KQ4[:, 512 * j:512 * j + 512].rearrange("p (k n) -> p k n", k=HP) for j in range(2)]
        V4 = sb("V4", [P, D])
        zeros = V4[:, 0:LISTN // P].bitcast(I32)
        BIAS = sb("BIAS", [P, PAGES * PAGE])
        LF = sb("LF", [P, NT, NH])
        SLi = sb("SLi", [P, 2, NT], I32)
        SSi = sb("SSi", [P, 2, NT], I32)
        gate = sb("gate", [P, 2, NT])
        gm = sb("gm", [P, 2, NT])
        gg = sb("gg", [P, 2, NT])
        SGi = sb("SGi", [P, 2, NT], I32)
        IDX = sb("IDX", [P, NE], I32)
        idc = sb("idc", [P, 2], I32)
        npi = sb("npi", [1, 1], I32)
        idg = sb("idg", [P, 1], I32)
        hss = sb("hss", [P, 2, NH])
        hms = sb("hms", [P, 2, NH])
        hsd = sb("hsd", [P, 2, NH])
        hrs = sb("hrs", [P, 2, NH])

        def c(name, rows=P):
            lo, hi = CONST[name]
            return C[0:rows, lo:hi]

        ident = c("ident")
        PS = ctx.enter_context(nc.psum_tensor("PS", [P, 8, 512], F32))

        K8 = KB[:, :, :].rearrange("p a (b n) -> p (a b) n", n=D)
        V8 = VB[:, :, :].rearrange("p a (b n) -> p (a b) n", n=D)
        Vf = VB[:, :, :].rearrange("p a n -> p (a n)")
        U = [K8[:, t, :] for t in range(NT)]
        ST = K8[:, 5, :]
        DT = [K8[:, 6 + j, :].rearrange("p (k n) -> p k n", k=8) for j in range(2)]
        bands = Vf[:, 0:NBAND]
        pw = Vf[:, NBAND:NBAND + 2 * D].rearrange("p (g c n) -> p g c n", g=NG, c=2)
        png = Vf[:, NBAND + 2 * D:NBAND + 3 * D]
        psc = Vf[:, NBAND + 3 * D:NBAND + 4 * D]
        LP = W[:, 5, 0:2 * D].rearrange("p (r h) -> p r h", h=NH)
        TT = W[:, 4, :].rearrange("p (h n) -> p h n", h=NH)
        RQ = BIAS[:, :].rearrange("p (h n) -> p h n", h=NH)
        XG = [V8[:, j, :] for j in range(2)]
        YS = [V8[:, 2 + j, :] for j in range(2)]
        XT = V8[:, 4, :].rearrange("p (k n) -> p k n", k=KC)
        SG = V8[:, 5, 0:FF]
        HH = V8[:, 5, FF:2 * FF]
        HT = V8[:, 6, 0:FF].rearrange("p (f n) -> p f n", f=FC)
        XU = [BIAS[:, D * j:D * j + D].rearrange("p (k n) -> p k n", k=KC) for j in range(2)]
        UR = [KQ4[:, :], V4[:, :]]
        PLACE = K8[:, 0:2, :].rearrange("p a n -> p (a n)")[:, 0:2 * NT * P].rearrange("p (x n) -> p x n", n=P)
        UPPER1 = V8[:, 4, :]

        rt = {}
        at = 6 * D + FF
        for name, n in (("L", NT * 20), ("mx", NT), ("dl", NT * 4), ("eg", NT * 4), ("sum", NT), ("ptop", NT),
                        ("oh", NT * 4), ("v4", NT * 4), ("vm", NT), ("pen", NT * 4), ("LM", NT * NE), ("LM2", NT * NE),
                        ("m1", NT), ("m2", NT), ("e1", NT * NE), ("oh1", NT * NE), ("oh2", NT * NE), ("A", (NT + 1) * NE),
                        ("RK", 2 * NT), ("EC", 2 * NT), ("hid", 2 * NT * NE),
                        ("ed", NT), ("den", NT), ("rden", NT), ("SL", 2 * NT), ("SS", 2 * NT), ("Sm", 2 * NT),
                        ("tot", NE), ("nm", 1), ("np", 4), ("nf", 1), ("d", NT)):
            rt[name] = Vf[:, at:at + n]
            at += n
        assert at <= 8 * D
        UN = V8[:, 0, :]
        UK = [a.rearrange("p (k n) -> p k n", k=KC) for a in (V8[:, 1, :], K8[:, 4, :])]
        UQ = [a.rearrange("p (k n) -> p k n", k=KC) for a in (V8[:, 2, :], K8[:, 5, :])]
        UPPER = K8[:, 6, :]
        SQ = V8[:, 3, :]
        KN = V8[:, 4, :]
        QN = V8[:, 5, :]
        VN = V8[:, 6, :]
        TS = V8[:, 7, :].rearrange("p (k n) -> p k n", k=HP)
        Wf = W[:, :, :].rearrange("p a n -> p (a n)")
        aat = [0]

        def carve(n):
            aat[0] += n
            return Wf[:, aat[0] - n:aat[0]]

        KTR = carve(4 * 512).rearrange("p (s n) -> p s n", s=4)
        SROW = carve(PAGES * PAGE + 64)
        PTT = carve((PAGES + 1) * P).rearrange("p (g n) -> p g n", n=P)
        QST = [carve(TP) for _ in range(2)]
        KST = [carve(TP) for _ in range(2)]
        VST = carve(NT * P).rearrange("p (t n) -> p t n", n=P)
        PR = carve(TP)
        PTS = carve(4 * P)
        QBLK = carve(HP * 32).rearrange("p (k n) -> p k n", n=32)
        OB = carve(256)
        smx = carve(NCH + 1)
        sst = carve(4)
        pst = carve(12)
        lfa, lfe = [K8[:, 7, j * P:j * P + NT * NH] for j in range(2)]
        LR = K8[:, 7, 2 * P:3 * P]
        CT = K8[:, 7, 3 * P:3 * P + TP]
        nots = HP * (4 * P + 64)
        OTS = Wf[:, 4 * 4 * D - nots:4 * 4 * D].rearrange("p (k n) -> p k n", k=HP)
        assert aat[0] + nots <= 4 * 4 * D, aat
        VSL = [W[:, 4, :], W[:, 5, :], VB[:, 0, :], VB[:, 1, :]]

        def paged(a):
            return a.rearrange("p (g n) -> p g n", n=D)

        XS = nc.dram_tensor("xs", (4 * P + 64, D), F32).ap()
        LIST = [nc.dram_tensor(f"list{i}", (LISTN, 1), I32).ap() for i in range(2)]
        YD = [nc.dram_tensor(f"yd{i}", (P * NE, D), F32).ap() for i in range(2)]
        YG = [nc.dram_tensor(f"yg{i}", (P * NE, D), F32).ap() for i in range(2)]
        QTD = nc.dram_tensor("qtd", (NH, DH + 1, TP), F32).ap()
        KTD = nc.dram_tensor("ktd", (NH, DH + 1, TP), F32).ap()
        RPD = nc.dram_tensor("rpd", (NH, NS, NB * PAGES, PAGE), F32).ap()
        k_rows = A["cache_k"].rearrange("n r h d -> (n r) (h d)")
        v_rows = A["cache_v"].rearrange("n r h d -> (n r) (h d)")
        kp_out = O["k_prompt"].rearrange("a t h d -> (a t) (h d)")
        vp_out = O["v_prompt"].rearrange("a t h d -> (a t) (h d)")
        fp_out = O["logf_prompt"].rearrange("a t h -> (a t) h")
        ks_out = O["k_sample"].rearrange("b s h d -> (b s) (h d)")
        vs_out = O["v_sample"].rearrange("b s h d -> (b s) (h d)")
        fs_out = O["logf_sample"].rearrange("b s h -> (b s) h")
        xs_rows = A["x_sample"].rearrange("b s d -> (b s) d")
        wkvf = A["w_kvf"].rearrange("(p k) n -> p k n", k=KC)
        wq = A["w_q"].rearrange("l (p k) n -> (l p) k n", k=KC)
        wo = A["w_o"].rearrange("l (k p) n -> p (l k) n", p=P)

        n_out = [0]

        def put_out(eng, dst, src):
            n_out[0] += 1
            eng.dma_start(dst, src).then_inc(sem("out_done"), 16)

        def w_src(l, e, which):
            if which < 2:
                return A["w_gate" if which == 0 else "w_up"][l, e].rearrange("(p k) f -> p (k f)", k=KC)
            return A["w_down"][l, e].rearrange("(p f) n -> p (f n)", f=FC)

        def w_src_dyn(l, e, which):
            name = ("w_gate", "w_up", "w_down")[which]
            t = A[name][l]
            if which < 2:
                return t[bass.ds(e, 1)].rearrange("e (p k) f -> p (e k f)", k=KC)
            return t[bass.ds(e, 1)].rearrange("e (p f) n -> p (e f n)", f=FC)

        def settled(eng):
            eng.nop(nofuse=True)

        block = ctx.enter_context(nc.Block())

        @block.sync
        def _(sp):
            sp.dma_start(H[0:META, 0, :], A["meta"]).then_inc(sem("tile_in_0"), 16)
            sp.dma_start(H[META:P, 0, :], A["x_prompt"][0, 0:P - META, :]).then_inc(sem("tile_in_0"), 16)
            sp.dma_start(png, A["pool_norm_g"][0:1, :].to_broadcast([P, D])).then_inc(sem("pool_in"), 16)
            sp.dma_start(bands, A["bands"]).then_inc(sem("pool_in"), 16)
            sp.dma_start(psc, A["pool_scale"][0:1, :].to_broadcast([P, D])).then_inc(sem("pool_w_in"), 16)
            sp.dma_start(pw, A["pool_w"].rearrange("a g (c p) n -> p (a g) c n", p=P)).then_inc(sem("pool_w_in"), 16)
            sp.dma_start(H[:, 1, :], A["x_prompt"][0, P - META:2 * P - META, :]).then_inc(sem("tile_in_1"), 16)
            sp.dma_start(C[:, :], A["consts"]).then_inc(sem("consts_in"), 16)
            for t in range(2, 4):
                sp.dma_start(H[:, t, :], A["x_prompt"][0, t * P - META:(t + 1) * P - META, :]).then_inc(sem(f"tile_in_{t}"), 16)
            sp.wait_ge(sem("zeros"), 1)
            sp.dma_start(H[0:LASTP, 4, :], A["x_prompt"][0, 4 * P - META:SEQ, :]).then_inc(sem("tile_in_4"), 16)
            sp.dma_start(H[S0:64, 4, :], xs_rows).then_inc(sem("tile_in_4"), 16)
            sp.dma_start(ST[0:NB * STATE, :], A["state_pool"].rearrange("a b s d -> (a b s) d")).then_inc(sem("tile_in_4"), 16)
            for n, (name, l) in enumerate((("ffn_norm_g", 0), ("ffn_norm_g", 1), ("kv_norm_g", None), ("attn_norm_g", 0))):
                g = A[name] if l is None else A[name][l]
                sp.dma_start(gains[:, n, :], g.rearrange("(p k) -> p k", k=KC)).then_inc(sem("small_in"), 16)
            for l in range(2):
                sp.dma_start(wr[:, l, :, 0:NG], A["w_router_group"][l].rearrange("(p k) n -> p k n", k=KC))\
                    .then_inc(sem("small_in"), 16)
                for g in range(NG):
                    sp.dma_start(wr[:, l, :, NG + 4 * g:NG + 4 * g + 4],
                                 A["w_router_expert"][l, g].rearrange("(p k) n -> p k n", k=KC)).then_inc(sem("small_in"), 16)
            sp.dma_start(wf[:, :, :], wkvf[:, :, 2 * D:2 * D + NH]).then_inc(sem("small_in"), 16)
            for half in range(2):
                sp.dma_start(qg[half * DH:(half + 1) * DH, :], A["q_norm_g"].rearrange("a d -> d a")).then_inc(sem("small_in"), 16)
            sp.dma_start(kgb[:, :], A["k_norm_g"].rearrange("(a d) -> a d", a=1).to_broadcast([P, DH])).then_inc(sem("small_in"), 16)
            sp.dma_start(bfb[:, :], A["b_f"].rearrange("(a d) -> a d", a=1).to_broadcast([P, NH])).then_inc(sem("small_in"), 16)
            sp.dma_start(pt[:, :], A["page_table"].rearrange("(a b) g -> a (b g)", a=1)).then_inc(sem("small_in"), 16)
            n_out[0] += 1
            sp.dma_start(O["pool_state_sample"][0, :, 0:STATE - NS, :], A["state_pool"][0, :, NS:STATE, :])\
                .then_inc(sem("out_done"), 16)

            def moe_weights(l):
                def load(e, which, j):
                    done = sem(f"{('gate', 'up', 'down')[which]}_done")
                    if isinstance(e, int):
                        after(sp, done, e - 1 + l * NE)
                        sp.dma_start(W[:, 3 * j + which, :], w_src(l, e, which)).then_inc(sem(f"w_in_{3 * j + which}"), 16)
                    else:
                        sp.wait_ge(done, e - 1 + l * NE)
                        settled(sp)
                        sp.dma_start(W[:, 3 * j + which, :], w_src_dyn(l, e, which)).then_inc(sem(f"w_in_{3 * j + which}"), 16)

                def first(part):
                    if part == 0:
                        load(0, 0, 0)
                        load(0, 1, 0)
                    else:
                        load(0, 2, 0)
                        load(1, 0, 1)

                def second():
                    load(1, 1, 1)
                    load(1, 2, 1)

                def rest():
                    with sp.Fori(2, NE - 1, 2) as e:
                        for j in range(2):
                            for which in range(3):
                                load(e + j, which, j)
                return first, second, rest

            def moe_general(l):
                sp.wait_ge(sem("np_ready"), 1 + l * 1)
                npass = sp.value_load(npi[0:1, 0:1], min_val=1, max_val=RANKS // P)
                with sp.If(npass > 1):
                    sp.wait_ge(sem("down_done"), NE + l * NE)
                    sp.wait_ge(sem("scattered"), 16 * 2 * NT + l * (32 * NT))
                    with sp.Fori(1, npass) as p:
                        with sp.Fori(0, NE) as e:
                            n = p * NE + e - NE
                            sp.dma_start(idg[:, :], LIST[l][0:RANKS * NE, :].rearrange("(r e) o -> r (e o)", e=NE)
                                         [bass.ds(p * P, P), bass.ds(e, 1)]).then_inc(sem(f"g_in{l}"), 16)
                            for which in range(3):
                                sp.dma_start(W[:, which, :], w_src_dyn(l, e, which)).then_inc(sem(f"g_in{l}"), 16)
                            sp.wait_ge(sem(f"g_y_out{l}"), 16 * (n + 1))
                            settled(sp)
                        sp.wait_ge(sem(f"g_sum{l}"), 6 * p)
                        settled(sp)
                sp.nop()

            first, second, rest = moe_weights(0)
            first(0)
            sp.wait_ge(sem("un_ready"), NT)
            first(1)
            sp.wait_ge(sem("forget_ready"), NH // 2 + 4)
            second()
            for q in range(NS):
                sp.dma_start(RPD[:, q].rearrange("h g r -> g h r"), RQ).then_inc(sem("rq_out"), 16)
            for j in range(NT):
                lo, n = CONST["ones"][0], min(P, TP - j * P)
                sp.dma_start(QTD[:, DH, j * P:j * P + n], C[0:NH, lo:lo + n]).then_inc(sem("rq_out"), 16)
            sp.wait_ge(sem("u_ready"), NT)
            sp.dma_start(O["pool_state_prompt"][0, 0], U[4][LASTP - STATE:LASTP, :]).then_inc(sem("state_out"), 16)
            for b in range(NB):
                sp.dma_start(O["pool_state_sample"][0, b, STATE - NS:STATE, :], U[4][S0 + NS * b:S0 + NS * b + NS, :])\
                    .then_inc(sem("state_out"), 16)
            rest()
            moe_general(0)
            for which, done in ((0, "gate"), (1, "up"), (2, "down"), (3, "gate"), (4, "up"), (5, "down")):
                sp.wait_ge(sem(f"{done}_done"), NE - 1 if which < 3 else NE)
                if which == 4:
                    sp.wait_ge(sem("h_sum"), 1)
                src = wkvf[:, :, 512 * which:512 * which + 512] if which < 4 else wq[:, :, 512 * (which - 4):512 * (which - 3)]
                sp.dma_start(W[:, which, :].rearrange("p (k n) -> p k n", k=KC), src)\
                    .then_inc(sem(f"proj_in_{'kvq'[which // 2]}"), 16)

            def load_chunk(dst, rows, i, ch, s):
                for g in range(CH):
                    page = sp.value_load(pt[0:1, bass.ds(i * PAGES + ch * CH + g, 1)], min_val=0,
                                         max_val=A["cache_k"].shape[0] - 1)
                    sp.dma_start(dst[:, g * D:(g + 1) * D], rows[bass.ds(page * PAGE, PAGE), :]).then_inc(s, 16)

            def load_bias(i, half):
                for a in range(4):
                    src = RPD[4 * a:4 * a + 4, :, 8 * half + PAGES * i:8 * half + PAGES * i + 8, :] if isinstance(i, int) else \
                        RPD[4 * a:4 * a + 4, :, bass.ds(PAGES * i + 8 * half, 8), :]
                    sp.dma_start(BIAS[32 * a:32 * a + 16, D * half:D * half + D], src.rearrange("h q g r -> (h q) (g r)"))\
                        .then_inc(sem(f"bias_in{half}"), 16)

            sp.wait_ge(sem("zeros"), 3)
            for half in range(2):
                load_bias(0, half)
            sp.wait_ge(sem("h_sum"), NT)
            sp.wait_ge(sem("small_in"), 16 * SMALL)
            load_chunk(KB[:, 0, :], k_rows, 0, 0, sem("k_in0"))
            sp.wait_ge(sem("q_mm"), NT)
            load_chunk(VSL[0], v_rows, 0, 0, sem("v_in0"))
            sp.wait_ge(sem("merged"), 3)
            sp.wait_ge(sem("ct_mm"), 2)
            sp.wait_ge(sem("ct_out"), 16)
            load_chunk(KB[:, 1, :], k_rows, 0, 1, sem("k_in1"))

            def attention_loads(i, last):
                if not (isinstance(i, int) and i == 0):
                    sp.wait_ge(sem("s_ready"), 4 * i)
                    settled(sp)
                    load_bias(i, 1)
                for ch in range(NCH):
                    sp.wait_ge(sem("kt_tr"), 32 * i + 8 * (ch + 1))
                    settled(sp)
                    if ch < 2:
                        load_chunk(KB[:, ch, :], k_rows, i, ch + 2, sem(f"k_in{ch}"))
                    elif not last:
                        load_chunk(KB[:, ch - 2, :], k_rows, i + 1, ch - 2, sem(f"k_in{ch - 2}"))
                    else:
                        h = ch - 2
                        sp.dma_start(KB[:, h, :].rearrange("p (k n) -> p k n", k=HP), wo[:, :, 512 * h:512 * h + 512])\
                            .then_inc(sem(f"wo_in{h}"), 16)
                    after(sp, sem("pv_done"), NCH * (i - 1) + ch + 1)
                    settled(sp)
                    if not (isinstance(i, int) and i == 0 and ch < 2):
                        load_chunk(VSL[ch], v_rows, i, ch, sem(f"v_in{ch}"))
                    if ch == 1 and not last:
                        sp.wait_ge(sem("s_ready"), 4 * i + 2)
                        settled(sp)
                        load_bias(i + 1, 0)

            load_chunk(VSL[1], v_rows, 0, 1, sem("v_in1"))
            sp.wait_ge(sem("qts_ready"), NT)
            sp.wait_ge(sem("ktd_out"), 32 * NT)
            sp.wait_ge(sem("qtd_out"), 32 * NT)
            sp.wait_ge(sem("kout"), 16 * (NT + 1))
            sp.wait_ge(sem("vout"), 16 * NT)
            attention_loads(0, False)
            with sp.Fori(1, NB - 1) as i:
                attention_loads(i, False)
            attention_loads(NB - 1, True)
            first, second, rest = moe_weights(1)
            sp.wait_ge(sem("pv_done"), NCH * NB - 2)
            second()
            sp.wait_ge(sem("ots_ready"), 2 * NB)
            sp.wait_ge(sem("pu_ot"), 10 * NB)
            first(0)
            sp.wait_ge(sem("wo_done"), NT)
            first(1)
            rest()
            moe_general(1)
            for t in range(NT):
                sp.wait_ge(sem("h_sum"), NT + t + 1)
                if t == 0:
                    put_out(sp, O["y_prompt"][0, 0:P - META, :], H[META:P, 0, :])
                elif t < 4:
                    put_out(sp, O["y_prompt"][0, t * P - META:(t + 1) * P - META, :], H[:, t, :])
                else:
                    put_out(sp, O["y_prompt"][0, 4 * P - META:SEQ, :], H[0:LASTP, 4, :])
                    put_out(sp, O["y_sample"].rearrange("b s d -> (b s) d"), H[S0:64, 4, :])

        @block.gpsimd
        def _(pool):
            pool.memset(H[0:64, 4, :], 0.0).then_inc(sem("zeros"), 1)
            pool.memset(zeros, 0).then_inc(sem("zeros"), 1)
            pool.dma_start(ptc[:, :], A["page_table"].rearrange("b (g a) -> (b g) a", a=1)).then_inc(sem("ptc_in"), 16)
            pool.dma_start(ids[:, :], A["ids"]).then_inc(sem("ptc_in"), 16)
            pool.wait_ge(sem("ptc_in"), 32)
            pool.indirect_dma_start(out=W[:, 5, 0:2 * D], out_offset=None,
                                    in_=A["cache_logf"].rearrange("n r h -> n (r h)"),
                                    in_offset=bass.IndirectOffsetOnAxis(ap=ptc[:, 0:1], axis=0)).then_inc(sem("ptc_in"), 16)
            pool.wait_ge(sem("zeros"), 2)
            for l in range(2):
                pool.dma_start(LIST[l].rearrange("(p n) o -> p (n o)", p=P), zeros).then_inc(sem("list_zero"), 16)

            def moe(l):
                for j in range(2):
                    pool.wait_ge(sem(f"xs_out_{j}"), (48 - 16 * j) * (l + 1))
                pool.wait_ge(sem("slots_ready"), 1 + l * 2)

                def gather(e, j):
                    if isinstance(e, int):
                        after(pool, sem("xt_tr"), e - 1 + l * NE)
                        settled(pool)
                        pool.indirect_dma_start(out=XG[j], out_offset=None, in_=XS,
                                                in_offset=bass.IndirectOffsetOnAxis(ap=IDX[:, e:e + 1], axis=0))\
                            .then_inc(sem(f"xg_in_{j}"), 16)
                        return
                    after(pool, sem("xt_tr"), e - 1 + l * NE)
                    settled(pool)
                    pool.tensor_copy(idc[:, j:j + 1], IDX[:, bass.ds(e, 1)]).then_inc(sem("idc_ready"), 1)
                    pool.wait_ge(sem("idc_ready"), e - 1 + l * (NE - 2))
                    settled(pool)
                    pool.indirect_dma_start(out=XG[j], out_offset=None, in_=XS,
                                            in_offset=bass.IndirectOffsetOnAxis(ap=idc[:, j:j + 1], axis=0))\
                        .then_inc(sem(f"xg_in_{j}"), 16)

                gather(0, 0)
                gather(1, 1)
                pool.wait_ge(sem("slots_ready"), 2 + l * 2)
                for ch in range(2):
                    for t in range(NT):
                        r = ROWS[t]
                        pool.indirect_dma_start(out=LIST[l], out_offset=bass.IndirectOffsetOnAxis(ap=SSi[0:r, ch, t:t + 1], axis=0),
                                                in_=ids[0:r, t:t + 1], in_offset=None).then_inc(sem("scattered"), 16)
                with pool.Fori(2, NE - 1, 2) as e:
                    for j in range(2):
                        gather(e + j, j)
                pool.wait_ge(sem("np_ready"), 1 + l * 1)
                npass = pool.value_load(npi[0:1, 0:1], min_val=1, max_val=RANKS // P)
                with pool.If(npass > 1):
                    with pool.Fori(1, npass) as p:
                        with pool.Fori(0, NE) as e:
                            pool.wait_ge(sem(f"g_in{l}"), 64 * (p * NE + e - NE + 1))
                            settled(pool)
                            pool.indirect_dma_start(out=XG[0], out_offset=None, in_=XS,
                                                    in_offset=bass.IndirectOffsetOnAxis(ap=idg[:, 0:1], axis=0))\
                                .then_inc(sem(f"g_xg{l}"), 16)
                            pool.wait_ge(sem(f"g_y_out{l}"), 16 * (p * NE + e - NE + 1))
                            settled(pool)
                        for t in range(NT):
                            r = ROWS[t]
                            pool.wait_ge(sem(f"g_sum{l}"), 6 * p + t - 5)
                            settled(pool)
                            for ch in range(2):
                                pool.indirect_dma_start(out=K8[0:r, ch, :], out_offset=None, in_=YG[l],
                                                        in_offset=bass.IndirectOffsetOnAxis(ap=SGi[0:r, ch, t:t + 1], axis=0))\
                                    .then_inc(sem(f"g_yg{l}"), 16)
                        pool.wait_ge(sem(f"g_sum{l}"), 6 * p)
                        settled(pool)
                    pool.nop()
                pool.wait_ge(sem("scattered"), 16 * 2 * NT + l * (32 * NT))
                for j in range(2):
                    pool.wait_ge(sem(f"y_out_{j}"), 16 * NE // 2 + l * (8 * NE))
                if l == 0:
                    pool.wait_ge(sem("state_out"), 16 * (NB + 1))
                for t in range(NT):
                    r = ROWS[t]
                    for ch in range(2):
                        buf = (2 * t + ch) % 8
                        if t == 4:
                            pool.wait_ge(sem("h_sum"), 1 + l * NT)
                        pool.indirect_dma_start(out=K8[0:r, buf, :], out_offset=None, in_=YD[l],
                                                in_offset=bass.IndirectOffsetOnAxis(ap=SLi[0:r, ch, t:t + 1], axis=0))\
                            .then_inc(sem(f"yg_in_{t}"), 16)

            moe(0)
            pool.wait_ge(sem("rq_out"), 16 * (NS + NT))
            pool.memset(BIAS[:, :], 0.0).then_inc(sem("zeros"), 1)

            def stage(i, hh):
                if not (isinstance(i, int) and i == 0):
                    pool.wait_ge(sem("pu_v"), 10 * i - 5 + 5 * hh)
                    settled(pool)
                for dst, src in ((QST, QTD), (KST, KTD)):
                    s = src[2 * i + hh] if isinstance(i, int) else src[bass.ds(2 * i + hh, 1)].rearrange("a d t -> (a d) t")
                    pool.dma_start(dst[hh][0:DH + 1, :], s).then_inc(sem(f"st_in{hh}"), 16)
                cols = slice(P * i + DH * hh, P * i + DH * hh + DH) if isinstance(i, int) else bass.ds(P * i + DH * hh, DH)
                own = slice(DH * hh, DH * hh + DH)
                pool.dma_start(VST[:, 0:4, own], vp_out[0:4 * P, cols].rearrange("(t p) n -> p t n", p=P)).then_inc(sem(f"st_in{hh}"), 16)
                pool.dma_start(VST[0:LASTP, 4, own], vp_out[4 * P:TP, cols]).then_inc(sem(f"st_in{hh}"), 16)

            pool.wait_ge(sem("ct_out"), 16)
            pool.wait_ge(sem("ktd_out"), 32 * NT)
            pool.wait_ge(sem("qtd_out"), 32 * NT)
            pool.wait_ge(sem("vout"), 16 * NT)
            for hh in range(2):
                stage(0, hh)
            with pool.Fori(1, HP) as i:
                for hh in range(2):
                    stage(i, hh)
            moe(1)
            pool.wait_ge(sem("kout"), 16 * (NT + 1))
            pool.wait_ge(sem("vout"), 16 * NT)
            pool.wait_ge(sem("state_out"), 16 * (NB + 1))
            pool.wait_ge(sem("out_done"), 16 * OUTS)
            pool.nop()

        @block.tensor
        def _(pe):
            def forget_sums(part):
                if part == 0:
                    pe.wait_ge(sem("ptc_in"), 48)
                    lo = CONST["ident"][0]
                    both = C[:, lo:lo + 2 * P]
                    for h in range(NH):
                        if h >= 4 and h % 2 == 0:
                            pe.wait_ge(sem("forget_ready"), h // 2 - 1)
                        mm = pe.matmul(PS[:, h // 2 % 2, 256 * (h % 2):256 * (h % 2) + 256], LP[:, :, h], both,
                                       start=True, stop=True)
                        if h % 2:
                            mm.then_inc(sem("forget_tr"), 1)
                else:
                    if part == 1:
                        pe.wait_ge(sem("forget_ready"), NH // 2)
                    for n in (0, 1) if part == 1 else (2, 3):
                        if n >= 2:
                            pe.wait_ge(sem("forget_ready"), NH // 2 + n - 1)
                        for h in range(4 * n, 4 * n + 4):
                            out = PS[:, 2 + n % 2, (h % 4) * P:(h % 4) * P + P]
                            pe.matmul(out, TT[:, h, 0:P], c("after"), start=True, stop=False)
                            mm = pe.matmul(out, TT[:, h, P:2 * P], c("ones"), start=False, stop=True)
                        mm.then_inc(sem("forget_mm"), 1)

            def bandv(name, g):
                lo, hi, n = BAND[name]
                return bands[:, lo + g * n:lo + (g + 1) * n]

            def pool_sums(t):
                r = ROWS[t]
                pe.wait_ge(sem("u_ready"), t + 1)
                after(pe, sem("dt_ready"), 2 * t)
                for k in range(8):
                    g = k // 2
                    cs = slice(k * P, k * P + P)
                    out = PS[:, k // 4, (k % 4) * P:(k % 4) * P + r]
                    if t == 4:
                        if k == 0:
                            pe.wait_ge(sem("tile_in_4"), 48)
                        pe.matmul(out, U[3][:, cs], bandv("prev4", g), start=True, stop=False)
                        pe.matmul(out, ST[0:NB * STATE, cs], bandv("state", g)[0:NB * STATE], start=False, stop=False)
                        mm = pe.matmul(out, U[4][0:64, cs], bandv("cur4", g)[0:64], start=False, stop=True)
                    else:
                        if t:
                            pe.matmul(out, U[t - 1][:, cs], bandv("prev", g), start=True, stop=False)
                        mm = pe.matmul(out, U[t][:, cs], bandv("cur" if t else "cur0", g), start=(t == 0), stop=True)
                mm.then_inc(sem("dt_mm"), 1)

            def pool_mix(t):
                r = ROWS[t]
                if t == 0:
                    pe.wait_ge(sem("ws_ready"), 1)
                pe.wait_ge(sem("dt_ready"), 2 * t + 2)
                after(pe, sem("h_pool"), t)
                for g in range(NG):
                    for cc in range(2):
                        mm = pe.matmul(PS[0:r, 2 + g // 2, 256 * (g % 2):256 * (g % 2) + 256],
                                       DT[t % 2][:, 2 * g + cc, 0:r], pw[:, g, cc, :], start=(cc == 0), stop=(cc == 1))
                mm.then_inc(sem("pool_mm"), 1)

            def transposes(src, bank, r, step):
                for k in range(KC):
                    s = src[0:r, :].rearrange("p (n k) -> p k n", k=KC)[:, k, :] if step > 1 else src[0:r, k * P:(k + 1) * P]
                    mm = pe.transpose(PS[:, bank + k // 4, (k % 4) * P:(k % 4) * P + r], s, ident[0:r, 0:r])
                return mm

            def router_tr(l, t):
                if t == 0 and l == 0:
                    pe.wait_ge(sem("consts_in"), 16)
                pe.wait_ge(sem("un_ready"), t + 1 + l * NT)
                after(pe, sem("xu_ready"), t + l * NT)
                transposes(UR[t % 2], 4, ROWS[t], KC).then_inc(sem("un_tr"), 1)

            def router_mm(l, t):
                r = ROWS[t]
                pe.wait_ge(sem("xu_ready"), t + 1 + l * NT)
                if t == 0 and l == 0:
                    pe.wait_ge(sem("small_in"), 16 * SMALL)
                for k in range(KC):
                    mm = pe.matmul(PS[0:r, 6, 20 * t:20 * t + 20], XU[t % 2][:, k, 0:r], wr[:, l, k, :],
                                   start=(k == 0), stop=(k == KC - 1))
                mm.then_inc(sem("router_done"), 1)

            def places(l):
                if l == 0:
                    forget_sums(0)
                pe.wait_ge(sem("picks_ready"), 1 + l * 2)
                pe.matmul(PS[:, 7, 0:(NT + 1) * NE], c("before"), rt["A"], start=True, stop=True)
                for d in range(1, NT + 1):
                    mm = pe.matmul(PS[:, 7, d * NE:(NT + 1) * NE], c("ones"), rt["A"][:, 0:(NT + 1 - d) * NE], start=False,
                                   stop=True, skip_group_check=True)
                mm.then_inc(sem("ranks"), 1)
                if l == 0:
                    forget_sums(1)
                pe.wait_ge(sem("picks_ready"), 2 + l * 2)
                for x in range(2 * NT):
                    r = ROWS[x % NT]
                    mm = pe.matmul(PS[:, 6, P:P + NE], PLACE[0:r, x, :], rt["hid"][0:r, x * NE:x * NE + NE],
                                   start=(x == 0), stop=(x == 2 * NT - 1))
                mm.then_inc(sem("ranks"), 1)
                if l == 0:
                    forget_sums(2)
                    pe.wait_ge(sem("forget_ready"), NH // 2 + 4)

            def moe(l):
                def x_tr(e, j):
                    k = 8 * e + 16 - 8 * j
                    pe.wait_ge(sem(f"xg_in_{j}"), k + l * (8 * NE))
                    after(pe, sem("xt_ready"), e + l * NE)
                    transposes(XG[j], 0, P, KC).then_inc(sem("xt_tr"), 1)

                def product(bank, slot, count, name):
                    pe.wait_ge(sem(f"w_in_{slot}"), count + l * (8 * NE))
                    w = W[:, slot, :].rearrange("p (k n) -> p k n", k=KC)
                    for k in range(KC):
                        mm = pe.matmul(PS[:, bank, :], XT[:, k, :], w[:, k, :], start=(k == 0), stop=(k == KC - 1))
                    mm.then_inc(sem(f"{name}_done"), 1)

                def h_tr(e):
                    pe.wait_ge(sem("h_ready"), e + 1 + l * NE)
                    after(pe, sem("ht_ready"), e + l * NE)
                    for f in range(FC):
                        mm = pe.transpose(PS[:, 4, f * P:(f + 1) * P], HH.rearrange("p (n f) -> p f n", f=FC)[:, f, :], ident)
                    mm.then_inc(sem("ht_tr"), 1)

                def down(e, j):
                    pe.wait_ge(sem("ht_ready"), e + 1 + l * NE)
                    pe.wait_ge(sem(f"w_in_{3 * j + 2}"), 8 * e + 16 - 8 * j + l * (8 * NE))
                    after(pe, sem("y_ready"), e + l * NE)
                    w = W[:, 3 * j + 2, :].rearrange("p (f n) -> p f n", f=FC)
                    for n in range(2):
                        for f in range(FC):
                            mm = pe.matmul(PS[:, 5 + n, :], HT[:, f, :], w[:, f, n * 512:(n + 1) * 512],
                                           start=(f == 0), stop=(f == FC - 1))
                    mm.then_inc(sem("down_done"), 1)

                def expert(e, j, last=False):
                    count = 8 * e + 16 - 8 * j
                    first = isinstance(e, int) and e == 0
                    pe.wait_ge(sem("xt_ready"), e + 1 + l * NE)
                    after(pe, sem("silu_done"), e + l * NE)
                    product(2, 3 * j, count, "gate")
                    if not first:
                        h_tr(e - 1)
                    product(3, 3 * j + 1, count, "up")
                    if not last:
                        x_tr(e + 1, 1 - j)
                    if not first:
                        down(e - 1, 1 - j)

                x_tr(0, 0)
                expert(0, 0)
                expert(1, 1)
                with pe.Fori(2, NE - 3, 2) as e:
                    expert(e, 0)
                    expert(e + 1, 1)
                expert(NE - 2, 0)
                expert(NE - 1, 1, last=True)
                h_tr(NE - 1)
                down(NE - 1, 1)

                pe.wait_ge(sem("np_ready"), 1 + l * 1)
                npass = pe.value_load(npi[0:1, 0:1], min_val=1, max_val=RANKS // P)
                with pe.If(npass > 1):
                    with pe.Fori(1, npass) as p:
                        with pe.Fori(0, NE) as e:
                            n = p * NE + e - NE
                            pe.wait_ge(sem(f"g_in{l}"), 64 * (n + 1))
                            pe.wait_ge(sem(f"g_xg{l}"), 16 * (n + 1))
                            transposes(XG[0], 0, P, KC).then_inc(sem(f"g_step{l}"), 1)
                            pe.wait_ge(sem(f"g_step{l}"), 9 * n + 2)
                            for which in range(2):
                                w = W[:, which, :].rearrange("p (k n) -> p k n", k=KC)
                                for k in range(KC):
                                    mm = pe.matmul(PS[:, 2 + which, :], XT[:, k, :], w[:, k, :], start=(k == 0), stop=(k == KC - 1))
                            mm.then_inc(sem(f"g_step{l}"), 1)
                            pe.wait_ge(sem(f"g_step{l}"), 9 * n + 5)
                            for f in range(FC):
                                mm = pe.transpose(PS[:, 4, f * P:(f + 1) * P], HH.rearrange("p (n f) -> p f n", f=FC)[:, f, :], ident)
                            mm.then_inc(sem(f"g_step{l}"), 1)
                            pe.wait_ge(sem(f"g_step{l}"), 9 * n + 7)
                            w = W[:, 2, :].rearrange("p (f n) -> p f n", f=FC)
                            for nn in range(2):
                                for f in range(FC):
                                    mm = pe.matmul(PS[:, 5 + nn, :], HT[:, f, :], w[:, f, nn * 512:(nn + 1) * 512],
                                                   start=(f == 0), stop=(f == FC - 1))
                            mm.then_inc(sem(f"g_step{l}"), 1)
                pe.nop()

            for t in range(NT + 1):
                if t < NT:
                    if t == 0:
                        pe.wait_ge(sem("pool_in"), 32)
                    pool_sums(t)
                if t:
                    router_tr(0, t - 1)
                if t < NT:
                    pool_mix(t)
                if t:
                    router_mm(0, t - 1)
            places(0)
            moe(0)

            wv = [W[:, s, :].rearrange("p (k n) -> p k n", k=KC) for s in range(6)]
            def project(t, x, banks, slots, done=None):
                r = ROWS[t]
                for b, s in zip(banks, slots):
                    for k in range(KC) if t < 4 else (0, 4, 1, 5, 2, 6, 3, 7):
                        if t < 4:
                            mm = pe.matmul(PS[0:r, b, :], x[:, k, 0:r], wv[s][:, k, :], start=(k == 0), stop=(k == KC - 1))
                        else:
                            up = 64 * (k // 4)
                            mm = pe.matmul(PS[up:up + 64, b, :], x[:, k, 0:r], wv[s][:, k, :], start=(k % 4 == 0),
                                           stop=(k % 4 == 3), tile_position=(0, up), skip_group_check=True)
                if done:
                    mm.then_inc(sem(done), 1)

            for t in range(NT):
                r = ROWS[t]
                x, y = UK[t % 2], UQ[t % 2]
                if t == 0:
                    pe.wait_ge(sem("pun_ready"), 1)
                    transposes(UN, 0, r, KC).then_inc(sem("pun_tr"), 1)
                    pe.wait_ge(sem("proj_in_k"), 32)
                pe.wait_ge(sem("ux_ready"), 2 * t + 1)
                after(pe, sem("kn_ready"), 2 * t)
                project(t, x, (2, 3), (0, 1), "k_mm")
                after(pe, sem("qn_ready"), t)
                for k in range(KC):
                    mm = pe.matmul(PS[0:r, 6, 0:NH], x[:, k, 0:r], wf[:, k, :], start=(k == 0), stop=(k == KC - 1))
                mm.then_inc(sem("f_mm"), 1)
                pe.wait_ge(sem("ux_ready"), 2 * t + 2)
                if t:
                    transposes(QN, 0, ROWS[t - 1], 1).then_inc(sem("qn_tr"), 1)
                if t == 0:
                    pe.wait_ge(sem("proj_in_v"), 32)
                if t == NT - 1:
                    pe.wait_ge(sem("f_ready"), NT)
                    project(t, y, (6, 7), (4, 5), "q_mm")
                after(pe, sem("vn_ready"), t)
                project(t, x, (4,), (2,))
                if t == NT - 1:
                    pe.wait_ge(sem("lf_step"), 5)
                    pe.wait_ge(sem("new_rows"), 1)
                    pe.wait_ge(sem("kn_ready"), 2 * NT)
                    for t1 in range(NT):
                        n = P if t1 < 4 else LASTP
                        out = PS[0:NH, 2 + t1 // 4, (t1 % 4) * P:(t1 % 4) * P + n]
                        for t2 in range(t1):
                            pe.matmul(out, LF[:, t2, :], c("ones")[:, 0:n], start=(t2 == 0), stop=False)
                        mm = pe.matmul(out, LF[0:n, t1, :], c("upto")[0:n, 0:n], start=(t1 == 0), stop=True)
                    mm.then_inc(sem("ct_mm"), 1)
                    pe.matmul(PS[:, 3, P:P + 64], LR[0:64, :], c("negnew", 64), start=True, stop=True).then_inc(sem("ct_mm"), 1)
                project(t, x, (5,), (3,), "v_mm")
                pe.wait_ge(sem("kn_ready"), 2 * t + 2)
                after(pe, sem("qts_ready"), t)
                transposes(KN, 0, r, 1).then_inc(sem("kn_tr"), 1)
                if t == NT - 1:
                    break
                if t == 0:
                    pe.wait_ge(sem("proj_in_q"), 32)
                pe.wait_ge(sem("f_ready"), t + 1)
                project(t, y, (6,), (4,))
                pe.wait_ge(sem("pun_ready"), t + 2)
                pe.wait_ge(sem("kts_ready"), t + 1)
                transposes(UN, 0, ROWS[t + 1], KC).then_inc(sem("pun_tr"), 1)
                project(t, y, (7,), (5,), "q_mm")
            pe.wait_ge(sem("qn_ready"), NT)
            pe.wait_ge(sem("kts_ready"), NT)
            transposes(QN, 0, ROWS[NT - 1], 1).then_inc(sem("qn_tr"), 1)
            pe.wait_ge(sem("qts_ready"), NT)
            pe.wait_ge(sem("ct_ready"), 2)
            pe.wait_ge(sem("new_rows"), 2)

            def attention(i, front=True, back=True, shift=0):
                def s_step(u):
                    hh, t = u // 5, u % 5
                    r = P if t < 4 else LASTP
                    nk = P * (t + 1) if t < 4 else 4 * P
                    if t == 0:
                        pe.wait_ge(sem(f"st_in{hh}"), 64 * (i + 1))
                    after(pe, sem("pu_exp"), 10 * i + u)
                    pe.matmul(PS[0:r, 6, 0:nk], QST[hh][0:DH + 1, t * P:t * P + r], KST[hh][0:DH + 1, 0:nk],
                              start=True, stop=True)
                    if t < 4:
                        mm = pe.matmul(PS[:, 6, t * P:t * P + P], ident, c("causal"), start=False, stop=True, skip_group_check=True)
                    else:
                        if back:
                            pe.wait_ge(sem("ptt_ready"), 5 * i - 5 + (4 if u == 4 else 5))
                        pe.matmul(PS[0:r, 4, 0:r], QST[hh][0:DH + 1, t * P:t * P + r], KST[hh][0:DH + 1, nk:TP],
                                  start=True, stop=False)
                        mm = pe.matmul(PS[0:r, 4, 0:r], ident[0:r, 0:r], c("causal")[0:r, 0:r], start=False, stop=True)
                    mm.then_inc(sem("pu_s"), 1)

                def t_step(u):
                    t = u % 5
                    pe.wait_ge(sem("pu_norm"), 10 * i + u + 1)
                    after(pe, sem("pu_pts"), 10 * i + u)
                    if t < 4:
                        for j in range(t + 1):
                            mm = pe.transpose(PS[:, 7, j * P:(j + 1) * P], PR[:, j * P:(j + 1) * P], ident)
                    else:
                        settled(pe)
                        r = LASTP
                        for j in range(4):
                            pe.transpose(PS[:, 7, j * r:(j + 1) * r], PR[0:r, j * P:(j + 1) * P], ident[0:r, 0:r])
                        mm = pe.transpose(PS[0:r, 7, 4 * r:5 * r], PR[0:r, 4 * P:TP], ident[0:r, 0:r])
                    mm.then_inc(sem("pu_t"), 1)

                def v_step(u):
                    hh, t = u // 5, u % 5
                    pe.wait_ge(sem("pu_pts"), 10 * i + u + 1)
                    after(pe, sem("pu_ot"), 10 * i + u)
                    r = P if t < 4 else LASTP
                    vc = slice(DH * hh, DH * hh + DH)
                    out = PS[DH * hh:DH * hh + DH, 3, 0:r]
                    for j in range(t + 1):
                        kr = P if j < 4 else LASTP
                        mm = pe.matmul(out, VST[0:kr, j, vc], PTS[0:kr, j * r:(j + 1) * r], start=(j == 0), stop=(j == t),
                                       tile_position=(0, DH * hh))
                    mm.then_inc(sem("pu_v"), 1)

                def k_tick(n):
                    ch, half, j, m = n // 8, n // 4 % 2, n // 2 % 2, n % 2
                    if n % 8 == 0:
                        pe.wait_ge(sem(f"k_in{ch % 2}"), 64 * (2 * i + ch // 2 + 1))
                    after(pe, sem("kt_even" if n % 2 == 0 else "kt_odd"), 16 * i + n // 2)
                    ks = paged(KB[:, ch % 2, :])
                    for x in range(2):
                        hp = 4 * m + 2 * x + j
                        for g in range(2):
                            mm = pe.transpose(PS[:, n % 2, (2 * x + g) * P:(2 * x + g + 1) * P],
                                              ks[:, 2 * half + g, hp * P:(hp + 1) * P], ident)
                    mm.then_inc(sem("kt_tr"), 1)

                def qk(x):
                    ch, half, j = x // 4, x // 2 % 2, x % 2
                    pe.wait_ge(sem("kt_even"), 16 * i + x + 1)
                    pe.wait_ge(sem("kt_odd"), 16 * i + x + 1)
                    if x == 0:
                        pe.wait_ge(sem("qb_ready"), i + 1)
                    if x % 4 == 0:
                        if ch == 2:
                            pe.wait_ge(sem("sn_ready"), i + 1)
                        else:
                            after(pe, sem("s_ready"), 4 * i + ch)
                    for a in range(4):
                        mm = pe.matmul(PS[32 * a:32 * a + 32, 2, 256 * half:256 * half + 256], QBLK[:, 2 * a + j, :],
                                       KTR[:, (2 * x + a // 2) % 4, 256 * (a % 2):256 * (a % 2) + 256],
                                       start=(j == 0), stop=(j == 1), tile_position=(0, 32 * a), skip_group_check=True)
                    mm.then_inc(sem("qk_done"), 1)

                def new_keys():
                    pe.wait_ge(sem("s_ready"), 4 * i + 2)
                    for j in range(2):
                        for a in range(4):
                            mm = pe.matmul(PS[32 * a:32 * a + 32, 2, 0:64], QBLK[:, 2 * a + j, :], KT4[:, 2 * a + j, :],
                                           start=(j == 0), stop=(j == 1), tile_position=(0, 32 * a), skip_group_check=True)
                    mm.then_inc(sem("sn_mm"), 1)

                def p_transposes(part):
                    if part == 0:
                        pe.wait_ge(sem("sp_exp"), i)
                    after(pe, sem("ptt_ready"), 5 * i - 5 + part)
                    if front and part == NCH:
                        pe.wait_ge(sem("pu_exp"), 10 * i + 5)
                    elif front and part == 0:
                        pe.wait_ge(sem("pu_exp"), 10 * i)
                    if part == NCH:
                        settled(pe)
                        mm = pe.transpose(PS[0:64, 4, 0:P], SROW[:, PAGES * PAGE:PAGES * PAGE + 64], ident)
                    else:
                        for g in range(CH):
                            at = (CH * part + g) * PAGE
                            mm = pe.transpose(PS[:, 4, g * P:(g + 1) * P], SROW[:, at:at + PAGE], ident)
                    mm.then_inc(sem("ptt_tr"), 1)

                def values(g):
                    ch = g // CH
                    if g == 0:
                        after(pe, sem("ots_ready"), 2 * i - 2)
                    if g % CH == 0:
                        pe.wait_ge(sem("ptt_ready"), 5 * i - 5 + ch + 1)
                        if ch < NCH:
                            pe.wait_ge(sem(f"v_in{ch}"), 64 * i)
                        else:
                            settled(pe)
                    nn = P if g < PAGES else 64
                    for q in range(4):
                        v = paged(VSL[ch])[:, g % CH, 256 * q:256 * q + 256] if ch < NCH else V4[0:64, 256 * q:256 * q + 256]
                        mm = pe.matmul(PS[32 * q:32 * q + 32, 5, 0:256], PTT[0:nn, g, 32 * q:32 * q + 32], v,
                                       start=(g == 0), stop=(g == PAGES), tile_position=(0, 32 * q), skip_group_check=True)
                    if g == PAGES:
                        mm.then_inc(sem("o_mm"), 1)
                    elif g % CH == CH - 1:
                        mm.then_inc(sem("pv_done"), 1)

                for n in range(TICKS + shift):
                    m = n - shift
                    if front:
                        if n < KTICKS:
                            k_tick(n)
                        if n in QK_TICK:
                            qk(QK_TICK.index(n))
                        if n == NEW_TICK:
                            new_keys()
                        if m in V_TICK:
                            v_step(V_TICK.index(m))
                        if m in T_TICK:
                            t_step(T_TICK.index(m))
                        if m in S_TICK:
                            s_step(S_TICK.index(m))
                    if back:
                        if n in P_TICK:
                            p_transposes(P_TICK.index(n))
                        if n in O_TICK:
                            values(O_TICK.index(n))
                        if n == OT_TICK:
                            pe.wait_ge(sem("ob_ready"), i)
                            for x in range(2):
                                mm = pe.transpose(PS[:, 5, 256 + x * P:256 + (x + 1) * P], OB[:, x * P:(x + 1) * P], ident)
                            mm.then_inc(sem("ob_tr"), 1)

            attention(0, back=False, shift=SHIFT)
            with pe.Fori(1, NB) as i:
                attention(i)

            def project_out(t):
                r = ROWS[t]
                if t >= 2:
                    pe.wait_ge(sem("h_attn"), t - 1)
                for n in range(2):
                    if t == 0:
                        pe.wait_ge(sem(f"wo_in{n}"), 16)
                    w = KB[:, n, :].rearrange("p (k n) -> p k n", k=HP)
                    for k in range(HP) if t < 4 else (0, 4, 1, 5, 2, 6, 3, 7):
                        if t < 4:
                            mm = pe.matmul(PS[0:r, 2 * (t % 2) + n, :], OTS[:, k, t * P:t * P + r], w[:, k, :],
                                           start=(k == 0), stop=(k == HP - 1))
                        else:
                            up = 64 * (k // 4)
                            mm = pe.matmul(PS[up:up + 64, n, :], OTS[:, k, t * P:t * P + r], w[:, k, :],
                                           start=(k % 4 == 0), stop=(k % 4 == 3), tile_position=(0, up), skip_group_check=True)
                mm.then_inc(sem("wo_done"), 1)

            pe.wait_ge(sem("pu_ot"), 10 * NB)
            project_out(0)
            attention(NB, front=False)
            pe.wait_ge(sem("s_ready"), NCH * NB)
            project_out(1)
            pe.wait_ge(sem("ots_ready"), 2 * NB)
            for t in range(2, NT + 2):
                if t < NT:
                    project_out(t)
                if t > 2:
                    router_mm(1, t - 3)
                router_tr(1, t - 2)
            router_mm(1, NT - 1)
            places(1)
            moe(1)

        @block.scalar
        def _(act):
            def norm(phase, t, scratch):
                r, n = ROWS[t], NORMS.index((phase, t))
                act.activation(scratch[0:r, :], H[0:r, t, :], ACT.Square, accum_out=ss[0:r, t:t + 1]).then_inc(sem("sq"), 1)
                act.wait_ge(sem("row_ms"), n + 1)
                act.activation(sd[0:r, t:t + 1], ms[0:r, t:t + 1], ACT.Sqrt).then_inc(sem("row_sd"), 1)

            def pool_norm(t):
                act.wait_ge(sem(f"tile_in_{t}"), (32, 16, 16, 16, 48)[t])
                norm("pool", t, U[t])

            def router_norm(l, t):
                act.wait_ge(sem("h_attn" if l else "h_pool"), t + 1)
                if l == 1 and t == 0:
                    act.wait_ge(sem("o_mm"), NB)
                if t >= 2:
                    act.wait_ge(sem("un_tr"), t - 1 + l * NT)
                    act.wait_ge(sem(f"xs_out_{t % 2}"), 16 * (t // 2) + (48 - 16 * (t % 2)) * l)
                norm(f"r{l}", t, UR[t % 2])

            def rows_out(l, t):
                r = ROWS[t]
                act.wait_ge(sem("un_ready"), t + 1 + l * NT)
                act.dma_start(XS[t * P:t * P + r, :], UR[t % 2][0:r, :]).then_inc(sem(f"xs_out_{t % 2}"), 16)

            def route(l):
                act.wait_ge(sem("rt_in"), 1 + l * 2)
                act.activation(rt["eg"], rt["dl"], ACT.Exp).then_inc(sem("rt_exp"), 1)
                act.wait_ge(sem("rt_in"), 2 + l * 2)
                act.activation(rt["ed"], rt["d"], ACT.Exp).then_inc(sem("rt_exp"), 1)

            pool_norm(0)
            for t in range(NT + 1):
                if t + 1 < NT:
                    pool_norm(t + 1)
                if t:
                    if t == 1:
                        act.wait_ge(sem("list_zero"), 32)
                    router_norm(0, t - 1)
                if t < NT:
                    r = ROWS[t]
                    act.wait_ge(sem("dt_mm"), t + 1)
                    if t >= 2:
                        act.wait_ge(sem("pool_mm"), t - 1)
                    act.activation(DT[t % 2][:, 4:8, 0:r], PS[:, 1, :].rearrange("p (k n) -> p k n", k=4)[:, :, 0:r], ACT.Copy)\
                        .then_inc(sem("dt_ready"), 1)
                if t:
                    rows_out(0, t - 1)
            for n in range(NH // 2):
                act.wait_ge(sem("forget_tr"), n + 1)
                act.activation(TT[:, 2 * n:2 * n + 2, :], PS[:, n % 2, :].rearrange("p (h m) -> p h m", h=2), ACT.Copy)\
                    .then_inc(sem("forget_ready"), 1)
            act.wait_ge(sem("router_done"), NT)
            for n in range(4):
                act.wait_ge(sem("forget_mm"), n + 1)
                act.activation(RQ[:, 4 * n:4 * n + 4, :], PS[:, 2 + n % 2, :].rearrange("p (h m) -> p h m", h=4), ACT.Copy)\
                    .then_inc(sem("forget_ready"), 1)
            route(0)

            def moe(l):
                def silu(e):
                    act.wait_ge(sem("gate_done"), e + 1 + l * NE)
                    after(act, sem("h_ready"), e + l * NE)
                    act.activation(SG, PS[:, 2, :], ACT.Silu).then_inc(sem("silu_done"), 1)

                def ht(e):
                    act.wait_ge(sem("ht_tr"), e + 1 + l * NE)
                    after(act, sem("down_done"), e + l * NE)
                    act.activation(HT.rearrange("p f n -> p (f n)"), PS[:, 4, :], ACT.Copy).then_inc(sem("ht_ready"), 1)

                def y(e, j):
                    act.wait_ge(sem("down_done"), e + 1 + l * NE)
                    after(act, sem(f"y_out_{j}"), 8 * e - 8 * j + l * (8 * NE))
                    act.activation(YS[j], PS[:, 5:7, :].rearrange("p a n -> p (a n)"), ACT.Copy).then_inc(sem("y_ready"), 1)
                    act.wait_ge(sem("y_ready"), e + 1 + l * NE)
                    settled(act)
                    rows = YD[l].rearrange("(r e) n -> e r n", e=NE)
                    dst = rows[e] if isinstance(e, int) else rows[bass.ds(e, 1)].rearrange("e r n -> (e r) n")
                    act.dma_start(dst, YS[j]).then_inc(sem(f"y_out_{j}"), 16)

                for j in range(2):
                    act.wait_ge(sem(f"xs_out_{j}"), (48 - 16 * j) * (l + 1))
                silu(0)
                silu(1)
                ht(0)
                y(0, 0)
                with act.Fori(2, NE - 1, 2) as e:
                    silu(e)
                    ht(e - 1)
                    y(e - 1, 1)
                    silu(e + 1)
                    ht(e)
                    y(e, 0)
                ht(NE - 1)
                y(NE - 1, 1)
                act.wait_ge(sem("np_ready"), 1 + l * 1)
                npass = act.value_load(npi[0:1, 0:1], min_val=1, max_val=RANKS // P)
                with act.If(npass > 1):
                    act.wait_ge(sem("y_out_0"), 16 * NE // 2 + l * (8 * NE))
                    with act.Fori(1, npass) as p:
                        with act.Fori(0, NE) as e:
                            n = p * NE + e - NE
                            act.wait_ge(sem(f"g_step{l}"), 9 * n + 3)
                            act.activation(SG, PS[:, 2, :], ACT.Silu).then_inc(sem(f"g_step{l}"), 1)
                            act.wait_ge(sem(f"g_step{l}"), 9 * n + 6)
                            act.activation(HT.rearrange("p f n -> p (f n)"), PS[:, 4, :], ACT.Copy).then_inc(sem(f"g_step{l}"), 1)
                            act.wait_ge(sem(f"g_step{l}"), 9 * n + 8)
                            act.activation(YS[0], PS[:, 5:7, :].rearrange("p a n -> p (a n)"), ACT.Copy).then_inc(sem(f"g_step{l}"), 1)
                            act.wait_ge(sem(f"g_step{l}"), 9 * n + 9)
                            settled(act)
                            rows = YG[l].rearrange("(r e) n -> e r n", e=NE)
                            act.dma_start(rows[bass.ds(e, 1)].rearrange("e r n -> (e r) n"), YS[0])\
                                .then_inc(sem(f"g_y_out{l}"), 16)
                act.nop()

            moe(0)

            act.wait_ge(sem("y_out_0"), 16 * NE // 2)
            act.wait_ge(sem("y_out_1"), 16 * NE // 2)
            def proj_norm(t):
                act.wait_ge(sem("h_sum"), t + 1)
                norm("proj", t, SQ)

            def merge(b, n):
                act.activation(UPPER[0:64, :], PS[64:128, b:b + 2, :].rearrange("p a n -> p (a n)"), ACT.Copy)\
                    .then_inc(sem("upper_ready"), 1)
                act.wait_ge(sem("merged"), n)

            def queries_squares(t):
                r = ROWS[t]
                if t == 4:
                    act.wait_ge(sem("lf_step"), 1)
                    act.activation(lfe, lfa, ACT.Exp, scale=-1.0).then_inc(sem("lf_step"), 1)
                    act.wait_ge(sem("lf_step"), 3)
                    act.activation(lfa, lfe, ACT.Ln).then_inc(sem("lf_step"), 1)
                act.wait_ge(sem("q_mm"), t + 1)
                if t == 4:
                    merge(6, 2)
                act.activation(SQ[0:r, :], PS[0:r, 6:8, :].rearrange("p a n -> p (a n)"), ACT.Square).then_inc(sem("head_sq"), 1)
                act.wait_ge(sem("head_ms"), 2 * t + 2)
                act.activation(hsd[:, 1, :], hms[:, 1, :], ACT.Sqrt).then_inc(sem("head_sd"), 1)

            def queries_out(t):
                r = ROWS[t]
                act.wait_ge(sem("qn_tr"), t + 1)
                dst = TS if t < 4 else QT4
                if t < 4:
                    act.wait_ge(sem("ktd_out"), 32 * (t + 1))
                act.activation(dst[:, :, 0:r], PS[:, 0:2, :].rearrange("p a (k n) -> p (a k) n", n=P)[:, :, 0:r], ACT.Copy,
                               scale=qg[:, 0:1]).then_inc(sem("qts_ready"), 1)
                act.wait_ge(sem("qts_ready"), t + 1)
                n = r if t < 4 else LASTP
                for hh in range(2):
                    act.dma_start(QTD[hh:NH:2, 0:DH, t * P:t * P + n].rearrange("h d t -> d h t"), dst[DH * hh:DH * hh + DH, :, 0:n])\
                        .then_inc(sem("qtd_out"), 16)

            for j in range(2):
                act.wait_ge(sem(f"y_out_{j}"), 16 * NE // 2)
            proj_norm(0)
            proj_norm(1)
            for t in range(NT):
                r = ROWS[t]
                two = lambda b: PS[0:r, b:b + 2, :].rearrange("p a n -> p (a n)")
                act.wait_ge(sem("k_mm"), t + 1)
                if t:
                    act.wait_ge(sem("ssq_ready"), t)
                if t == 4:
                    merge(2, 1)
                act.activation(SQ[0:r, :], two(2), ACT.Square).then_inc(sem("head_sq"), 1)
                act.wait_ge(sem("head_ms"), 2 * t + 1)
                act.activation(hsd[:, 0, :], hms[:, 0, :], ACT.Sqrt).then_inc(sem("head_sd"), 1)
                act.wait_ge(sem("kn_ready"), 2 * t + 2)
                act.dma_start(kp_out[t * P:t * P + min(P, TP - t * P), :], KN[0:min(r, TP - t * P), :]).then_inc(sem("kout"), 16)
                if t == 4:
                    act.dma_start(ks_out, KN[S0:64, :]).then_inc(sem("kout"), 16)
                if t:
                    queries_out(t - 1)
                if t == NT - 1:
                    queries_squares(t)
                    act.wait_ge(sem("ct_mm"), 2)
                    act.activation(CT[0:NH, 0:4 * P], PS[0:NH, 2, :], ACT.Copy, scale=-1.0).then_inc(sem("ct_ready"), 1)
                    act.activation(CT[0:NH, 4 * P:TP], PS[0:NH, 3, 0:LASTP], ACT.Copy, scale=-1.0).then_inc(sem("ct_ready"), 1)
                    act.wait_ge(sem("ct_ready"), 2)
                    act.dma_start(KTD[:, DH, :], CT[0:NH, :]).then_inc(sem("ct_out"), 16)

                act.wait_ge(sem("v_mm"), t + 1)
                dst = VN if t < 4 else V4
                if t:
                    act.wait_ge(sem("vout"), 16 * t)
                if t == 4:
                    merge(4, 3)
                act.activation(dst[0:r, :], two(4), ACT.Copy).then_inc(sem("vn_ready"), 1)
                act.wait_ge(sem("vn_ready"), t + 1)
                act.dma_start(vp_out[t * P:t * P + min(P, TP - t * P), :], dst[0:min(r, TP - t * P), :]).then_inc(sem("vout"), 16)
                if t == 4:
                    put_out(act, vs_out, V4[S0:64, :])
                act.wait_ge(sem("kn_tr"), t + 1)
                dst = TS if t < 4 else KT4
                if 0 < t < 4:
                    act.wait_ge(sem("qtd_out"), 32 * t)
                act.activation(dst[:, :, 0:r], PS[:, 0:2, :].rearrange("p a (k n) -> p (a k) n", n=P)[:, :, 0:r], ACT.Copy)\
                    .then_inc(sem("kts_ready"), 1)
                act.wait_ge(sem("kts_ready"), t + 1)
                n = r if t < 4 else LASTP
                for hh in range(2):
                    act.dma_start(KTD[hh:NH:2, 0:DH, t * P:t * P + n].rearrange("h d t -> d h t"), dst[DH * hh:DH * hh + DH, :, 0:n])\
                        .then_inc(sem("ktd_out"), 16)
                if t + 2 < NT:
                    proj_norm(t + 2)
                if t < NT - 1:
                    queries_squares(t)
            queries_out(NT - 1)
            act.wait_ge(sem("lf_step"), 5)
            for t in range(NT):
                n = P if t < 4 else LASTP
                put_out(act, fp_out[t * P:t * P + n, :], LF[0:n, t, :])
            put_out(act, fs_out, LF[S0:64, 4, :])
            def attention(i, front=True, back=True, shift=0):
                def evac(n):
                    act.wait_ge(sem("kt_tr"), 32 * i + n + 1)
                    after(act, sem("qk_done"), 16 * i + n // 2 - 1)
                    act.activation(KTR[:, n % 4, :], PS[:, n % 2, :], ACT.Copy).then_inc(sem("kt_odd"), 1)

                def exp(u):
                    t = u % 5
                    r = P if t < 4 else LASTP
                    nk = P * (t + 1) if t < 4 else 4 * P
                    act.wait_ge(sem("pu_max"), 10 * i + u + 1)
                    after(act, sem("pu_t"), 10 * i + u)
                    if t < 4:
                        act.activation(PR[0:r, 0:nk], PS[0:r, 6, 0:nk], ACT.Exp, bias=pst[0:r, 0:1], accum_out=pst[0:r, 3:4])\
                            .then_inc(sem("pu_exp"), 1)
                    else:
                        act.activation(PR[0:r, 0:nk], PS[0:r, 6, 0:nk], ACT.Exp, bias=pst[0:r, 0:1], accum_out=pst[0:r, 4:5])
                        act.activation(PR[0:r, nk:TP], PS[0:r, 4, 0:r], ACT.Exp, bias=pst[0:r, 0:1], accum_out=pst[0:r, 5:6])\
                            .then_inc(sem("pu_exp"), 1)

                def ot(u):
                    hh, t = u // 5, u % 5
                    r = P if t < 4 else LASTP
                    act.wait_ge(sem("pu_v"), 10 * i + u + 1)
                    dst = OTS[DH * hh:DH * hh + DH, i, t * P:t * P + r] if isinstance(i, int) else \
                        OTS[DH * hh:DH * hh + DH, bass.ds(i, 1), t * P:t * P + r].rearrange("p a n -> p (a n)")
                    act.activation(dst, PS[DH * hh:DH * hh + DH, 3, 0:r], ACT.Copy).then_inc(sem("pu_ot"), 1)

                def p_out(part):
                    act.wait_ge(sem("ptt_tr"), 5 * i - 5 + part + 1)
                    after(act, sem("o_mm"), i - 1)
                    if part < NCH:
                        act.activation(PTT[:, CH * part:CH * part + CH, :], PS[:, 4, :].rearrange("p (g n) -> p g n", n=P), ACT.Copy)\
                            .then_inc(sem("ptt_ready"), 1)
                    else:
                        act.activation(PTT[0:64, PAGES, :], PS[0:64, 4, 0:P], ACT.Copy).then_inc(sem("ptt_ready"), 1)

                for n in range(TICKS + shift):
                    m = n - shift
                    if front:
                        if n % 2 == 1 and n < KTICKS:
                            evac(n)
                        if m in V_TICK:
                            ot(V_TICK.index(m))
                        if n % 2 == 1 and (m in S_TICK or m - 1 in S_TICK):
                            exp(S_TICK.index(m if m in S_TICK else m - 1))
                    if back:
                        if n == 1:
                            act.wait_ge(sem("sp_max"), 2 * i)
                            act.activation(SROW[:, :], SROW[:, :], ACT.Exp, bias=sst[:, 0:1], accum_out=sst[:, 1:2])\
                                .then_inc(sem("sp_exp"), 1)
                        if n in P_TICK:
                            p_out(P_TICK.index(n))
                        if n == OT_TICK - 1:
                            act.wait_ge(sem("o_mm"), i)
                            act.wait_ge(sem("sp_rec"), i)
                            after(act, sem("ob_tr"), i - 1)
                            act.activation(OB, PS[:, 5, 0:256], ACT.Copy, scale=sst[:, 2:3]).then_inc(sem("ob_ready"), 1)

            attention(0, back=False, shift=SHIFT)
            with act.Fori(1, NB) as i:
                attention(i)
            attention(NB, front=False)
            for t in range(NT):
                if t == NT - 1:
                    act.wait_ge(sem("wo_done"), NT)
                    act.activation(UPPER1[0:64, :], PS[64:128, 0:2, :].rearrange("p a n -> p (a n)"), ACT.Copy)\
                        .then_inc(sem("upper_ready"), 1)
                router_norm(1, t)
                rows_out(1, t)
            route(1)
            moe(1)

        @block.vector
        def _(dve):
            steps = [0]

            def then(ins):
                steps[0] += 1
                ins.then_inc(sem("dve_step"), 1)
                dve.wait_ge(sem("dve_step"), steps[0])

            def norm(phase, t, out, gain=None):
                r, n = ROWS[t], NORMS.index((phase, t))
                dve.wait_ge(sem("sq"), n + 1)
                dve.tensor_scalar(ms[0:r, t:t + 1], ss[0:r, t:t + 1], 1.0 / D, EPS, ALU.mult, ALU.add).then_inc(sem("row_ms"), 1)
                dve.wait_ge(sem("row_sd"), n + 1)
                then(dve.reciprocal(rs[0:r, t:t + 1], sd[0:r, t:t + 1]))
                if gain is None:
                    return dve.tensor_scalar(out[0:r, :], H[0:r, t, :], rs[0:r, t:t + 1], None, ALU.mult)
                return dve.scalar_tensor_tensor(out=out[0:r, :], in0=H[0:r, t, :], scalar=rs[0:r, t:t + 1], in1=gain[0:r, :],
                                                op0=ALU.mult, op1=ALU.mult)

            def pool_rows(t):
                if t == 0:
                    dve.wait_ge(sem("pool_in"), 32)
                norm("pool", t, U[t], png).then_inc(sem("u_ready"), 1)
                if t == 0:
                    dve.wait_ge(sem("pool_w_in"), 32)
                    for cc in range(2):
                        ins = dve.tensor_tensor(pw[:, :, cc, :], pw[:, :, cc, :], psc.rearrange("p (g n) -> p g n", g=NG), ALU.mult)
                    ins.then_inc(sem("ws_ready"), 1)

            def gained(dst, bank, which, r):
                for half in range(2):
                    g = gains[:, which, 4 * half:4 * half + 4].rearrange("p (k a) -> p k a", a=1).to_broadcast([P, 4, r])
                    ins = dve.tensor_tensor(dst[:, 4 * half:4 * half + 4, 0:r],
                                            PS[:, bank + half, :].rearrange("p (k n) -> p k n", k=4)[:, :, 0:r], g, ALU.mult)
                return ins

            def router_rows(l, t):
                norm(f"r{l}", t, UR[t % 2]).then_inc(sem("un_ready"), 1)

            def router_gains(l, t):
                if t == 0 and l == 0:
                    dve.wait_ge(sem("small_in"), 16 * SMALL)
                dve.wait_ge(sem("un_tr"), t + 1 + l * NT)
                if t >= 2:
                    dve.wait_ge(sem("router_done"), t - 1 + l * NT)
                gained(XU[t % 2], 4, l, ROWS[t]).then_inc(sem("xu_ready"), 1)

            pool_rows(0)
            for t in range(NT + 1):
                if t + 1 < NT:
                    pool_rows(t + 1)
                if t:
                    router_rows(0, t - 1)
                if t < NT:
                    r = ROWS[t]
                    dve.wait_ge(sem("dt_mm"), t + 1)
                    if t >= 2:
                        dve.wait_ge(sem("pool_mm"), t - 1)
                    dve.tensor_copy(DT[t % 2][:, 0:4, 0:r], PS[:, 0, :].rearrange("p (k n) -> p k n", k=4)[:, :, 0:r])\
                        .then_inc(sem("dt_ready"), 1)
                if t:
                    router_gains(0, t - 1)
                if t < NT:
                    dve.wait_ge(sem("pool_mm"), t + 1)
                    dve.tensor_tensor(H[0:r, t, :], H[0:r, t, :], PS[0:r, 2:4, :].rearrange("p a n -> p (a n)"), ALU.add)\
                        .then_inc(sem("h_pool"), 1)

            def router(l):
                dve.wait_ge(sem("router_done"), NT + l * NT)

                def v(name, n=None):
                    return rt[name] if n is None else rt[name].rearrange("p (t e) -> p t e", e=n)

                def bc(name, n):
                    return rt[name].rearrange("p (t a) -> p t a", a=1).to_broadcast([P, NT, n])

                def cb(name, n):
                    return c(name).rearrange("p (a n) -> p a n", a=1).to_broadcast([P, NT, n])

                dve.memset(v("A"), 0.0)
                then(dve.memset(v("L"), 0.0))
                dve.tensor_copy(v("L")[:, 0:80], PS[:, 6, 0:80])
                then(dve.tensor_copy(v("L")[0:64, 80:100], PS[0:64, 6, 80:100]))
                lg = v("L", 20)[:, :, 0:4]
                le = v("L", 20)[:, :, 4:20].rearrange("p t (g e) -> p t g e", g=NG)
                then(dve.tensor_reduce(v("mx"), lg, X, ALU.max))
                dve.tensor_tensor(v("dl", 4), lg, bc("mx", 4), ALU.subtract).then_inc(sem("rt_in"), 1)
                then(dve.tensor_tensor(v("v4", 4), lg, bc("mx", 4), ALU.is_equal))
                then(dve.tensor_tensor(v("v4", 4), v("v4", 4), cb("w4", 4), ALU.mult))
                then(dve.tensor_reduce(v("vm"), v("v4", 4), X, ALU.max))
                then(dve.tensor_tensor(v("oh", 4), v("v4", 4), bc("vm", 4), ALU.is_equal))
                dve.tensor_scalar(v("pen"), v("oh"), 1.0, BIG, ALU.subtract, ALU.mult)
                ohb = v("oh").rearrange("p (n a) -> p n a", a=1).to_broadcast([P, NT * 4, 4])
                penb = v("pen").rearrange("p (n a) -> p n a", a=1).to_broadcast([P, NT * 4, 4])
                LMg = v("LM").rearrange("p (n e) -> p n e", e=4)
                for t in range(NT):
                    ins = dve.tensor_tensor(LMg[:, 4 * t:4 * t + 4, :], le[:, t], ohb[:, 4 * t:4 * t + 4, :], ALU.mult)
                then(ins)
                then(dve.tensor_tensor(LMg, LMg, penb, ALU.add))
                then(dve.tensor_reduce(v("m1"), v("LM", NE), X, ALU.max))
                then(dve.tensor_tensor(v("e1", NE), v("LM", NE), bc("m1", NE), ALU.is_equal))
                then(dve.tensor_tensor(v("e1", NE), v("e1", NE), cb("w16", NE), ALU.mult))
                then(dve.tensor_reduce(v("vm"), v("e1", NE), X, ALU.max))
                then(dve.tensor_tensor(v("oh1", NE), v("e1", NE), bc("vm", NE), ALU.is_equal))
                then(dve.scalar_tensor_tensor(out=v("LM2"), in0=v("oh1"), scalar=-2 * BIG, in1=v("LM"), op0=ALU.mult, op1=ALU.add))
                then(dve.tensor_reduce(v("m2"), v("LM2", NE), X, ALU.max))
                dve.tensor_tensor(v("d"), v("m2"), v("m1"), ALU.subtract).then_inc(sem("rt_in"), 1)
                then(dve.tensor_tensor(v("e1", NE), v("LM2", NE), bc("m2", NE), ALU.is_equal))
                then(dve.tensor_tensor(v("e1", NE), v("e1", NE), cb("w16", NE), ALU.mult))
                then(dve.tensor_reduce(v("vm"), v("e1", NE), X, ALU.max))
                then(dve.tensor_tensor(v("oh2", NE), v("e1", NE), bc("vm", NE), ALU.is_equal))
                val = c("valid").rearrange("p (t a) -> p t a", a=1).to_broadcast([P, NT, NE])
                dve.tensor_tensor(v("oh1", NE), v("oh1", NE), val, ALU.mult)
                then(dve.tensor_tensor(v("oh2", NE), v("oh2", NE), val, ALU.mult))
                dve.tensor_tensor(v("A")[:, 0:NT * NE], v("oh1"), v("oh2"), ALU.add).then_inc(sem("picks_ready"), 1)
                rid = c("rid").rearrange("p (t a) -> p t a", a=1).to_broadcast([P, NT, NE])
                for ch, oh in enumerate(("oh1", "oh2")):
                    dve.tensor_tensor(v("hid")[:, ch * NT * NE:(ch + 1) * NT * NE].rearrange("p (t e) -> p t e", e=NE),
                                      v(oh, NE), rid, ALU.mult)
                    then(dve.tensor_tensor(v("e1", NE), v(oh, NE), cb("eid", NE), ALU.mult))
                    then(dve.tensor_reduce(v("EC")[:, ch * NT:(ch + 1) * NT], v("e1", NE), X, ALU.add))
                dve.wait_ge(sem("ranks"), 1 + l * 2)
                R = PS[:, 7, 0:NT * NE]
                dve.tensor_tensor(v("oh1"), v("oh1"), R, ALU.mult)
                dve.tensor_tensor(v("oh2"), v("oh2"), R, ALU.mult)
                then(dve.tensor_copy(v("tot"), PS[:, 7, NT * NE:(NT + 1) * NE]))
                dve.tensor_reduce(v("RK")[:, 0:NT], v("oh1", NE), X, ALU.add)
                then(dve.tensor_reduce(v("RK")[:, NT:], v("oh2", NE), X, ALU.add))
                dve.tensor_tensor(PLACE, c("place").rearrange("p (a n) -> p a n", a=1).to_broadcast([P, 2 * NT, P]),
                                  v("RK").rearrange("p (x a) -> p x a", a=1).to_broadcast([P, 2 * NT, P]), ALU.is_equal)\
                    .then_inc(sem("picks_ready"), 1)
                then(dve.scalar_tensor_tensor(out=v("SL"), in0=v("RK"), scalar=float(NE), in1=v("EC"), op0=ALU.mult, op1=ALU.add))
                then(dve.tensor_tensor(v("SS"), v("SL"), c("junk"), ALU.add))
                dve.wait_ge(sem("ranks"), 2 + l * 2)
                dve.tensor_copy(IDX[:, :], PS[:, 6, P:P + NE]).then_inc(sem("slots_ready"), 1)
            def gates(l):
                def v(name, n=None):
                    return rt[name] if n is None else rt[name].rearrange("p (t e) -> p t e", e=n)

                dve.wait_ge(sem("rt_exp"), 1 + l * 2)
                then(dve.tensor_reduce(v("sum"), v("eg", 4), X, ALU.add))
                dve.reciprocal(v("ptop"), v("sum"))
                dve.wait_ge(sem("rt_exp"), 2 + l * 2)
                then(dve.tensor_scalar(v("den"), v("ed"), 1.0, None, ALU.add))
                then(dve.reciprocal(v("rden"), v("den")))
                then(dve.tensor_tensor(gate[:, 0, :], v("ptop"), v("rden"), ALU.mult))
                then(dve.tensor_tensor(gate[:, 1, :], gate[:, 0, :], v("ed"), ALU.mult))
                then(dve.tensor_scalar(v("Sm"), v("SL"), float(P * NE), None, ALU.is_lt))
                dve.tensor_tensor(gm[:, :, :].rearrange("p c t -> p (c t)"), gate[:, :, :].rearrange("p c t -> p (c t)"), v("Sm"), ALU.mult)
                then(dve.tensor_tensor(v("Sm"), v("Sm"), v("SL"), ALU.mult))
                dve.tensor_copy(SLi[:, :, :].rearrange("p c t -> p (c t)"), v("Sm"))
                then(dve.tensor_copy(SSi[:, :, :].rearrange("p c t -> p (c t)"), v("SS")))
                dve.sem_inc(sem("slots_ready"), 1)
                then(dve.tensor_reduce(v("nm"), v("tot"), X, ALU.max))
                for k in range(1, 5):
                    ins = dve.tensor_scalar(v("np")[:, k - 1:k], v("nm"), P * k + 0.5, None, ALU.is_ge)
                then(ins)
                then(dve.tensor_reduce(v("nf"), v("np"), X, ALU.add))
                then(dve.tensor_scalar(v("nf"), v("nf"), 1.0, None, ALU.add))
                dve.tensor_copy(npi[0:1, 0:1], v("nf")[0:1, :]).then_inc(sem("np_ready"), 1)

            def moe(l):
                def xt(e):
                    dve.wait_ge(sem("xt_tr"), e + 1 + l * NE)
                    gained(XT, 0, l, P).then_inc(sem("xt_ready"), 1)

                def hidden(e):
                    dve.wait_ge(sem("silu_done"), e + 1 + l * NE)
                    dve.wait_ge(sem("up_done"), e + 1 + l * NE)
                    after(dve, sem("ht_tr"), e + l * NE)
                    dve.tensor_tensor(HH, SG, PS[:, 3, :], ALU.mult).then_inc(sem("h_ready"), 1)

                xt(0)
                gates(l)
                hidden(0)
                xt(1)
                with dve.Fori(1, NE - 1) as e:
                    hidden(e)
                    xt(e + 1)
                hidden(NE - 1)
                dve.wait_ge(sem("np_ready"), 1 + l * 1)
                npass = dve.value_load(npi[0:1, 0:1], min_val=1, max_val=RANKS // P)
                with dve.If(npass > 1):
                    with dve.Fori(1, npass) as p:
                        with dve.Fori(0, NE) as e:
                            n = p * NE + e - NE
                            dve.wait_ge(sem(f"g_step{l}"), 9 * n + 1)
                            gained(XT, 0, l, P).then_inc(sem(f"g_step{l}"), 1)
                            dve.wait_ge(sem(f"g_step{l}"), 9 * n + 4)
                            dve.tensor_tensor(HH, SG, PS[:, 3, :], ALU.mult).then_inc(sem(f"g_step{l}"), 1)
                        chain = [0]

                        def link(ins):
                            chain[0] += 1
                            ins.then_inc(sem(f"g_dve{l}"), 1)
                            dve.wait_ge(sem(f"g_dve{l}"), LINKS * p - LINKS + chain[0])

                        SL, Sm = rt["SL"], rt["Sm"]
                        link(dve.tensor_scalar(SL, SL, float(P * NE), None, ALU.subtract))
                        link(dve.tensor_scalar(Sm, SL, 0.0, None, ALU.is_ge))
                        link(dve.scalar_tensor_tensor(out=Sm, in0=SL, scalar=float(P * NE), in1=Sm, op0=ALU.is_lt, op1=ALU.mult))
                        link(dve.tensor_tensor(gg[:, :, :].rearrange("p c t -> p (c t)"), gate[:, :, :].rearrange("p c t -> p (c t)"),
                                               Sm, ALU.mult))
                        link(dve.tensor_tensor(Sm, SL, Sm, ALU.mult))
                        dve.tensor_copy(SGi[:, :, :].rearrange("p c t -> p (c t)"), Sm).then_inc(sem(f"g_sum{l}"), 1)
                        for t in range(NT):
                            r = ROWS[t]
                            dve.wait_ge(sem(f"g_yg{l}"), 32 * NT * p + 32 * (t + 1 - NT))
                            link(dve.scalar_tensor_tensor(out=H[0:r, t, :], in0=K8[0:r, 0, :], scalar=gg[0:r, 0, t:t + 1],
                                                          in1=H[0:r, t, :], op0=ALU.mult, op1=ALU.add))
                            dve.scalar_tensor_tensor(out=H[0:r, t, :], in0=K8[0:r, 1, :], scalar=gg[0:r, 1, t:t + 1],
                                                     in1=H[0:r, t, :], op0=ALU.mult, op1=ALU.add).then_inc(sem(f"g_sum{l}"), 1)
                        assert chain[0] == LINKS

            def combine(l, t):
                r = ROWS[t]
                dve.wait_ge(sem(f"yg_in_{t}"), 32 + l * 32)
                for ch in range(2):
                    ins = dve.scalar_tensor_tensor(out=H[0:r, t, :], in0=K8[0:r, (2 * t + ch) % 8, :], scalar=gm[0:r, ch, t:t + 1],
                                                   in1=H[0:r, t, :], op0=ALU.mult, op1=ALU.add)
                    if ch == 0:
                        then(ins)
                ins.then_inc(sem("h_sum"), 1)

            router(0)
            moe(0)

            then(dve.memset(LF[:, :, :], 0.0))
            dve.memset(hms[:, :, :], 1.0)
            dve.memset(hss[:, :, :], 1.0)
            ins = dve.tensor_scalar(qg[:, :], qg[:, :], float(DH) ** -0.5, None, ALU.mult)
            then(ins)

            def head_norm(which, r, t):
                dve.wait_ge(sem("head_sq"), 2 * t + which + 1)
                then(dve.tensor_reduce(hss[0:r, which, :], SQ[0:r, :].rearrange("p (h d) -> p h d", d=DH), X, ALU.add))
                dve.tensor_scalar(hms[0:r, which, :], hss[0:r, which, :], 1.0 / DH, EPS, ALU.mult, ALU.add).then_inc(sem("head_ms"), 1)
                dve.wait_ge(sem("head_sd"), 2 * t + which + 1)
                then(dve.reciprocal(hrs[:, which, :], hsd[:, which, :]))
                return hrs[0:r, which, :].rearrange("p (h a) -> p h a", a=1).to_broadcast([r, NH, DH])

            def rows(t):
                combine(0, t)
                after(dve, sem("pun_tr"), t)
                norm("proj", t, UN).then_inc(sem("pun_ready"), 1)

            def gains_in(t):
                r = ROWS[t]
                dve.wait_ge(sem("pun_tr"), t + 1)
                after(dve, sem("v_mm"), t - 1)
                gained(UK[t % 2], 0, 2, r).then_inc(sem("ux_ready"), 1)
                after(dve, sem("q_mm"), t - 1)
                gained(UQ[t % 2], 0, 3, r).then_inc(sem("ux_ready"), 1)

            def merge(b, done, n):
                dve.wait_ge(sem(done), NT)
                dve.wait_ge(sem("upper_ready"), n)
                both = PS[0:64, b:b + 2, :].rearrange("p a n -> p (a n)")
                dve.tensor_tensor(both, both, UPPER[0:64, :], ALU.add).then_inc(sem("merged"), 1)

            def forgets(t):
                r = ROWS[t]
                dve.wait_ge(sem("f_mm"), t + 1)
                dve.tensor_tensor(LF[0:r, t, :], PS[0:r, 6, 0:NH], bfb[0:r, :], ALU.add).then_inc(sem("f_ready"), 1)

            rows(0)
            gains_in(0)
            rows(1)
            for t in range(NT):
                r = ROWS[t]
                heads = lambda a: a.rearrange("p (h d) -> p h d", d=DH)
                two = lambda b: PS[0:r, b:b + 2, :].rearrange("p a (h d) -> p (a h) d", d=DH)
                if t == 4:
                    forgets(t)
                    merge(2, "k_mm", 1)
                rk = head_norm(0, r, t)
                if t:
                    dve.wait_ge(sem("kn_tr"), t)
                    dve.wait_ge(sem("kout"), 16 * t)
                dve.tensor_tensor(heads(KN[0:r, :]), two(2), rk, ALU.mult).then_inc(sem("kn_ready"), 1)
                dve.wait_ge(sem("kn_ready"), 2 * t + 1)
                kg = kgb[0:r, :].rearrange("p (a d) -> p a d", a=1).to_broadcast([r, NH, DH])
                dve.tensor_tensor(heads(KN[0:r, :]), heads(KN[0:r, :]), kg, ALU.mult).then_inc(sem("kn_ready"), 1)
                if t < 4:
                    forgets(t)
                if t == 0:
                    rows(2)
                if t + 1 < NT:
                    gains_in(t + 1)
                if 0 < t and t + 2 < NT:
                    rows(t + 2)
                if t == 4:
                    lf = LF[:, :, :].rearrange("p t h -> p (t h)")
                    dve.wait_ge(sem("f_ready"), NT)
                    then(dve.scalar_tensor_tensor(out=lfa, in0=lf, scalar=-1.0, in1=lf, op0=ALU.mult, op1=ALU.max))
                    dve.sem_inc(sem("lf_step"), 1)
                    dve.wait_ge(sem("lf_step"), 2)
                    dve.tensor_scalar(lfe, lfe, 1.0, None, ALU.add).then_inc(sem("lf_step"), 1)
                    dve.wait_ge(sem("lf_step"), 4)
                    then(dve.scalar_tensor_tensor(out=lf, in0=lf, scalar=0.0, in1=lfa, op0=ALU.min, op1=ALU.subtract))
                    dve.sem_inc(sem("lf_step"), 1)
                    then(dve.memset(LR[0:64, :], 0.0))
                    dve.tensor_copy(LR[0:64, :].rearrange("p (a h q) -> p a h q", a=4, q=NS)[:, :, 0:4, :],
                                    LF[0:64, 4, :].rearrange("p (a h o) -> p a h o", a=4, o=1).to_broadcast([64, 4, 4, NS]))\
                        .then_inc(sem("new_rows"), 1)
                    merge(6, "q_mm", 2)
                rq = head_norm(1, r, t)
                dve.sem_inc(sem("ssq_ready"), 1)
                if t:
                    dve.wait_ge(sem("qn_tr"), t)
                dve.tensor_tensor(heads(QN[0:r, :]), two(6), rq, ALU.mult).then_inc(sem("qn_ready"), 1)
                if t == 4:
                    dve.wait_ge(sem("ct_mm"), 2)
                    dve.wait_ge(sem("ct_ready"), 2)
                    sm = c("smask").rearrange("p (b n) -> p b n", b=NB)
                    for b in range(NB):
                        ins = dve.tensor_tensor(sm[:, b, :], sm[:, b, :], PS[:, 3, P:P + 64], ALU.add)
                    ins.then_inc(sem("new_rows"), 1)
                    merge(4, "v_mm", 3)
            dve.memset(OTS[:, :, 4 * P:4 * P + 64], 0.0)
            then(dve.memset(QBLK[:, :, :], 0.0))
            dve.wait_ge(sem("qts_ready"), NT)

            def attention(i, front=True, back=True, shift=0):
                one = isinstance(i, int)

                def evac(n):
                    dve.wait_ge(sem("kt_tr"), 32 * i + n + 1)
                    after(dve, sem("qk_done"), 16 * i + n // 2 - 1)
                    dve.tensor_copy(KTR[:, n % 4, :], PS[:, n % 2, :]).then_inc(sem("kt_even"), 1)

                def pmax(u):
                    t = u % 5
                    r = P if t < 4 else LASTP
                    nk = P * (t + 1) if t < 4 else 4 * P
                    dve.wait_ge(sem("pu_s"), 10 * i + u + 1)
                    after(dve, sem("pu_exp"), 10 * i + u)
                    if t < 4:
                        dve.tensor_reduce(pst[0:r, 0:1], PS[0:r, 6, 0:nk], X, ALU.max, negate=True).then_inc(sem("pu_max"), 1)
                    else:
                        dve.tensor_reduce(pst[0:r, 1:2], PS[0:r, 6, 0:nk], X, ALU.max, negate=True)
                        dve.tensor_reduce(pst[0:r, 2:3], PS[0:r, 4, 0:r], X, ALU.max, negate=True).then_inc(sem("pu_last"), 1)
                        dve.wait_ge(sem("pu_last"), 4 * i + 2 * (u // 5) + 1)
                        dve.tensor_tensor(pst[0:r, 0:1], pst[0:r, 1:2], pst[0:r, 2:3], ALU.min).then_inc(sem("pu_max"), 1)

                def pnorm(u):
                    t = u % 5
                    r = P if t < 4 else LASTP
                    nk = P * (t + 1) if t < 4 else TP
                    dve.wait_ge(sem("pu_exp"), 10 * i + u + 1)
                    if t == 4:
                        dve.tensor_tensor(pst[0:r, 3:4], pst[0:r, 4:5], pst[0:r, 5:6], ALU.add).then_inc(sem("pu_last"), 1)
                        dve.wait_ge(sem("pu_last"), 4 * i + 2 * (u // 5) + 2)
                    dve.reciprocal(pst[0:r, 6:7], pst[0:r, 3:4]).then_inc(sem("pu_rec"), 1)
                    dve.wait_ge(sem("pu_rec"), 10 * i + u + 1)
                    dve.tensor_scalar(PR[0:r, 0:nk], PR[0:r, 0:nk], pst[0:r, 6:7], None, ALU.mult).then_inc(sem("pu_norm"), 1)

                def pts(u):
                    t = u % 5
                    dve.wait_ge(sem("pu_t"), 10 * i + u + 1)
                    after(dve, sem("pu_v"), 10 * i + u)
                    if t < 4:
                        dve.tensor_copy(PTS[:, 0:P * (t + 1)], PS[:, 7, 0:P * (t + 1)]).then_inc(sem("pu_pts"), 1)
                    else:
                        r = LASTP
                        dve.tensor_copy(PTS[:, 0:4 * r], PS[:, 7, 0:4 * r])
                        dve.tensor_copy(PTS[0:r, 4 * r:5 * r], PS[0:r, 7, 4 * r:5 * r]).then_inc(sem("pu_pts"), 1)

                def scores(b, ch):
                    dve.wait_ge(sem("qk_done"), 16 * b + 4 * ch + 4)
                    dve.wait_ge(sem(f"bias_in{ch // 2}"), 64 * (b + 1))
                    if ch < NCH - 1 and not (isinstance(b, int) and b == 0):
                        dve.wait_ge(sem("ptt_tr"), 5 * b - 5 + ch + 1)
                    row = SROW[:, 512 * ch:512 * ch + 512]
                    dve.tensor_tensor(row, PS[:, 2, :], BIAS[:, 512 * ch:512 * ch + 512], ALU.add).then_inc(sem("s_ready"), 1)

                def largest(b, ch):
                    dve.wait_ge(sem("s_ready"), 4 * b + ch + 1)
                    return dve.tensor_reduce(smx[:, ch:ch + 1], SROW[:, 512 * ch:512 * ch + 512], X, ALU.max)

                if back:
                    scores(i - 1, NCH - 1)
                for n in range(TICKS + shift):
                    m = n - shift
                    if front and n % 2 == 0 and n < KTICKS:
                        evac(n)
                    if n == 0:
                        if back:
                            largest(i - 1, NCH - 1).then_inc(sem("sp_max"), 1)
                            dve.wait_ge(sem("sp_max"), 2 * i - 1)
                            dve.tensor_reduce(sst[:, 0:1], smx[:, :], X, ALU.max, negate=True).then_inc(sem("sp_max"), 1)
                        if front:
                            after(dve, sem("qk_done"), 16 * i)
                            for half in range(2):
                                for j in range(2):
                                    src = QT4[DH * half:DH * half + DH, j:HP:2, :]
                                    src = src[:, :, S0 + NS * i:S0 + NS * i + NS] if one else src[:, :, bass.ds(NS * i + S0, NS)]
                                    at = 8 * j + NS * half
                                    ins = dve.tensor_copy(QBLK[DH * half:DH * half + DH, j:HP:2, at:at + NS], src)
                            ins.then_inc(sem("qb_ready"), 1)
                    if back and n == P_TICK[0]:
                        dve.wait_ge(sem("sp_exp"), i)
                        after(dve, sem("ob_ready"), i - 1)
                        dve.reciprocal(sst[:, 2:3], sst[:, 1:2]).then_inc(sem("sp_rec"), 1)
                    if front:
                        if n in QK_TICK[3:-1:4]:
                            ch = QK_TICK.index(n) // 4
                            scores(i, ch)
                            largest(i, ch)
                        if n == NEW_TICK:
                            dve.wait_ge(sem("sn_mm"), i + 1)
                            after(dve, sem("ptt_tr"), 5 * i)
                            mask = sm[:, i, :] if one else sm[:, bass.ds(i, 1), :].rearrange("p a n -> p (a n)")
                            dve.tensor_tensor(SROW[:, PAGES * PAGE:], PS[:, 2, 0:64], mask, ALU.add).then_inc(sem("sn_ready"), 1)
                            dve.wait_ge(sem("sn_ready"), i + 1)
                            dve.tensor_reduce(smx[:, NCH:NCH + 1], SROW[:, PAGES * PAGE:], X, ALU.max)
                        if m in T_TICK:
                            pts(T_TICK.index(m))
                        if m in S_TICK:
                            pmax(S_TICK.index(m))
                        if m - 1 in S_TICK:
                            pnorm(S_TICK.index(m - 1))
                    if back and n == OT_TICK:
                        dve.wait_ge(sem("ob_tr"), i)
                        for half in range(2):
                            for x in range(2):
                                rows = slice(DH * half, DH * half + DH)
                                src = PS[rows, 5, 256 + x * P:256 + (x + 1) * P].rearrange("p (q n) -> p q n", q=4)
                                src = src[:, :, 8 * x + 4 * half:8 * x + 4 * half + NS]
                                at = 4 * P + S0 - NS
                                dst = OTS[rows, x:HP:2, :]
                                dst = dst[:, :, at + NS * i:at + NS * i + NS] if one else dst[:, :, bass.ds(NS * i + at, NS)]
                                ins = dve.tensor_copy(dst, src)
                            ins.then_inc(sem("ots_ready"), 1)

            attention(0, back=False, shift=SHIFT)
            with dve.Fori(1, NB) as i:
                attention(i)
            attention(NB, front=False)

            for t in range(NT + 1):
                if t >= 2:
                    router_gains(1, t - 2)
                if t < NT:
                    r = ROWS[t]
                    dve.wait_ge(sem("wo_done"), t + 1)
                    b = 2 * (t % 2)
                    ins = dve.tensor_tensor(H[0:r, t, :], H[0:r, t, :], PS[0:r, b:b + 2, :].rearrange("p a n -> p (a n)"), ALU.add)
                    if t == 4:
                        then(ins)
                        dve.wait_ge(sem("upper_ready"), 4)
                        ins = dve.tensor_tensor(H[0:r, t, :], H[0:r, t, :], UPPER1[0:r, :], ALU.add)
                    ins.then_inc(sem("h_attn"), 1)
                    router_rows(1, t)
            router_gains(1, NT - 1)
            router(1)
            moe(1)
            for t in range(NT):
                combine(1, t)

        assert n_out[0] == OUTS, n_out


INPUTS = ["x_prompt", "x_sample", "state_pool", "cache_k", "cache_v", "cache_logf", "page_table", "meta", "pool_norm_g",
          "pool_w", "pool_scale", "kv_norm_g", "w_kvf", "b_f", "k_norm_g", "attn_norm_g", "w_q", "q_norm_g", "w_o",
          "ffn_norm_g", "w_router_group", "w_router_expert", "w_gate", "w_up", "w_down"]
OUTPUTS = [("y_prompt", (1, SEQ, D)), ("y_sample", (NB, NS, D)), ("pool_state_prompt", (1, 1, STATE, D)),
           ("pool_state_sample", (1, NB, STATE, D)), ("k_prompt", (1, TP, NH, DH)), ("v_prompt", (1, TP, NH, DH)),
           ("logf_prompt", (1, TP, NH)), ("k_sample", (NB, NS, NH, DH)), ("v_sample", (NB, NS, NH, DH)),
           ("logf_sample", (NB, NS, NH))]


def kernel(**inputs):
    import concourse.bacc as bacc
    from concourse.bass_utils import run_bass_kernel_spmd

    nc = bacc.Bacc("TRN2", target_bir_lowering=False, num_devices=1)
    consts, bands, ids = shape_constants()
    arrays = {name: np.ascontiguousarray(inputs[name]) for name in INPUTS}
    arrays.update(consts=consts, bands=bands, ids=ids)
    A = {name: nc.dram_tensor(f"in_{name}", a.shape, mybir.dt.from_np(a.dtype), kind="ExternalInput").ap()
         for name, a in arrays.items()}
    O = {name: nc.dram_tensor(f"out_{name}", shape, F32, kind="ExternalOutput").ap() for name, shape in OUTPUTS}
    build(nc, A, O)
    r = run_bass_kernel_spmd(nc, [{f"in_{name}": a for name, a in arrays.items()}], core_ids=[0])
    return tuple(r.results[0][f"out_{name}"] for name, _ in OUTPUTS)
```
